# Optimizing a Trainium2 kernel written in Bass

```python
import math
import jax, jax.numpy as jnp
from jax import lax
import numpy as np

D_MODEL = 1024
BATCH = 1
SEQ = 256
DEPTH = 2

CHUNK = 64
N_HEADS = 16
HEAD_DIM = 64
IDX_HEADS = 8
IDX_DIM = 64
TOPK_MAX = 256
A_QBLOCK = 64
B_QBLOCK = 128
ROPE_THETA = 10000.0
D_FF = 2816
N_EXPERTS = 8
TOP_K = 2
RMS_EPS = 1e-6

kernel_name = "yoco_dsa_fox_moe_trunk"

def rms_norm(x, g):
    xf = x.astype(jnp.float32)
    y = xf * lax.rsqrt(jnp.mean(xf * xf, axis=-1, keepdims=True) + RMS_EPS)
    return (y * g.astype(jnp.float32)).astype(x.dtype)

def rope_tables(seq_len, dim):
    pos = jnp.arange(seq_len, dtype=jnp.float32)
    inv_freq = 1.0 / (ROPE_THETA ** (jnp.arange(0, dim, 2, dtype=jnp.float32) / dim))
    ang = pos[:, None] * inv_freq[None, :]
    return jnp.cos(ang), jnp.sin(ang)

def apply_rope(x, cos, sin):
    half = x.shape[-1] // 2
    c = cos[None, :, None, :].astype(x.dtype)
    s = sin[None, :, None, :].astype(x.dtype)
    x1, x2 = x[..., :half], x[..., half:]
    return jnp.concatenate([x1 * c - x2 * s, x2 * c + x1 * s], axis=-1)

def to_blocks(a, qb):
    b, s = a.shape[0], a.shape[1]
    return a.reshape(b, s // qb, qb, *a.shape[2:]).swapaxes(0, 1)

def from_blocks(a):
    a = a.swapaxes(0, 1)
    return a.reshape(a.shape[0], a.shape[1] * a.shape[2], *a.shape[3:])

def swiglu(x, w_gate_up, w_down):
    gu = x @ w_gate_up
    g, u = jnp.split(gu, 2, axis=-1)
    return (jax.nn.silu(g) * u) @ w_down

def moe_swiglu(x, w_router, w_gate_up, w_down):
    logits = (x @ w_router).astype(jnp.float32)
    top_vals, top_idx = lax.top_k(logits, TOP_K)
    gates = jax.nn.softmax(top_vals, axis=-1)
    combine = jnp.sum(jax.nn.one_hot(top_idx, N_EXPERTS, dtype=jnp.float32)
                      * gates[..., None], axis=-2).astype(x.dtype)
    out = jnp.zeros_like(x)
    for e in range(N_EXPERTS):
        out = out + combine[..., e:e + 1] * swiglu(x, w_gate_up[e], w_down[e])
    return out

def mixer_a(hn, w_in, w_out, cos, sin):
    B, S, _ = hn.shape
    hd = N_HEADS * HEAD_DIM
    splits = [hd, 2 * hd, 3 * hd, 3 * hd + IDX_HEADS * IDX_DIM,
              3 * hd + IDX_HEADS * IDX_DIM + IDX_DIM]
    p = hn @ w_in
    q, k, v, qi, ki, wi = jnp.split(p, splits, axis=-1)
    q = apply_rope(q.reshape(B, S, N_HEADS, HEAD_DIM), cos, sin)
    k = apply_rope(k.reshape(B, S, N_HEADS, HEAD_DIM), cos, sin)
    v = v.reshape(B, S, N_HEADS, HEAD_DIM)
    qi = apply_rope(qi.reshape(B, S, IDX_HEADS, IDX_DIM), cos, sin)
    ki = apply_rope(ki[:, :, None, :], cos, sin)[:, :, 0, :]
    wi = wi * (IDX_HEADS ** -0.5)
    k_sel = min(TOPK_MAX, S // 4)
    scale = HEAD_DIM ** -0.5
    key_pos = jnp.arange(S)

    def block(args):
        qb, qib, wib, b0 = args
        t = b0 * A_QBLOCK + jnp.arange(A_QBLOCK)
        limit = (t // CHUNK + 1) * CHUNK
        visible = key_pos[None, :] < limit[:, None]
        sc = jnp.einsum('bqhd,bsd->bqhs', qib, ki).astype(jnp.float32)
        idx_score = jnp.einsum('bqhs,bqh->bqs', jax.nn.relu(sc), wib.astype(jnp.float32))
        idx_score = jnp.where(visible[None], idx_score, -jnp.inf)
        _, sel = lax.top_k(idx_score, k_sel)
        valid = sel < limit[None, :, None]
        kg = jax.vmap(lambda a, i: a[i])(k, sel)
        vg = jax.vmap(lambda a, i: a[i])(v, sel)
        logits = jnp.einsum('bqhd,bqkhd->bqhk', qb, kg).astype(jnp.float32) * scale
        logits = jnp.where(valid[:, :, None, :], logits, -jnp.inf)
        probs = jax.nn.softmax(logits, axis=-1).astype(qb.dtype)
        return jnp.einsum('bqhk,bqkhd->bqhd', probs, vg)

    nb = S // A_QBLOCK
    o = lax.map(block, (to_blocks(q, A_QBLOCK), to_blocks(qi, A_QBLOCK),
                        to_blocks(wi, A_QBLOCK), jnp.arange(nb)))
    o = from_blocks(o).reshape(B, S, N_HEADS * HEAD_DIM)
    return o @ w_out

def shared_kv(h, g, w_kv, b_f):
    B, S, _ = h.shape
    hd = N_HEADS * HEAD_DIM
    hn = rms_norm(h, g)
    p = hn @ w_kv
    k, v, f_logit = jnp.split(p, [hd, 2 * hd], axis=-1)
    k = k.reshape(B, S, N_HEADS, HEAD_DIM)
    v = v.reshape(B, S, N_HEADS, HEAD_DIM)
    log_f = jax.nn.log_sigmoid(f_logit.astype(jnp.float32) + b_f.astype(jnp.float32))
    cum_log_f = jnp.cumsum(log_f, axis=1)
    return k, v, cum_log_f

def mixer_b(hn, w_q, w_out, k, v, cum_log_f):
    B, S, _ = hn.shape
    q = (hn @ w_q).reshape(B, S, N_HEADS, HEAD_DIM)
    scale = HEAD_DIM ** -0.5
    f_keys = cum_log_f.transpose(0, 2, 1)
    key_pos = jnp.arange(S)

    def block(args):
        qb, fq, b0 = args
        t = b0 * B_QBLOCK + jnp.arange(B_QBLOCK)
        causal = key_pos[None, :] <= t[:, None]
        logits = jnp.einsum('bqhd,bshd->bhqs', qb, k).astype(jnp.float32) * scale
        logits = logits + fq.transpose(0, 2, 1)[..., None] - f_keys[:, :, None, :]
        logits = jnp.where(causal[None, None], logits, -jnp.inf)
        probs = jax.nn.softmax(logits, axis=-1).astype(qb.dtype)
        return jnp.einsum('bhqs,bshd->bqhd', probs, v)

    nb = S // B_QBLOCK
    o = lax.map(block, (to_blocks(q, B_QBLOCK), to_blocks(cum_log_f, B_QBLOCK),
                        jnp.arange(nb)))
    o = from_blocks(o).reshape(B, S, N_HEADS * HEAD_DIM)
    return o @ w_out

def setup_inputs(seed: int = 0) -> dict:
    key = jax.random.key(seed)
    ks = jax.random.split(key, 20)
    n_a = DEPTH // 2
    n_b = DEPTH - n_a
    n_dense = (DEPTH + 1) // 2
    n_moe = DEPTH // 2
    hd = N_HEADS * HEAD_DIM
    a_in_width = 3 * hd + IDX_HEADS * IDX_DIM + IDX_DIM + IDX_HEADS
    out_scale = (2.0 * DEPTH) ** -0.5

    def w(k, shape, fan_in, extra=1.0):
        return jax.random.normal(k, shape, jnp.float32) * (fan_in ** -0.5) * extra

    def gain(k, shape):
        return 1.0 + 0.02 * jax.random.normal(k, shape, jnp.float32)

    return {
        "x": jax.random.normal(ks[0], (BATCH, SEQ, D_MODEL), jnp.float32),
        "a_norm": gain(ks[1], (n_a, D_MODEL)),
        "a_w_in": w(ks[2], (n_a, D_MODEL, a_in_width), D_MODEL),
        "a_w_out": w(ks[3], (n_a, hd, D_MODEL), hd, out_scale),
        "kv_norm": gain(ks[4], (D_MODEL,)),
        "w_kv": w(ks[5], (D_MODEL, 2 * hd + N_HEADS), D_MODEL),
        "b_f": 3.0 + 0.5 * jax.random.normal(ks[6], (N_HEADS,), jnp.float32),
        "b_norm": gain(ks[7], (n_b, D_MODEL)),
        "b_w_q": w(ks[8], (n_b, D_MODEL, hd), D_MODEL),
        "b_w_out": w(ks[9], (n_b, hd, D_MODEL), hd, out_scale),
        "ffn_norm": gain(ks[10], (DEPTH, D_MODEL)),
        "dense_w_gate_up": w(ks[11], (n_dense, D_MODEL, 2 * D_FF), D_MODEL),
        "dense_w_down": w(ks[12], (n_dense, D_FF, D_MODEL), D_FF, out_scale),
        "moe_router": w(ks[13], (n_moe, D_MODEL, N_EXPERTS), D_MODEL),
        "moe_w_gate_up": w(ks[14], (n_moe, N_EXPERTS, D_MODEL, 2 * D_FF), D_MODEL),
        "moe_w_down": w(ks[15], (n_moe, N_EXPERTS, D_FF, D_MODEL), D_FF, out_scale),
        "final_norm": gain(ks[16], (D_MODEL,)),
    }

def reference(x, a_norm, a_w_in, a_w_out, kv_norm, w_kv, b_f, b_norm, b_w_q,
              b_w_out, ffn_norm, dense_w_gate_up, dense_w_down, moe_router,
              moe_w_gate_up, moe_w_down, final_norm):
    S = x.shape[1]
    n_a = DEPTH // 2
    cos, sin = rope_tables(S, HEAD_DIM)
    h = x
    k_sh = v_sh = f_sh = None
    for i in range(DEPTH):
        if i < n_a:
            h = h + mixer_a(rms_norm(h, a_norm[i]), a_w_in[i], a_w_out[i], cos, sin)
        else:
            if i == n_a:
                k_sh, v_sh, f_sh = shared_kv(h, kv_norm, w_kv, b_f)
            j = i - n_a
            h = h + mixer_b(rms_norm(h, b_norm[j]), b_w_q[j], b_w_out[j], k_sh, v_sh, f_sh)
        hn = rms_norm(h, ffn_norm[i])
        if i % 2 == 0:
            h = h + swiglu(hn, dense_w_gate_up[i // 2], dense_w_down[i // 2])
        else:
            h = h + moe_swiglu(hn, moe_router[i // 2], moe_w_gate_up[i // 2], moe_w_down[i // 2])
    return rms_norm(h, final_norm)


_drawn_inputs = setup_inputs


def setup_inputs(seed=0):
    import zlib

    import numpy as np

    out = dict(_drawn_inputs(seed))
    spreads = {}
    factors = {'kv_norm': 3.601, 'b_norm': 8.0, 'final_norm': 2.862}
    for name, (base, spread) in spreads.items():
        noise = np.random.default_rng([zlib.crc32(name.encode()), seed]).standard_normal(out[name].shape)
        drawn = base * np.exp(spread * noise) if base else spread * noise
        out[name] = __import__('jax').numpy.asarray(drawn.astype(out[name].dtype))
    for name, factor in factors.items():
        out[name] = (out[name] * factor).astype(out[name].dtype)
    return out
```

```python
from contextlib import ExitStack

import numpy as np

import concourse.bass as bass
from concourse import mybir

F32 = mybir.dt.float32
F32R = mybir.dt.float32r
I32 = mybir.dt.int32
ALU = mybir.AluOpType
ACT = mybir.ActivationFunctionType
AX_X = mybir.AxisListType.X

P = 128
SEQ = 256
D = 1024
HEADS = 16
HD = 64
IDX_HEADS = 8
F = 2816
EXPERTS = 8
CHUNK = 64
TOPK = 64
EPS = 1e-6
T = SEQ // P
KC = D // P
FB = F // 256
HALF = 512
UNIT = 4 * HALF
A_TAIL = HD + IDX_HEADS
LOG = P + SEQ

BLOCKS = [
    ("rope_index", 0), ("tail_a", 0), ("rope_q", 0), ("rope_q", 1), ("rope_k", 0), ("rope_k", 1), ("v", 0), ("v", 1),
    ("res", 0), ("res", 1),
    ("copy_k", 0), ("copy_k", 1), ("v", 0), ("v", 1), ("tail_f", 0),
    ("copy_q", 0), ("copy_q", 1),
    ("res", 0), ("res", 1),
    ("router", 0),
]
WIDTH = {"tail_a": A_TAIL, "tail_f": HEADS, "router": EXPERTS}
B_A, B_OUT_A, B_KV, B_Q, B_OUT_B, B_ROUTER = range(0, 8), range(8, 10), range(10, 15), range(15, 17), range(17, 19), 19
FFN_UNITS = 3 * FB


def first_unit(b):
    before = sum(1 if BLOCKS[i][0] in WIDTH else 2 for i in range(b))
    return before + (FFN_UNITS if b >= 10 else 0)


DENSE_U = first_unit(9) + 2
PRE = first_unit(B_ROUTER) + 1
MOE_UNITS = EXPERTS * FFN_UNITS
RING_PRE = 7
RING = 11
SPLIT = 3
AHEAD = 3
ROUTE_EXP, ROUTE_CHOSEN, ROUTE_STEPS = 5, 9, 17

NEG = -1e30
TAKEN = -3e38


def unit_words(u):
    for b, (kind, _) in enumerate(BLOCKS):
        if kind in WIDTH and first_unit(b) == u:
            return KC * WIDTH[kind]
    return UNIT


def gate_up_unit(b, half):
    return 3 * b - (1 if b else 0) + half


def down_unit(b):
    return 3 * b + 4 if b < FB - 1 else FFN_UNITS - 1


def dve_part(words):
    return (words * 21 // 32) // 8 * 8


class Count:

    def __init__(self, sem, n=0):
        self.sem, self.n = sem, n

    def by(self, instruction, k=1):
        instruction.then_inc(self.sem, k)
        self.n = self.n + k
        return self.n


def trunk(nc, x, pre_stream, moe_stream, gain_cols, final_norm, b_f, consts, out):
    with ExitStack() as ctx:
        def sb(name, shape, dt=F32):
            return ctx.enter_context(nc.sbuf_tensor(name, shape, dt))

        def sem(name):
            return ctx.enter_context(nc.semaphore(name))

        raw = sb("raw", [P, RING * UNIT])
        w_hi = sb("w_hi", [P, SPLIT, UNIT], F32R)
        w_lo = sb("w_lo", [P, SPLIT, UNIT], F32R)
        x_hi = sb("x_hi", [P, KC, SEQ], F32R)
        x_lo = sb("x_lo", [P, KC, SEQ], F32R)
        hid_hi = sb("hid_hi", [P, 2, 2, SEQ], F32R)
        hid_lo = sb("hid_lo", [P, 2, 2, SEQ], F32R)
        h = sb("h", [P, T, D])
        xhat = sb("xhat", [P, T, D])
        scratch = sb("scratch", [P, 2304])
        cst = sb("cst", [P, 5 * P + LOG + 4 * HD])
        score = sb("score", [P, LOG])
        masks = sb("masks", [P, LOG])
        gains = sb("gains", [P, 5 * KC])
        bf_rows = sb("bf_rows", [P, HEADS])
        small = sb("small", [P, 480])
        flag = sb("flag", [P, 1], I32)
        ps = ctx.enter_context(nc.psum_tensor("ps", [P, 8, HALF], F32))

        region = raw[:, RING_PRE * UNIT:RING * UNIT]
        qT = region[:, 0:2048].rearrange("p (c t) -> p c t", c=KC)
        kT = region[:, 2048:4096].rearrange("p (c t) -> p c t", c=KC)
        val = region[:, 4096:6144].rearrange("p (t d) -> p t d", t=T)
        qiT = region[:, 6144:7168].rearrange("p (c t) -> p c t", c=IDX_HEADS // 2)
        kiT = region[:, 7168:7424]
        relu = region[:, 7424:7424 + 2 * LOG].rearrange("p (b n) -> p b n", b=2)
        stage = scratch[:, 0:1024].rearrange("p (t n) -> p t n", t=T)
        turned = scratch[:, 1024:2048].rearrange("p (t n) -> p t n", t=T)
        logit = scratch[:, 0:2 * LOG].rearrange("p (b n) -> p b n", b=2)
        prob = scratch[:, 2 * LOG:4 * LOG].rearrange("p (b n) -> p b n", b=2)
        probT = scratch[:, 4 * LOG:6 * LOG].rearrange("p (b n) -> p b n", b=2)
        silu = scratch[:, 0:512].rearrange("p (b n) -> p b n", b=2)
        hid = scratch[:, 512:1024].rearrange("p (b n) -> p b n", b=2)
        y_out = scratch[:, 1024:2048]
        gateT = scratch[:, 2048:2304]
        pick = score[:, 0:256].rearrange("p (t s) -> p t s", t=T)
        pick_gate = masks[:, 0:256].rearrange("p (t s) -> p t s", t=T)
        ident = cst[:, 0:P]
        upper = cst[:, P:2 * P]
        ones = cst[:, 2 * P:3 * P]
        iota1 = cst[:, 3 * P:4 * P]
        chunk_mask = cst[:, 4 * P:5 * P]
        causal = cst[:, 5 * P:5 * P + LOG]
        cos = cst[:, 5 * P + LOG:5 * P + LOG + 2 * HD].rearrange("p (t n) -> p t n", t=T)
        sin = cst[:, 5 * P + LOG + 2 * HD:5 * P + LOG + 4 * HD].rearrange("p (t n) -> p t n", t=T)
        neg_fT = sb("neg_fT", [P, SEQ])
        at = [0]

        def part(n):
            at[0] += n
            assert at[0] <= 480
            return small[:, at[0] - n:at[0]]

        ssq, ms, std, rstd = part(10), part(10), part(10), part(10)
        wi = part(16).rearrange("p (t n) -> p t n", t=T)
        top8 = part(16).rearrange("p (t n) -> p t n", t=T)
        row_max, neg_max, row_sum, row_inv, full_max = part(32), part(32), part(32), part(32), part(32)
        fz = part(32).rearrange("p (t n) -> p t n", t=T)
        fa, fe, fl, lf = part(32), part(32), part(32), part(32)
        f_tok = part(32).rearrange("p (t n) -> p t n", t=T)
        r_in = row_max[:, 0:28].rearrange("p (t n) -> p t n", t=T)
        r_out = neg_max[:, 0:28].rearrange("p (t n) -> p t n", t=T)
        r_top = row_sum[:, 0:16].rearrange("p (t n) -> p t n", t=T)
        r_rep = row_inv[:, 0:16].rearrange("p (t n) -> p t n", t=T)
        chosen = full_max[:, 0:16].rearrange("p (t n) -> p t n", t=T)
        r_exp = fa[:, 0:16].rearrange("p (t n) -> p t n", t=T)
        gate = fe[:, 0:16].rearrange("p (t n) -> p t n", t=T)
        slot = fl[:, 0:16].rearrange("p (t n) -> p t n", t=T)
        r_den, r_inv, r_neg = lf[:, 0:2], lf[:, 2:4], lf[:, 4:6]
        r_most = lf[:, 6:7]
        fin_gain = raw[:, 0:D]

        x_landed, consts_landed, small_landed = sem("x_landed"), sem("consts_landed"), sem("small_landed")
        landed = [sem(f"landed{s}") for s in range(RING)]
        hi_made, lo_made_dve, lo_made_pool, used = sem("hi_made"), sem("lo_made_dve"), sem("lo_made_pool"), sem("used")
        squares, mean_made, std_made, rstd_made, xhat_made = (sem(n) for n in ("squares", "mean_made", "std_made", "rstd_made", "xhat_made"))
        spread_turned, spread_hi, spread_lo = sem("spread_turned"), sem("spread_hi"), sem("spread_lo")
        tile0_done, evict_dve, evict_act = sem("tile0_done"), sem("evict_dve"), sem("evict_act")
        rope_cos, rope_done, block_turned, turned_out = sem("rope_cos"), sem("rope_done"), sem("block_turned"), sem("turned_out")
        index_key_copy = sem("index_key_copy")
        index_done, relu_done, score_step = sem("index_done"), sem("relu_done"), sem("score_step")
        mask_made = sem("mask_made")
        logits_done, masked, exp_done, probs_turned, probT_made = (sem(n) for n in ("logits_done", "masked", "exp_done", "probs_turned", "probT_made"))
        pv_done, inv_made, head_out = sem("pv_done"), sem("inv_made"), sem("head_out")
        max_step = sem("max_step")
        f_step, f_exp, f_ln, f_cum, f_out, padded = (sem(n) for n in ("f_step", "f_exp", "f_ln", "f_cum", "f_out", "padded"))
        gu_tile0, silu_done, hid_done, hid_turned, hid_hi_made, hid_lo_made = (sem(n) for n in (
            "gu_tile0", "silu_done", "hid_done", "hid_turned", "hid_hi_made", "hid_lo_made"))
        added = sem("added")
        route_step, route_exp, route_cum = sem("route_step"), sem("route_exp"), sem("route_cum")
        pick_made, gathered, token_hi, token_lo = sem("pick_made"), sem("gathered"), sem("token_hi"), sem("token_lo")
        gate_picked, scattered = sem("gate_picked"), sem("scattered")
        shifted = sem("shifted")
        h_final, gain_landed, out_made, stored = sem("h_final"), sem("gain_landed"), sem("out_made"), sem("stored")

        def raw_slot(u):
            if u < PRE:
                return u % RING_PRE, u // RING_PRE + 1
            m = u - PRE
            s = m % RING
            return s, (sum(1 for v in range(PRE) if v % RING_PRE == s)) + m // RING + 1

        def raw_at(s, words):
            return raw[:, s * UNIT:s * UNIT + words]

        def words_of(u):
            return unit_words(u) if u < PRE else UNIT

        SPREAD = [0, None, 1, 2, 3, None, 4]
        block_evict = []
        n_dve = n_act = 0
        for kind, _ in BLOCKS:
            for t in range(T):
                if kind in ("v", "copy_k", "copy_q"):
                    n_act += 1
                    block_evict.append((evict_act, n_act))
                else:
                    n_dve += 1
                    block_evict.append((evict_dve, n_dve))
        TURNING = [b for b, (kind, _) in enumerate(BLOCKS) if kind.startswith(("rope", "copy", "tail_a"))]
        ROPING = [b for b, (kind, _) in enumerate(BLOCKS) if kind.startswith(("rope", "tail_a"))]

        TURNED = T * len(TURNING)

        def turn_no(b, t):
            return T * TURNING.index(b) + t + 1

        def rope_no(b, t):
            return T * ROPING.index(b) + t + 1

        def evict_of(b, t):
            return block_evict[T * b + t]

        def bank_of(b, t):
            return (b % 2) * 2 + t

        def block_ready(eng, b, t):
            if t == 0:
                eng.wait_ge(tile0_done, b + 1)
            else:
                eng.wait_ge(used, units_of(b)[-1] + 1)

        def moe_used(eng, it, m):
            eng.wait_ge(used, it * (2 * FFN_UNITS) + (PRE + m + 1))

        def units_of(b):
            n = 1 if BLOCKS[b][0] in WIDTH else 2
            return range(first_unit(b), first_unit(b) + n)

        block = ctx.enter_context(nc.Block())

        @block.sync
        def _(sp):
            sp.dma_start(h[:, :, :], x[0].rearrange("(t p) d -> p t d", p=P)).then_inc(x_landed, 16)

            def load(u):
                words = words_of(u)
                s, _ = raw_slot(u)
                src = pre_stream[u, :, 0:words] if u < PRE else moe_stream[u - PRE, :, :]
                sp.dma_start(raw_at(s, words), src).then_inc(landed[s], 16)

            def split_done(n):
                sp.wait_ge(lo_made_dve, n)
                sp.wait_ge(lo_made_pool, n)

            for u in range(RING_PRE):
                if u == 1:
                    sp.dma_start(cst[:, :], consts).then_inc(consts_landed, 16)
                    sp.dma_start(gains[:, :], gain_cols).then_inc(small_landed, 16)
                    sp.dma_start(bf_rows[:, :], b_f.partition_broadcast(P)).then_inc(small_landed, 16)
                load(u)
            for u in range(RING_PRE, PRE):
                split_done(u - RING_PRE + 1)
                load(u)
            for m in range(RING):
                if m < RING_PRE:
                    split_done(max(v for v in range(PRE) if v % RING_PRE == m) + 1)
                elif m == RING_PRE:
                    sp.wait_ge(pv_done, 2 * HEADS)
                load(PRE + m)

            def stream(first, last, back):
                with sp.Fori(first, last) as j:
                    for s in range(RING):
                        split_done(j * RING + (PRE - RING + s + 1))
                        sp.dma_start(raw_at(s, UNIT), moe_stream[j * RING + (s - back)]).then_inc(landed[s], 16)

            stream(1, MOE_UNITS // RING, 0)
            sp.wait_ge(route_step, ROUTE_STEPS)
            with sp.If(sp.value_load(flag[0:1, 0:1], min_val=0, max_val=1) > 0):
                stream(MOE_UNITS // RING, 2 * MOE_UNITS // RING, MOE_UNITS)
            sp.wait_ge(h_final, 1)
            sp.dma_start(fin_gain, final_norm.partition_broadcast(P)).then_inc(gain_landed, 16)
            for t in range(T):
                sp.wait_ge(out_made, t + 1)
                sp.dma_start(out[0, t * P:(t + 1) * P, :], xhat[:, t, :]).then_inc(stored, 16)
            sp.wait_ge(stored, 16 * T)

        @block.scalar
        def _(act):
            def hi(u):
                s, n = raw_slot(u)
                words = words_of(u)
                act.wait_ge(landed[s], 16 * n)
                if u >= SPLIT:
                    act.wait_ge(used, u - (SPLIT - 1))
                nc.scalar.activation(w_hi[:, u % SPLIT, 0:words], raw_at(s, words), ACT.Copy).then_inc(hi_made, 1)

            def norm(n):
                for t in range(T):
                    nc.scalar.activation(xhat[:, t, :], h[:, t, :], ACT.Square,
                                         accum_out=ssq[:, 2 * n + t:2 * n + t + 1]).then_inc(squares, 1)
                act.wait_ge(mean_made, n + 1)
                c = 2 * n
                nc.scalar.activation(std[:, c:c + 2], ms[:, c:c + 2], ACT.Sqrt).then_inc(std_made, 1)

            def spread(s):
                for j in range(KC // 2):
                    act.wait_ge(spread_turned, 4 * s + j + 1)
                    if s == 0 and j == 0:
                        act.wait_ge(small_landed, 32)
                    for c in (2 * j, 2 * j + 1):
                        src = ps[:, 4 + j % 2, (c % 2) * SEQ:(c % 2 + 1) * SEQ]
                        g = SPREAD[s]
                        scale = 1.0 if g is None else gains[:, g * KC + c:g * KC + c + 1]
                        nc.scalar.activation(x_hi[:, c, :], src, ACT.Copy, scale=scale).then_inc(spread_hi, 1)

            def turn_out(b):
                kind, c = BLOCKS[b]
                for t in range(T):
                    act.wait_ge(block_turned, turn_no(b, t))
                    src = ps[:, 4 + t, :].rearrange("p (c n) -> p c n", c=4)
                    tok = slice(t * P, (t + 1) * P)
                    if kind == "tail_a":
                        nc.scalar.activation(kiT[:, tok], ps[:, 4 + t, 0:P], ACT.Copy).then_inc(turned_out, 1)
                    else:
                        dst = {"rope_index": qiT}.get(kind, kT if kind.endswith("k") else qT)
                        scale = HD ** -0.5 if kind.endswith("q") else 1.0
                        nc.scalar.activation(dst[:, 4 * c:4 * c + 4, tok], src, ACT.Copy, scale=scale).then_inc(turned_out, 1)

            def use(u):
                hi(u + AHEAD)

            def after_block(b):
                kind, c = BLOCKS[b]
                if kind == "v":
                    for t in range(T):
                        block_ready(act, b, t)
                        nc.scalar.activation(val[:, t, c * HALF:(c + 1) * HALF], ps[:, bank_of(b, t), :],
                                             ACT.Copy).then_inc(evict_act, 1)
                if kind in ("copy_k", "copy_q"):
                    for t in range(T):
                        block_ready(act, b, t)
                        if t == 0 and b - 1 in TURNING:
                            act.wait_ge(block_turned, turn_no(b - 1, T - 1))
                        nc.scalar.activation(stage[:, t, :], ps[:, bank_of(b, t), :], ACT.Copy).then_inc(evict_act, 1)

            def blocks(bs):
                for b in bs:
                    for u in units_of(b):
                        use(u)
                    if b - 1 in bs and b - 1 in TURNING:
                        turn_out(b - 1)
                    after_block(b)
                    if b == 3:
                        for i in range(IDX_HEADS):
                            act.wait_ge(index_done, i + 1)
                            if i >= 2:
                                act.wait_ge(score_step, 2 * (i - 1))
                            nc.scalar.activation(relu[:, i % 2, :], ps[:, 6 + i % 2, 0:LOG], ACT.Relu).then_inc(relu_done, 1)
                if bs[-1] in TURNING:
                    turn_out(bs[-1])

            def attention(k):
                for n in range(HEADS + 1):
                    if n < HEADS:
                        g = k * HEADS + n
                        act.wait_ge(masked, g + 1)
                        if n >= 2:
                            act.wait_ge(probs_turned, g - 1)
                        for t, cols in ((0, slice(0, P)), (1, slice(P, LOG))):
                            nc.scalar.activation(prob[:, n % 2, cols], logit[:, n % 2, cols], ACT.Exp,
                                                 bias=neg_max[:, 2 * n + t:2 * n + t + 1],
                                                 accum_out=row_sum[:, 2 * n + t:2 * n + t + 1]).then_inc(exp_done, 1)
                    if n >= 1:
                        g = k * HEADS + n - 1
                        act.wait_ge(probs_turned, g + 1)
                        if n - 1 >= 2:
                            act.wait_ge(pv_done, g - 1)
                        nc.scalar.activation(probT[:, (n - 1) % 2, :], ps[:, 4 + (n - 1) % 2, 0:LOG], ACT.Copy).then_inc(probT_made, 1)

            act.wait_ge(x_landed, 16)
            norm(0)
            for u in range(AHEAD):
                hi(u)
            spread(0)
            blocks(B_A)
            attention(0)
            spread(1)
            blocks(B_OUT_A)
            act.wait_ge(evict_dve, evict_of(B_OUT_A[-1], T - 1)[1])
            norm(1)
            spread(2)
            for b in range(FB + 1):
                if b < FB:
                    use(DENSE_U + gate_up_unit(b, 0))
                if b >= 1:
                    act.wait_ge(hid_turned, b)
                    if b >= 3:
                        act.wait_ge(used, DENSE_U + down_unit(b - 3) + 1)
                    nc.scalar.activation(hid_hi[:, (b - 1) % 2, :, :],
                                         ps[:, 6 + (b - 1) % 2, :].rearrange("p (c n) -> p c n", c=2),
                                         ACT.Copy).then_inc(hid_hi_made, 1)
                if b < FB:
                    use(DENSE_U + gate_up_unit(b, 1))
                    for t in range(T):
                        if t == 0:
                            act.wait_ge(gu_tile0, b + 1)
                        else:
                            act.wait_ge(used, DENSE_U + gate_up_unit(b, 1) + 1)
                        if b >= 1:
                            act.wait_ge(hid_done, T * (b - 1) + t + 1)
                        nc.scalar.activation(silu[:, t, :], ps[:, 4 + t, 0:256], ACT.Silu).then_inc(silu_done, 1)
                if b >= 1:
                    use(DENSE_U + down_unit(b - 1))
            act.wait_ge(added, 4)
            norm(2)
            spread(3)
            blocks(B_KV)
            act.wait_ge(f_step, 2)
            nc.scalar.activation(fe[:, :], fa[:, :], ACT.Exp, scale=-1.0).then_inc(f_exp, 1)
            act.wait_ge(f_exp, 1)
            nc.scalar.activation(fl[:, :], fe[:, :], ACT.Ln, bias=1.0).then_inc(f_ln, 1)
            spread(4)
            blocks(B_Q)
            attention(1)
            spread(5)
            blocks(B_OUT_B)
            act.wait_ge(evict_dve, evict_of(B_OUT_B[-1], T - 1)[1])
            norm(3)
            spread(6)
            blocks([B_ROUTER])
            act.wait_ge(route_step, ROUTE_EXP)
            for t in range(T):
                nc.scalar.activation(r_exp[:, t, :], r_in[:, t, 0:EXPERTS], ACT.Exp, bias=r_neg[:, t:t + 1]).then_inc(route_exp, 1)

            def hi_moe(it, m):
                s = m % RING
                _, n = raw_slot(PRE + m)
                act.wait_ge(landed[s], it * (16 * 2 * FFN_UNITS // RING) + 16 * n)
                moe_used(act, it, m - SPLIT)
                nc.scalar.activation(w_hi[:, (PRE + m) % SPLIT, :], raw_at(s, UNIT), ACT.Copy).then_inc(hi_made, 1)

            def tokens_out(it, e, buf):
                act.wait_ge(gathered, it * 2 + (e + 1))
                for c in range(KC):
                    nc.scalar.activation(x_hi[:, c, buf * P:(buf + 1) * P],
                                         ps[:, 6 + c // 4, (c % 4) * P:(c % 4 + 1) * P], ACT.Copy,
                                         scale=gains[:, 4 * KC + c:4 * KC + c + 1]).then_inc(token_hi, 1)

            def silu_moe(it, n):
                moe_used(act, it, FFN_UNITS * (n // FB) + gate_up_unit(n % FB, 1))
                act.wait_ge(hid_done, it * (2 * FB) + (T * FB + n - 1))
                nc.scalar.activation(silu[:, n % 2, :], ps[:, 2 + n % 2, 0:256], ACT.Silu).then_inc(silu_done, 1)

            def hid_moe(it, n):
                act.wait_ge(hid_turned, it * (2 * FB) + (FB + n + 1))
                moe_used(act, it, FFN_UNITS * ((n - 2) // FB) + down_unit((n - 2) % FB))
                nc.scalar.activation(hid_hi[:, n % 2, :, 0:P],
                                     ps[:, 4 + n % 2, 0:256].rearrange("p (c n) -> p c n", c=2),
                                     ACT.Copy).then_inc(hid_hi_made, 1)

            def expert(it, e, last):
                m, n = FFN_UNITS * e + 2, FB * e
                end = MOE_UNITS * (1 + (e >= EXPERTS))
                used_up = [m]

                def step():
                    u = used_up[0] + AHEAD
                    used_up[0] += 1
                    if not (last and u >= end):
                        hi_moe(it, u)

                for b in range(1, FB):
                    step()
                    hid_moe(it, n + b - 1)
                    if b == 7 and not last:
                        tokens_out(it, e + 1, (e + 1) % 2)
                    step()
                    silu_moe(it, n + b)
                    step()
                hid_moe(it, n + FB - 1)
                act.wait_ge(block_turned, it * 2 + (TURNED + e + 1))
                nc.scalar.activation(gateT, ps[:, 4 + (n + FB) % 2, 0:256], ACT.Copy).then_inc(turned_out, 1)
                step()
                moe_used(act, it, FFN_UNITS * e + down_unit(FB - 1))
                nc.scalar.activation(y_out[:, 0:HALF], ps[:, 0, :], ACT.Copy).then_inc(evict_act, 1)
                if not last:
                    step()
                    step()
                    silu_moe(it, n + FB)

            def experts(second):
                e0 = EXPERTS * second
                m0 = MOE_UNITS * second
                if second:
                    for m in range(m0, m0 + AHEAD):
                        hi_moe(0, m)
                tokens_out(0, e0, 0)
                hi_moe(0, m0 + AHEAD)
                hi_moe(0, m0 + AHEAD + 1)
                silu_moe(0, FB * e0)
                with act.Fori(0, EXPERTS // 2 - 1) as it:
                    for p in range(2):
                        expert(it, e0 + p, False)
                expert(0, e0 + EXPERTS - 2, False)
                expert(0, e0 + EXPERTS - 1, True)

            experts(0)
            with act.If(act.value_load(flag[0:1, 0:1], min_val=0, max_val=1) > 0):
                experts(1)
            act.wait_ge(h_final, 1)
            norm(4)

        @block.vector
        def _(dve):
            def lo(u):
                words = words_of(u)
                s, _ = raw_slot(u)
                n = dve_part(words)
                dve.wait_ge(hi_made, u + 1)
                nc.vector.tensor_tensor(w_lo[:, u % SPLIT, 0:n], raw_at(s, n), w_hi[:, u % SPLIT, 0:n].bitcast(F32),
                                        ALU.subtract).then_inc(lo_made_dve, 1)

            def norm(n):
                c = 2 * n
                dve.wait_ge(squares, 2 * (n + 1))
                nc.vector.tensor_scalar(ms[:, c:c + 2], ssq[:, c:c + 2], 1.0 / D, EPS, ALU.mult, ALU.add).then_inc(mean_made, 1)
                dve.wait_ge(std_made, n + 1)
                nc.vector.reciprocal(rstd[:, c:c + 2], std[:, c:c + 2]).then_inc(rstd_made, 1)
                dve.wait_ge(rstd_made, n + 1)
                if n < 4:
                    for t in range(T):
                        nc.vector.tensor_scalar(xhat[:, t, :], h[:, t, :], rstd[:, c + t:c + t + 1], None,
                                                ALU.mult).then_inc(xhat_made, 1)

            def spread(s):
                for j in range(KC // 2):
                    for c in (2 * j, 2 * j + 1):
                        src = ps[:, 4 + j % 2, (c % 2) * SEQ:(c % 2 + 1) * SEQ]
                        g = SPREAD[s]
                        dve.wait_ge(spread_hi, KC * s + 2 * (j + 1))
                        hi_part = x_hi[:, c, :].bitcast(F32)
                        if g is None:
                            ins = nc.vector.tensor_tensor(x_lo[:, c, :], src, hi_part, ALU.subtract)
                        else:
                            ins = nc.vector.scalar_tensor_tensor(x_lo[:, c, :], src, gains[:, g * KC + c:g * KC + c + 1],
                                                                 hi_part, ALU.mult, ALU.subtract)
                        ins.then_inc(spread_lo, 1)

            f_steps = Count(f_step)

            def rope(b):
                kind, _ = BLOCKS[b]
                heads = 1 if kind == "tail_a" else 8
                for t in range(T):
                    block_ready(dve, b, t)
                    if t == 0 and b - 1 in TURNING:
                        dve.wait_ge(block_turned, turn_no(b - 1, T - 1))
                    src = ps[:, bank_of(b, t), 0:heads * HD].rearrange("p (h j d) -> p h j d", j=2, d=HD // 2)
                    w = turned[:, t, 0:heads * HD].rearrange("p (h j d) -> p h j d", j=2, d=HD // 2)
                    if kind == "tail_a":
                        nc.vector.tensor_scalar(wi[:, t, :], ps[:, bank_of(b, t), HD:A_TAIL], IDX_HEADS ** -0.5, None,
                                                ALU.mult).then_inc(rope_cos, 1)
                    c = cos[:, t, :].rearrange("p (j d) -> p j d", j=2)
                    s = sin[:, t, :].rearrange("p (j d) -> p j d", j=2)
                    nc.vector.tensor_tensor(
                        stage[:, t, 0:heads * HD].rearrange("p (h n) -> p h n", n=HD),
                        ps[:, bank_of(b, t), 0:heads * HD].rearrange("p (h n) -> p h n", n=HD),
                        cos[:, t, :].unsqueeze(1).to_broadcast([P, heads, HD]), ALU.mult).then_inc(rope_cos, 1)
                    for j in range(2):
                        ins = nc.vector.tensor_tensor(w[:, :, j, :], src[:, :, 1 - j, :],
                                                      s[:, j:j + 1, :].to_broadcast([P, heads, HD // 2]), ALU.mult)
                        ins.then_inc(rope_cos if j == 0 else evict_dve, 1)

            def forget():
                b = B_KV[-1]
                for t in range(T):
                    block_ready(dve, b, t)
                    nc.vector.tensor_tensor(fz[:, t, :], ps[:, bank_of(b, t), 0:HEADS], bf_rows[:, :], ALU.add).then_inc(evict_dve, 1)
                dve.wait_ge(evict_dve, evict_of(b, T - 1)[1])
                zf = fz.rearrange("p t n -> p (t n)")
                f_steps.by(nc.vector.scalar_tensor_tensor(fa[:, :], zf, -1.0, zf, ALU.mult, ALU.max))
                f_steps.by(nc.vector.tensor_scalar(f_tok.rearrange("p t n -> p (t n)"), zf, 0.0, None, ALU.min))
                dve.wait_ge(f_ln, 1)
                dve.wait_ge(f_step, 2)
                f_steps.by(nc.vector.tensor_tensor(lf[:, :], f_tok.rearrange("p t n -> p (t n)"), fl[:, :], ALU.subtract))
                dve.wait_ge(f_cum, 1)
                nc.vector.tensor_copy(f_tok.rearrange("p t n -> p (t n)"), ps[:, 6, 0:2 * HEADS]).then_inc(f_out, 1)
                nc.vector.memset(neg_fT[:, :], 0.0).then_inc(padded, 1)
                dve.wait_ge(padded, 1)
                nc.vector.tensor_scalar(neg_fT[0:HEADS, :], ps[0:HEADS, 7, 0:SEQ], -1.0, None, ALU.mult).then_inc(f_out, 1)

            def after_block(b):
                kind, c = BLOCKS[b]
                if b in ROPING:
                    rope(b)
                elif kind == "res":
                    for t in range(T):
                        block_ready(dve, b, t)
                        cols = h[:, t, c * HALF:(c + 1) * HALF]
                        nc.vector.tensor_tensor(cols, ps[:, bank_of(b, t), :], cols, ALU.add).then_inc(evict_dve, 1)
                elif kind == "tail_f":
                    forget()
                elif kind == "router":
                    for t in range(T):
                        block_ready(dve, b, t)
                        nc.vector.tensor_copy(r_in[:, t, 0:EXPERTS], ps[:, bank_of(b, t), 0:EXPERTS]).then_inc(evict_dve, 1)

            scores = Count(score_step)
            spans = ((slice(0, P), slice(0, P)), (slice(P, LOG), slice(2 * P, LOG)))

            def add_scores():
                for i in range(IDX_HEADS):
                    dve.wait_ge(relu_done, i + 1)
                    if i:
                        dve.wait_ge(score_step, scores.n)
                    for t, (cols, _) in enumerate(spans):
                        if i == 0:
                            scores.by(nc.vector.tensor_scalar(score[:, cols], relu[:, 0, cols], wi[:, t, 0:1], None, ALU.mult))
                        else:
                            scores.by(nc.vector.scalar_tensor_tensor(score[:, cols], relu[:, i % 2, cols], wi[:, t, i:i + 1],
                                                                     score[:, cols], ALU.mult, ALU.add))
                dve.wait_ge(score_step, scores.n)
                for t, (_, own) in enumerate(spans):
                    scores.by(nc.vector.tensor_tensor(score[:, own], score[:, own], chunk_mask, ALU.add))
                dve.wait_ge(score_step, scores.n)

            def choose_keys():
                for t, (cols, _) in enumerate(spans):
                    scores.by(nc.vector.max(top8[:, t, :], score[:, cols]))
                dve.wait_ge(score_step, scores.n)
                for t, (cols, _) in enumerate(spans):
                    scores.by(nc.vector.match_replace(score[:, cols], top8[:, t, :], score[:, cols], TAKEN))
                dve.wait_ge(score_step, scores.n)

            rounds = [0]

            def blocks(bs):
                for b in bs:
                    for u in units_of(b):
                        lo(u + AHEAD)
                        if b in range(4, 8):
                            choose_keys()
                            rounds[0] += 1
                    after_block(b)
                    if b == 3:
                        add_scores()

            def attention(k):
                for n in range(HEADS + 2):
                    if n < HEADS:
                        g = k * HEADS + n
                        dve.wait_ge(logits_done, g + 1)
                        if n >= 2:
                            dve.wait_ge(exp_done, 2 * (g - 1))
                        for t, cols in ((0, slice(0, P)), (1, slice(P, LOG))):
                            src, dst = ps[:, n % 2, cols], logit[:, n % 2, cols]
                            add = (masks if k == 0 else causal)[:, cols]
                            steps.by(nc.vector.tensor_tensor_reduce(dst, src, add, 1.0, TAKEN, ALU.add, ALU.max,
                                                                    row_max[:, 2 * n + t:2 * n + t + 1]))
                        dve.wait_ge(max_step, steps.n)
                        two = slice(2 * n, 2 * n + 2)
                        if k == 0:
                            nc.vector.tensor_scalar(neg_max[:, two], row_max[:, two], -1.0, None, ALU.mult).then_inc(masked, 1)
                        else:
                            steps.by(nc.vector.tensor_tensor(full_max[:, two], row_max[:, two], f_tok[:, :, n], ALU.add))
                            dve.wait_ge(max_step, steps.n)
                            nc.vector.tensor_tensor(neg_max[:, two], f_tok[:, :, n], full_max[:, two], ALU.subtract).then_inc(masked, 1)
                    if n >= 2:
                        m = n - 2
                        g = k * HEADS + m
                        two = slice(2 * m, 2 * m + 2)
                        dve.wait_ge(exp_done, 2 * (g + 1))
                        nc.vector.reciprocal(row_inv[:, two], row_sum[:, two]).then_inc(inv_made, 1)
                        dve.wait_ge(inv_made, g + 1)
                        dve.wait_ge(pv_done, g + 1)
                        for t in range(T):
                            nc.vector.tensor_scalar(xhat[:, t, m * HD:(m + 1) * HD], ps[:, 6 + m % 2, t * HD:(t + 1) * HD],
                                                    row_inv[:, 2 * m + t:2 * m + t + 1], None, ALU.mult).then_inc(head_out, 1)

            steps = Count(max_step)
            dve.wait_ge(x_landed, 16)
            norm(0)
            for u in range(AHEAD):
                lo(u)
            dve.wait_ge(small_landed, 32)
            spread(0)
            dve.wait_ge(consts_landed, 16)
            blocks(B_A)
            assert rounds[0] * 8 == TOPK
            nc.vector.tensor_scalar(masks[:, :], score[:, :], TAKEN / 2, NEG, ALU.is_gt, ALU.mult).then_inc(mask_made, 1)
            dve.wait_ge(mask_made, 1)
            attention(0)
            spread(1)
            blocks(B_OUT_A)
            norm(1)
            spread(2)
            for b in range(FB + 1):
                if b < FB:
                    lo(DENSE_U + gate_up_unit(b, 0) + AHEAD)
                if b >= 1:
                    dve.wait_ge(hid_hi_made, b)
                    nc.vector.tensor_tensor(hid_lo[:, (b - 1) % 2, :, :],
                                            ps[:, 6 + (b - 1) % 2, :].rearrange("p (c n) -> p c n", c=2),
                                            hid_hi[:, (b - 1) % 2, :, :].bitcast(F32), ALU.subtract).then_inc(hid_lo_made, 1)
                if b < FB:
                    lo(DENSE_U + gate_up_unit(b, 1) + AHEAD)
                    for t in range(T):
                        dve.wait_ge(silu_done, T * b + t + 1)
                        if b >= 1 and t == 0:
                            dve.wait_ge(hid_turned, b)
                        nc.vector.tensor_tensor(hid[:, t, :], ps[:, 4 + t, 256:512], silu[:, t, :], ALU.mult).then_inc(hid_done, 1)
                if b >= 1:
                    lo(DENSE_U + down_unit(b - 1) + AHEAD)
            dve.wait_ge(used, DENSE_U + FFN_UNITS)
            for t in range(T):
                for c in range(2):
                    cols = h[:, t, c * HALF:(c + 1) * HALF]
                    nc.vector.tensor_tensor(cols, ps[:, 2 * t + c, :], cols, ALU.add).then_inc(added, 1)
            norm(2)
            spread(3)
            blocks(B_KV)
            spread(4)
            blocks(B_Q)
            dve.wait_ge(f_out, 2)
            attention(1)
            spread(5)
            blocks(B_OUT_B)
            norm(3)
            spread(6)
            route = Count(route_step)

            def link(ins):
                route.by(ins)
                dve.wait_ge(route_step, route.n)

            nc.vector.memset(r_in[:, :, EXPERTS:14], TAKEN).then_inc(route_step, 1)
            nc.vector.memset(r_rep[:, :, :], TAKEN).then_inc(route_step, 1)
            route.n = 2
            blocks([B_ROUTER])
            dve.wait_ge(evict_dve, n_dve)
            dve.wait_ge(route_step, 2)
            for t in range(T):
                route.by(nc.vector.max(r_top[:, t, :], r_in[:, t, :]))
            dve.wait_ge(route_step, route.n)
            link(nc.vector.tensor_scalar(r_neg, r_top[:, :, 0], -1.0, None, ALU.mult))
            assert route.n == ROUTE_EXP
            link(nc.vector.tensor_copy(r_rep[:, :, 0:2], r_top[:, :, 0:2]))
            for t in range(T):
                route.by(nc.vector.match_replace(r_out[:, t, :], r_rep[:, t, :], r_in[:, t, :], -TAKEN))
            dve.wait_ge(route_step, route.n)
            link(nc.vector.tensor_scalar(chosen, r_out[:, :, 0:EXPERTS], -TAKEN / 2, None, ALU.is_gt))
            assert route.n == ROUTE_CHOSEN
            dve.wait_ge(route_exp, 2)
            link(nc.vector.tensor_tensor(gate, r_exp, chosen, ALU.mult))
            link(nc.vector.tensor_reduce(r_den, gate, AX_X, ALU.add))
            link(nc.vector.reciprocal(r_inv, r_den))
            for t in range(T):
                route.by(nc.vector.tensor_scalar(gate[:, t, :], gate[:, t, :], r_inv[:, t:t + 1], None, ALU.mult))
            dve.wait_ge(route_step, route.n)
            dve.wait_ge(route_cum, 1)
            link(nc.vector.tensor_copy(slot, ps[:, 6, 0:16].rearrange("p (t n) -> p t n", t=T)))
            link(nc.vector.tensor_reduce(r_most, ps[:, 6, 16:24], AX_X, ALU.max))
            link(nc.vector.tensor_scalar(flag[:, :], r_most, float(P), None, ALU.is_gt))
            assert route.n == ROUTE_STEPS

            def lo_moe(it, m):
                s = m % RING
                n = dve_part(UNIT)
                i = (PRE + m) % SPLIT
                dve.wait_ge(hi_made, it * 66 + (PRE + m + 1))
                nc.vector.tensor_tensor(w_lo[:, i, 0:n], raw_at(s, n), w_hi[:, i, 0:n].bitcast(F32),
                                        ALU.subtract).then_inc(lo_made_dve, 1)

            def column(table, t, it, e):
                e = e % EXPERTS
                if isinstance(it, int):
                    return table[:, t, e + 2 * it:e + 2 * it + 1]
                return table[:, t, bass.ds(it * 2 + e, 1)]

            def pick_tokens(it, e):
                dve.wait_ge(gathered, it * 2 + e)
                for t in range(T):
                    ins = nc.vector.tensor_scalar(pick[:, t, :], iota1, column(slot, t, it, e), column(chosen, t, it, e),
                                                  ALU.is_equal, ALU.mult)
                    ins.then_inc(pick_made, 1)

            def pick_gates(it, e):
                dve.wait_ge(block_turned, it * 2 + (TURNED + e))
                for t in range(T):
                    ins = nc.vector.tensor_scalar(pick_gate[:, t, :], iota1, column(slot, t, it, e), column(gate, t, it, e),
                                                  ALU.is_equal, ALU.mult)
                    ins.then_inc(gate_picked, 1)

            def tokens_out(it, e, buf):
                for c in range(KC):
                    dve.wait_ge(token_hi, it * (2 * KC) + (KC * e + 4 * (c // 4 + 1)))
                    nc.vector.scalar_tensor_tensor(x_lo[:, c, buf * P:(buf + 1) * P],
                                                   ps[:, 6 + c // 4, (c % 4) * P:(c % 4 + 1) * P],
                                                   gains[:, 4 * KC + c:4 * KC + c + 1],
                                                   x_hi[:, c, buf * P:(buf + 1) * P].bitcast(F32),
                                                   ALU.mult, ALU.subtract).then_inc(token_lo, 1)

            def hid_moe(it, n):
                dve.wait_ge(silu_done, it * (2 * FB) + (T * FB + n + 1))
                dve.wait_ge(hid_turned, it * (2 * FB) + (FB + n - 1))
                nc.vector.tensor_tensor(hid[:, n % 2, :], ps[:, 2 + n % 2, 256:512], silu[:, n % 2, :], ALU.mult).then_inc(hid_done, 1)

            def hid_lo_moe(it, n):
                dve.wait_ge(hid_hi_made, it * (2 * FB) + (FB + n + 1))
                nc.vector.tensor_tensor(hid_lo[:, n % 2, :, 0:P],
                                        ps[:, 4 + n % 2, 0:256].rearrange("p (c n) -> p c n", c=2),
                                        hid_hi[:, n % 2, :, 0:P].bitcast(F32), ALU.subtract).then_inc(hid_lo_made, 1)

            def expert(it, e, last):
                m, n = FFN_UNITS * e + 2, FB * e
                end = MOE_UNITS * (1 + (e >= EXPERTS))
                used_up = [m]

                def step():
                    u = used_up[0] + AHEAD
                    used_up[0] += 1
                    if not (last and u >= end):
                        lo_moe(it, u)

                for b in range(1, FB):
                    step()
                    hid_lo_moe(it, n + b - 1)
                    if b == 4 and not last:
                        pick_tokens(it, e + 1)
                    if b == 5:
                        pick_gates(it, e)
                    if b == 7 and not last:
                        tokens_out(it, e + 1, (e + 1) % 2)
                    step()
                    hid_moe(it, n + b)
                    step()
                hid_lo_moe(it, n + FB - 1)
                step()
                moe_used(dve, it, FFN_UNITS * e + down_unit(FB - 1))
                nc.vector.tensor_copy(y_out[:, HALF:D], ps[:, 1, :]).then_inc(evict_dve, 1)
                if not last:
                    step()
                for q in range(4):
                    t, c = q // 2, q % 2
                    dve.wait_ge(scattered, it * 8 + (4 * e + q + 1))
                    cols = h[:, t, c * HALF:(c + 1) * HALF]
                    nc.vector.tensor_tensor(cols, ps[:, 6 + q % 2, :], cols, ALU.add).then_inc(added, 1)
                if not last:
                    step()
                    hid_moe(it, n + FB)

            def experts(second):
                e0 = EXPERTS * second
                m0 = MOE_UNITS * second
                if second:
                    dve.wait_ge(gate_picked, 2 * EXPERTS)
                    dve.wait_ge(pick_made, 2 * EXPERTS)
                    nc.vector.tensor_scalar(slot, slot, -float(P), None, ALU.add).then_inc(shifted, 1)
                    dve.wait_ge(shifted, 1)
                    for m in range(m0, m0 + AHEAD):
                        lo_moe(0, m)
                pick_tokens(0, e0)
                tokens_out(0, e0, 0)
                lo_moe(0, m0 + AHEAD)
                lo_moe(0, m0 + AHEAD + 1)
                hid_moe(0, FB * e0)
                with dve.Fori(0, EXPERTS // 2 - 1) as it:
                    for p in range(2):
                        expert(it, e0 + p, False)
                expert(0, e0 + EXPERTS - 2, False)
                expert(0, e0 + EXPERTS - 1, True)

            experts(0)
            with dve.If(dve.value_load(flag[0:1, 0:1], min_val=0, max_val=1) > 0):
                experts(1)
            nc.vector.tensor_copy(top8[:, 0, 0:1], row_sum[:, 0:1]).then_inc(h_final, 1)
            norm(4)
            dve.wait_ge(gain_landed, 16)
            for t in range(T):
                nc.vector.scalar_tensor_tensor(xhat[:, t, :], h[:, t, :], rstd[:, 8 + t:9 + t], fin_gain,
                                               ALU.mult, ALU.mult).then_inc(out_made, 1)

        @block.gpsimd
        def _(pool):
            def lo_part(i, s, words):
                n = dve_part(words)
                nc.gpsimd.tensor_tensor(w_lo[:, i, n:words], raw[:, s * UNIT + n:s * UNIT + words],
                                        w_hi[:, i, n:words].bitcast(F32), ALU.subtract).then_inc(lo_made_pool, 1)

            def lo(u):
                pool.wait_ge(hi_made, u + 1)
                lo_part(u % SPLIT, raw_slot(u)[0], words_of(u))

            def rope(b):
                heads = 1 if BLOCKS[b][0] == "tail_a" else 8
                for t in range(T):
                    pool.wait_ge(evict_dve, evict_of(b, t)[1])
                    a, w = stage[:, t, 0:heads * HD], turned[:, t, 0:heads * HD]
                    if heads == 1:
                        nc.gpsimd.tensor_tensor(stage[:, t, HD:2 * HD], a, w, ALU.add).then_inc(index_key_copy, 1)
                        pool.wait_ge(index_key_copy, t + 1)
                    nc.gpsimd.tensor_tensor(a, a, w, ALU.add).then_inc(rope_done, 1)

            for u in range(AHEAD):
                lo(u)
            for b in range(len(BLOCKS)):
                if b == B_KV[0]:
                    for u in range(DENSE_U, DENSE_U + FFN_UNITS):
                        lo(u + AHEAD)
                for u in units_of(b):
                    lo(u + AHEAD)
                if b in ROPING:
                    rope(b)

            def stream(first, last):
                with pool.Fori(first, last) as j:
                    for m in range(FFN_UNITS):
                        pool.wait_ge(hi_made, j * FFN_UNITS + (PRE + AHEAD + m + 1))
                        lo_part((PRE + AHEAD + m) % SPLIT, (AHEAD + m) % RING, UNIT)

            def tail(base):
                for m in range(base + MOE_UNITS - FFN_UNITS + AHEAD, base + MOE_UNITS):
                    lo(PRE + m)

            stream(0, EXPERTS - 1)
            tail(0)
            with pool.If(pool.value_load(flag[0:1, 0:1], min_val=0, max_val=1) > 0):
                for m in range(MOE_UNITS, MOE_UNITS + AHEAD):
                    lo(PRE + m)
                stream(EXPERTS, 2 * EXPERTS - 1)
                tail(MOE_UNITS)

        @block.tensor
        def _(pe):
            def mm3(dst, xh, xl, wh, wl, first, last):
                pe.matmul(dst, xh, wh, start=first, stop=False)
                pe.matmul(dst, xh, wl, start=False, stop=False)
                return pe.matmul(dst, xl, wh, start=False, stop=last)

            def split_of(u):
                pe.wait_ge(lo_made_dve, u + 1)
                pe.wait_ge(lo_made_pool, u + 1)
                return w_hi[:, u % SPLIT, :], w_lo[:, u % SPLIT, :]

            def spread(s):
                if s in (1, 5):
                    pe.wait_ge(head_out, 2 * HEADS * (1 if s == 1 else 2))
                else:
                    pe.wait_ge(xhat_made, T * {0: 1, 2: 2, 3: 3, 4: 3, 6: 4}[s])
                if s == 4:
                    pe.wait_ge(turned_out, turn_no(B_KV[1], T - 1))
                for j in range(KC // 2):
                    if j >= 2:
                        pe.wait_ge(spread_lo, KC * s + 2 * (j - 1))
                    for c in (2 * j, 2 * j + 1):
                        for t in range(T):
                            at_col = (c % 2) * SEQ + t * P
                            mm = pe.transpose(ps[:, 4 + j % 2, at_col:at_col + P], xhat[:, t, c * P:(c + 1) * P], ident)
                    mm.then_inc(spread_turned, 1)
                pe.wait_ge(spread_lo, KC * (s + 1))

            def project(b):
                kind, _ = BLOCKS[b]
                width = WIDTH.get(kind, HALF)
                us = units_of(b)
                chunks = KC // len(us)
                for i, u in enumerate(us):
                    wh, wl = split_of(u)
                    for t in range(T):
                        for k in range(chunks):
                            c = i * chunks + k
                            cols = slice(k * width, (k + 1) * width)
                            toks = slice(t * P, (t + 1) * P)
                            mm = mm3(ps[:, bank_of(b, t), 0:width], x_hi[:, c, toks], x_lo[:, c, toks],
                                     wh[:, cols], wl[:, cols], c == 0, c == KC - 1)
                        if i == len(us) - 1 and t == 0:
                            mm.then_inc(tile0_done, 1)
                    mm.then_inc(used, 1)

            def turn(b):
                for t in range(T):
                    if b in ROPING:
                        pe.wait_ge(rope_done, rope_no(b, t))
                    else:
                        pe.wait_ge(*evict_of(b, t))
                    before = TURNING.index(b) - 1
                    if before >= 0:
                        pe.wait_ge(turned_out, T * before + t + 1)
                    n = 1 if BLOCKS[b][0] == "tail_a" else 4
                    for i in range(n):
                        mm = pe.transpose(ps[:, 4 + t, i * P:(i + 1) * P], stage[:, t, i * P:(i + 1) * P], ident)
                    mm.then_inc(block_turned, 1)

            def blocks(bs):
                for b in bs:
                    if b - 2 in bs:
                        for t in range(T):
                            pe.wait_ge(*evict_of(b - 2, t))
                    project(b)
                    if b - 1 in bs and b - 1 in TURNING:
                        turn(b - 1)
                    if b == 3:
                        index()
                if bs[-1] in TURNING:
                    turn(bs[-1])

            def index():
                pe.wait_ge(turned_out, turn_no(1, T - 1))
                for i in range(IDX_HEADS):
                    if i >= 2:
                        pe.wait_ge(relu_done, i - 1)
                    rows, c, bank = slice((i % 2) * HD, (i % 2 + 1) * HD), i // 2, 6 + i % 2
                    pe.matmul(ps[:, bank, 0:P], qiT[rows, c, 0:P], kiT[rows, 0:P], start=True, stop=True)
                    pe.matmul(ps[:, bank, P:LOG], qiT[rows, c, P:SEQ], kiT[rows, :], start=True, stop=True).then_inc(index_done, 1)

            def attention(k):
                for n in range(HEADS + 2):
                    if n < HEADS:
                        g = k * HEADS + n
                        if n >= 2:
                            pe.wait_ge(masked, g - 1)
                        rows, c = slice((n % 2) * HD, (n % 2 + 1) * HD), n // 2
                        for t, cols, keys in ((0, slice(0, P), P), (1, slice(P, LOG), SEQ)):
                            mm = pe.matmul(ps[:, n % 2, cols], qT[rows, c, t * P:(t + 1) * P], kT[rows, c, 0:keys],
                                           start=True, stop=(k == 0))
                            if k == 1:
                                mm = pe.matmul(ps[:, n % 2, cols], ident[:, n:n + 1].to_broadcast([P, P]), neg_fT[:, 0:keys],
                                               start=False, stop=True)
                        mm.then_inc(logits_done, 1)
                    if 1 <= n <= HEADS:
                        m = n - 1
                        g = k * HEADS + m
                        pe.wait_ge(exp_done, 2 * (g + 1))
                        if m >= 2:
                            pe.wait_ge(probT_made, g - 1)
                        for i in range(3):
                            mm = pe.transpose(ps[:, 4 + m % 2, i * P:(i + 1) * P], prob[:, m % 2, i * P:(i + 1) * P], ident)
                        mm.then_inc(probs_turned, 1)
                    if n >= 2:
                        m = n - 2
                        g = k * HEADS + m
                        pe.wait_ge(probT_made, g + 1)
                        if m >= 2:
                            pe.wait_ge(head_out, 2 * (g - 1))
                        cols = slice(m * HD, (m + 1) * HD)
                        bank = 6 + m % 2
                        pe.matmul(ps[:, bank, 0:HD], probT[:, m % 2, 0:P], val[:, 0, cols], start=True, stop=True)
                        pe.matmul(ps[:, bank, HD:2 * HD], probT[:, m % 2, P:2 * P], val[:, 0, cols], start=True, stop=False)
                        pe.matmul(ps[:, bank, HD:2 * HD], probT[:, m % 2, 2 * P:LOG], val[:, 1, cols],
                                  start=False, stop=True).then_inc(pv_done, 1)

            def forget():
                pe.wait_ge(f_step, 3)
                l0, l1 = lf[:, 0:HEADS], lf[:, HEADS:2 * HEADS]
                pe.matmul(ps[:, 6, 0:HEADS], upper, l0, start=True, stop=True)
                pe.matmul(ps[:, 6, HEADS:2 * HEADS], ones, l0, start=True, stop=False)
                pe.matmul(ps[:, 6, HEADS:2 * HEADS], upper, l1, start=False, stop=True)
                pe.matmul(ps[0:HEADS, 7, 0:P], l0, upper, start=True, stop=True)
                pe.matmul(ps[0:HEADS, 7, P:SEQ], l0, ones, start=True, stop=False)
                pe.matmul(ps[0:HEADS, 7, P:SEQ], l1, upper, start=False, stop=True).then_inc(f_cum, 1)

            pe.wait_ge(consts_landed, 16)
            spread(0)
            blocks(B_A)
            pe.wait_ge(mask_made, 1)
            pe.wait_ge(*evict_of(7, T - 1))
            pe.wait_ge(turned_out, turn_no(5, T - 1))
            attention(0)
            spread(1)
            blocks(B_OUT_A)
            spread(2)
            for b in range(FB + 1):
                for i in range(2):
                    if b < FB:
                        wh, wl = split_of(DENSE_U + gate_up_unit(b, i))
                        for t in range(T):
                            if b >= 1 and i == 0:
                                pe.wait_ge(hid_done, T * (b - 1) + t + 1)
                            toks = slice(t * P, (t + 1) * P)
                            for k in range(4):
                                c = 4 * i + k
                                mm = mm3(ps[:, 4 + t, :], x_hi[:, c, toks], x_lo[:, c, toks],
                                         wh[:, k * HALF:(k + 1) * HALF], wl[:, k * HALF:(k + 1) * HALF], c == 0, c == KC - 1)
                            if i == 1 and t == 0:
                                mm.then_inc(gu_tile0, 1)
                        mm.then_inc(used, 1)
                    if b >= 1 and i == 0:
                        n = b - 1
                        pe.wait_ge(hid_done, T * (n + 1))
                        if n >= 2:
                            pe.wait_ge(hid_lo_made, n - 1)
                        for c in range(2):
                            for t in range(T):
                                at_col = c * SEQ + t * P
                                mm = pe.transpose(ps[:, 6 + n % 2, at_col:at_col + P], hid[:, t, c * P:(c + 1) * P], ident)
                        mm.then_inc(hid_turned, 1)
                if b >= 1:
                    n = b - 1
                    pe.wait_ge(hid_lo_made, n + 1)
                    wh, wl = split_of(DENSE_U + down_unit(n))
                    for t in range(T):
                        toks = slice(t * P, (t + 1) * P)
                        for c in range(2):
                            for k in range(2):
                                cols = slice(k * D + c * HALF, k * D + (c + 1) * HALF)
                                mm = mm3(ps[:, 2 * t + c, :], hid_hi[:, n % 2, k, toks], hid_lo[:, n % 2, k, toks],
                                         wh[:, cols], wl[:, cols], n == 0 and k == 0, n == FB - 1 and k == 1)
                    mm.then_inc(used, 1)
            spread(3)
            blocks(B_KV)
            forget()
            spread(4)
            blocks(B_Q)
            pe.wait_ge(turned_out, turn_no(B_Q[-1], T - 1))
            pe.wait_ge(*evict_of(B_KV[3], T - 1))
            pe.wait_ge(f_out, 2)
            attention(1)
            spread(5)
            blocks(B_OUT_B)
            spread(6)
            blocks([B_ROUTER])
            pe.wait_ge(route_step, ROUTE_CHOSEN)
            pe.matmul(ps[:, 6, 0:8], upper, chosen[:, 0, :], start=True, stop=True)
            pe.matmul(ps[:, 6, 8:16], ones, chosen[:, 0, :], start=True, stop=False)
            pe.matmul(ps[:, 6, 8:16], upper, chosen[:, 1, :], start=False, stop=True)
            pe.matmul(ps[:, 6, 16:24], ones, chosen[:, 0, :], start=True, stop=False)
            pe.matmul(ps[:, 6, 16:24], ones, chosen[:, 1, :], start=False, stop=True).then_inc(route_cum, 1)

            def split_of_moe(it, m):
                pe.wait_ge(lo_made_dve, it * (2 * FFN_UNITS) + (PRE + m + 1))
                pe.wait_ge(lo_made_pool, it * (2 * FFN_UNITS) + (PRE + m + 1))
                i = (PRE + m) % SPLIT
                return w_hi[:, i, :], w_lo[:, i, :]

            def gather(it, e):
                pe.wait_ge(pick_made, it * 4 + 2 * (e + 1))
                if e >= 1:
                    pe.wait_ge(added, it * 8 + 4 * e)
                for c in range(KC):
                    for t in range(T):
                        mm = pe.matmul(ps[:, 6 + c // 4, (c % 4) * P:(c % 4 + 1) * P], xhat[:, t, c * P:(c + 1) * P],
                                       pick[:, t, :], start=(t == 0), stop=(t == T - 1))
                mm.then_inc(gathered, 1)

            def gate_up(it, e, b, i):
                n = FB * e + b
                if i == 0:
                    pe.wait_ge(hid_done, it * (2 * FB) + (T * FB + n - 1))
                wh, wl = split_of_moe(it, FFN_UNITS * e + gate_up_unit(b, i))
                toks = slice((e % 2) * P, (e % 2 + 1) * P)
                for k in range(4):
                    c = 4 * i + k
                    mm = mm3(ps[:, 2 + n % 2, :], x_hi[:, c, toks], x_lo[:, c, toks],
                             wh[:, k * HALF:(k + 1) * HALF], wl[:, k * HALF:(k + 1) * HALF], c == 0, c == KC - 1)
                mm.then_inc(used, 1)

            def turn_hid(it, e, b):
                n = FB * e + b
                pe.wait_ge(hid_done, it * (2 * FB) + (T * FB + n + 1))
                pe.wait_ge(hid_lo_made, it * (2 * FB) + (FB + n - 1))
                if b == 0:
                    pe.wait_ge(turned_out, it * 2 + (TURNED + e))
                for c in range(2):
                    mm = pe.transpose(ps[:, 4 + n % 2, c * P:(c + 1) * P], hid[:, n % 2, c * P:(c + 1) * P], ident)
                mm.then_inc(hid_turned, 1)

            def down(it, e, b):
                n = FB * e + b
                pe.wait_ge(hid_lo_made, it * (2 * FB) + (FB + n + 1))
                if b == 0:
                    pe.wait_ge(evict_act, it * 2 + (n_act + e))
                    pe.wait_ge(evict_dve, it * 2 + (n_dve + e))
                wh, wl = split_of_moe(it, FFN_UNITS * e + down_unit(b))
                for c in range(2):
                    for k in range(2):
                        cols = slice(k * D + c * HALF, k * D + (c + 1) * HALF)
                        mm = mm3(ps[:, c, :], hid_hi[:, n % 2, k, 0:P], hid_lo[:, n % 2, k, 0:P],
                                 wh[:, cols], wl[:, cols], b == 0 and k == 0, b == FB - 1 and k == 1)
                mm.then_inc(used, 1)

            def turn_gates(it, e):
                pe.wait_ge(gate_picked, it * 4 + 2 * (e + 1))
                pe.wait_ge(hid_lo_made, it * (2 * FB) + (FB + FB * e + FB - 1))
                for t in range(T):
                    mm = pe.transpose(ps[:, 4 + (FB * e + FB) % 2, t * P:(t + 1) * P], pick_gate[:, t, :], ident)
                mm.then_inc(block_turned, 1)

            def scatter(it, e, last):
                pe.wait_ge(evict_act, it * 2 + (n_act + e + 1))
                pe.wait_ge(evict_dve, it * 2 + (n_dve + e + 1))
                pe.wait_ge(turned_out, it * 2 + (TURNED + e + 1))
                pe.wait_ge(token_lo, it * (2 * KC) + KC * (e + (1 if last else 2)))
                for q in range(4):
                    t, c = q // 2, q % 2
                    if q >= 2:
                        pe.wait_ge(added, it * 8 + (4 + 4 * e + q - 1))
                    pe.matmul(ps[:, 6 + q % 2, :], gateT[:, t * P:(t + 1) * P], y_out[:, c * HALF:(c + 1) * HALF],
                              start=True, stop=True).then_inc(scattered, 1)

            def expert(it, e, last):
                for b in range(1, FB):
                    gate_up(it, e, b, 0)
                    turn_hid(it, e, b - 1)
                    gate_up(it, e, b, 1)
                    down(it, e, b - 1)
                    if b == 6 and not last:
                        gather(it, e + 1)
                turn_hid(it, e, FB - 1)
                turn_gates(it, e)
                down(it, e, FB - 1)
                if not last:
                    pe.wait_ge(token_lo, it * (2 * KC) + KC * (e + 2))
                    gate_up(it, e + 1, 0, 0)
                scatter(it, e, last)
                if not last:
                    gate_up(it, e + 1, 0, 1)

            def experts(second):
                e0 = EXPERTS * second
                gather(0, e0)
                pe.wait_ge(token_lo, KC * (e0 + 1))
                gate_up(0, e0, 0, 0)
                gate_up(0, e0, 0, 1)
                with pe.Fori(0, EXPERTS // 2 - 1) as it:
                    for p in range(2):
                        expert(it, e0 + p, False)
                expert(0, e0 + EXPERTS - 2, False)
                expert(0, e0 + EXPERTS - 1, True)

            experts(0)
            with pe.If(pe.value_load(flag[0:1, 0:1], min_val=0, max_val=1) > 0):
                experts(1)


def constants():
    row, col = np.arange(P)[:, None], np.arange(P)[None, :]
    upper = (row <= col).astype(np.float32)
    chunks = np.where(col // CHUNK <= row // CHUNK, 0.0, NEG)
    own = np.where(col <= row, 0.0, NEG)
    causal = np.concatenate([own, np.zeros((P, P)), own], 1)
    pos = np.arange(SEQ, dtype=np.float32)
    inv_freq = (np.float32(1.0) / (np.float32(10000.0) ** (np.arange(0, HD, 2, dtype=np.float32) / np.float32(HD)))).astype(np.float32)
    ang = pos[:, None] * inv_freq[None, :]
    cos, sin = np.cos(ang), np.sin(ang)
    by_tile = lambda a: a.reshape(T, P, HD).transpose(1, 0, 2).reshape(P, T * HD)
    return np.concatenate([np.eye(P), upper, np.ones((P, P)), np.broadcast_to(col + 1.0, (P, P)), chunks, causal,
                           by_tile(np.concatenate([cos, cos], 1)), by_tile(np.concatenate([-sin, sin], 1))],
                          1).astype(np.float32)


def kernel(x, a_norm, a_w_in, a_w_out, kv_norm, w_kv, b_f, b_norm, b_w_q, b_w_out, ffn_norm, dense_w_gate_up,
           dense_w_down, moe_router, moe_w_gate_up, moe_w_down, final_norm):
    from concourse import bacc
    from concourse.bass_utils import run_bass_kernel_spmd

    def block_units(w, c):
        part = np.asarray(w)[:, c * HALF:(c + 1) * HALF]
        return list(part.reshape(2, 4, P, HALF).transpose(0, 2, 1, 3).reshape(2, P, UNIT))

    def tail_unit(w):
        n = w.shape[1]
        unit = np.zeros((P, UNIT), w.dtype)
        unit[:, 0:KC * n] = np.asarray(w).reshape(KC, P, n).transpose(1, 0, 2).reshape(P, KC * n)
        return [unit]

    def ffn_units(gate_up, down, to):
        gu = gate_up.reshape(2, 4, P, 2, FB, 256).transpose(4, 0, 2, 1, 3, 5).reshape(FB, 2, P, UNIT)
        dn = down.reshape(FB, 2, P, D).transpose(0, 2, 1, 3).reshape(FB, P, UNIT)
        for b in range(FB):
            to[gate_up_unit(b, 0)], to[gate_up_unit(b, 1)], to[down_unit(b)] = gu[b, 0], gu[b, 1], dn[b]

    w_in, w_kv = np.asarray(a_w_in)[0], np.asarray(w_kv)
    hd = HEADS * HD
    q, k, v, qi = 0, hd // HALF, 2 * hd // HALF, 3 * hd // HALF
    units = block_units(w_in, qi) + tail_unit(w_in[:, 3 * hd + HALF:])
    for c in (q, q + 1, k, k + 1, v, v + 1):
        units += block_units(w_in, c)
    for c in range(2):
        units += block_units(a_w_out[0], c)
    dense = np.empty((FFN_UNITS, P, UNIT), np.float32)
    ffn_units(np.asarray(dense_w_gate_up)[0], np.asarray(dense_w_down)[0], dense)
    units += list(dense)
    for c in range(4):
        units += block_units(w_kv, c)
    units += tail_unit(w_kv[:, 2 * hd:])
    for w in (b_w_q, b_w_out):
        for c in range(2):
            units += block_units(w[0], c)
    units += tail_unit(np.asarray(moe_router)[0])
    pre = np.stack(units)
    assert len(pre) == PRE
    moe = np.empty((EXPERTS, FFN_UNITS, P, UNIT), np.float32)
    for e in range(EXPERTS):
        ffn_units(np.asarray(moe_w_gate_up)[0, e], np.asarray(moe_w_down)[0, e], moe[e])
    gain_rows = [a_norm[0], ffn_norm[0], kv_norm, b_norm[0], ffn_norm[1]]
    arrays = {
        "x": np.asarray(x), "pre_stream": pre, "moe_stream": moe.reshape(MOE_UNITS, P, UNIT),
        "gain_cols": np.ascontiguousarray(np.stack([np.asarray(g) for g in gain_rows]).reshape(5 * KC, P).T),
        "final_norm": np.asarray(final_norm), "b_f": np.asarray(b_f), "consts": constants(),
    }
    nc = bacc.Bacc("TRN2", target_bir_lowering=False, num_devices=1)
    aps = {n: nc.dram_tensor(n, a.shape, F32, kind="ExternalInput").ap() for n, a in arrays.items()}
    out = nc.dram_tensor("out", (1, SEQ, D), F32, kind="ExternalOutput").ap()
    trunk(nc, out=out, **aps)
    return run_bass_kernel_spmd(nc, [arrays], core_ids=[0]).results[0]["out"]
```

```python
from contextlib import ExitStack

import numpy as np

import concourse.bass as bass
from concourse import mybir

F32 = mybir.dt.float32
F32R = mybir.dt.float32r
I32 = mybir.dt.int32
ALU = mybir.AluOpType
ACT = mybir.ActivationFunctionType
AX_X = mybir.AxisListType.X

P = 128
SEQ = 256
D = 1024
HEADS = 16
HD = 64
IDX_HEADS = 8
F = 2816
EXPERTS = 8
CHUNK = 64
TOPK = 64
EPS = 1e-6
T = SEQ // P
KC = D // P
FB = F // 256
HALF = 512
UNIT = 4 * HALF
A_TAIL = HD + IDX_HEADS
LOG = P + SEQ

BLOCKS = [
    ("rope_index", 0), ("tail_a", 0), ("rope_q", 0), ("rope_q", 1), ("rope_k", 0), ("rope_k", 1), ("v", 0), ("v", 1),
    ("res", 0), ("res", 1),
    ("copy_k", 0), ("copy_k", 1), ("v", 0), ("v", 1), ("tail_f", 0),
    ("copy_q", 0), ("copy_q", 1),
    ("res", 0), ("res", 1),
    ("router", 0),
]
WIDTH = {"tail_a": A_TAIL, "tail_f": HEADS, "router": EXPERTS}
B_A, B_OUT_A, B_KV, B_Q, B_OUT_B, B_ROUTER = range(0, 8), range(8, 10), range(10, 15), range(15, 17), range(17, 19), 19
SPREAD_A, SPREAD_B = 1, 5
FFN_UNITS = 3 * FB


def first_unit(b):
    before = sum(1 if BLOCKS[i][0] in WIDTH else 2 for i in range(b))
    return before + (FFN_UNITS if b >= 10 else 0)


DENSE_U = first_unit(9) + 2
PRE = first_unit(B_ROUTER) + 1
MOE_UNITS = EXPERTS * FFN_UNITS
RING_PRE = 6
RING = 11
SPLIT = 3
AHEAD = 3
ROUTE_EXP, ROUTE_CHOSEN, ROUTE_STEPS = 5, 9, 17
ZEROED = 5

NEG = -1e30
TAKEN = -3e38


def unit_words(u):
    for b, (kind, _) in enumerate(BLOCKS):
        if kind in WIDTH and first_unit(b) == u:
            return KC * WIDTH[kind]
    return UNIT


def gate_up_unit(b, half):
    return 3 * b - (1 if b else 0) + half


def down_unit(b, blocks=FB):
    return 3 * b + (4 if b < blocks - 1 else 2)


def expert_unit(n, what, half=0):
    second, n = divmod(n, EXPERTS * FB)
    at = gate_up_unit(n, half) if what == "gate_up" else down_unit(n, EXPERTS * FB)
    return second * MOE_UNITS + at


def dve_part(words):
    return (words * 21 // 32) // 8 * 8


class Count:

    def __init__(self, sem, n=0):
        self.sem, self.n = sem, n

    def by(self, instruction, k=1):
        instruction.then_inc(self.sem, k)
        self.n = self.n + k
        return self.n


def trunk(nc, x, pre_stream, moe_stream, gain_cols, final_norm, b_f, consts, out):
    with ExitStack() as ctx:
        def sb(name, shape, dt=F32):
            return ctx.enter_context(nc.sbuf_tensor(name, shape, dt))

        def sem(name):
            return ctx.enter_context(nc.semaphore(name))

        raw = sb("raw", [P, RING * UNIT])
        w_hi = sb("w_hi", [P, SPLIT, UNIT], F32R)
        w_lo = sb("w_lo", [P, SPLIT, UNIT], F32R)
        x_hi = sb("x_hi", [P, KC, SEQ], F32R)
        x_lo = sb("x_lo", [P, KC, SEQ], F32R)
        hid_hi = sb("hid_hi", [P, 2, 2, SEQ], F32R)
        hid_lo = sb("hid_lo", [P, 2, 2, SEQ], F32R)
        h = sb("h", [P, T, D])
        xhat = sb("xhat", [P, T, D])
        scratch = sb("scratch", [P, 2304])
        cst = sb("cst", [P, 5 * P + LOG + 4 * HD])
        score = sb("score", [P, LOG])
        masks = sb("masks", [P, LOG])
        gains = sb("gains", [P, 5 * KC])
        bf_rows = sb("bf_rows", [P, HEADS])
        small = sb("small", [P, 480])
        flag = sb("flag", [P, 1], I32)
        ps = ctx.enter_context(nc.psum_tensor("ps", [P, 8, HALF], F32))

        region = raw[:, RING_PRE * UNIT:RING * UNIT]
        qT = region[:, 0:2048].rearrange("p (c t) -> p c t", c=KC)
        kT = region[:, 2048:6144].rearrange("p (o c t) -> p o c t", o=2, c=KC)
        val = region[:, 6144:8192].rearrange("p (t d) -> p t d", t=T)
        qiT = region[:, 8192:9216].rearrange("p (c t) -> p c t", c=IDX_HEADS // 2)
        relu = region[:, 9216:9216 + 2 * LOG].rearrange("p (b n) -> p b n", b=2)
        kiT_low = region[:, 9984:10240]
        kiT_high = scratch[:, 2048:2304]
        stage = scratch[:, 0:1024].rearrange("p (t n) -> p t n", t=T)
        turned = scratch[:, 1024:2048].rearrange("p (t n) -> p t n", t=T)
        logit = scratch[:, 0:2 * LOG].rearrange("p (b n) -> p b n", b=2)
        prob = scratch[:, 2 * LOG:4 * LOG].rearrange("p (b n) -> p b n", b=2)
        probT = scratch[:, 4 * LOG:6 * LOG].rearrange("p (b n) -> p b n", b=2)
        silu = scratch[:, 0:512].rearrange("p (b n) -> p b n", b=2)
        hid = scratch[:, 512:1024].rearrange("p (b n) -> p b n", b=2)
        y_out = scratch[:, 1024:2048]
        gateT = scratch[:, 2048:2304]
        pick = score[:, 0:256].rearrange("p (t s) -> p t s", t=T)
        pick_gate = masks[:, 0:256].rearrange("p (t s) -> p t s", t=T)
        ident = cst[:, 0:P]
        upper = cst[:, P:2 * P]
        ones = cst[:, 2 * P:3 * P]
        iota1 = cst[:, 3 * P:4 * P]
        chunk_mask = cst[:, 4 * P:5 * P]
        causal = cst[:, 5 * P:5 * P + LOG]
        cos = cst[:, 5 * P + LOG:5 * P + LOG + 2 * HD].rearrange("p (t n) -> p t n", t=T)
        sin = cst[:, 5 * P + LOG + 2 * HD:5 * P + LOG + 4 * HD].rearrange("p (t n) -> p t n", t=T)
        neg_fT = sb("neg_fT", [P, SEQ])
        at = [0]

        def part(n):
            at[0] += n
            assert at[0] <= 480
            return small[:, at[0] - n:at[0]]

        ssq, ms, std, rstd = part(10), part(10), part(10), part(10)
        wi = part(16).rearrange("p (t n) -> p t n", t=T)
        top8 = part(16).rearrange("p (t n) -> p t n", t=T)
        row_max, neg_max, row_sum, row_inv, full_max = part(32), part(32), part(32), part(32), part(32)
        fz = part(32).rearrange("p (t n) -> p t n", t=T)
        fa, fe, fl, lf = part(32), part(32), part(32), part(32)
        f_tok = part(32).rearrange("p (t n) -> p t n", t=T)
        r_in = row_max[:, 0:28].rearrange("p (t n) -> p t n", t=T)
        r_out = neg_max[:, 0:28].rearrange("p (t n) -> p t n", t=T)
        r_top = row_sum[:, 0:16].rearrange("p (t n) -> p t n", t=T)
        r_rep = row_inv[:, 0:16].rearrange("p (t n) -> p t n", t=T)
        chosen = full_max[:, 0:16].rearrange("p (t n) -> p t n", t=T)
        r_exp = fa[:, 0:16].rearrange("p (t n) -> p t n", t=T)
        gate = fe[:, 0:16].rearrange("p (t n) -> p t n", t=T)
        slot = fl[:, 0:16].rearrange("p (t n) -> p t n", t=T)
        r_den, r_inv, r_neg = lf[:, 0:2], lf[:, 2:4], lf[:, 4:6]
        r_most = lf[:, 6:7]
        fin_gain = raw[:, 0:D]

        x_landed, ident_landed, consts_landed, small_landed = (sem(n) for n in (
            "x_landed", "ident_landed", "consts_landed", "small_landed"))
        zeroed = sem("zeroed")
        landed = [sem(f"landed{s}") for s in range(RING)]
        hi_made, lo_made_dve, lo_made_pool, used = sem("hi_made"), sem("lo_made_dve"), sem("lo_made_pool"), sem("used")
        squares, mean_made, std_made, rstd_made, xhat_made = (sem(n) for n in ("squares", "mean_made", "std_made", "rstd_made", "xhat_made"))
        spread_turned, spread_hi, spread_lo = sem("spread_turned"), sem("spread_hi"), sem("spread_lo")
        tile0_done, evict_dve, evict_act = sem("tile0_done"), sem("evict_dve"), sem("evict_act")
        rope_cos, rope_done, block_turned, turned_out = sem("rope_cos"), sem("rope_done"), sem("block_turned"), sem("turned_out")
        index_key_copy = sem("index_key_copy")
        index_done, relu_done, score_step = sem("index_done"), sem("relu_done"), sem("score_step")
        mask_made = sem("mask_made")
        logits_done, masked, exp_done, probs_turned, probT_made = (sem(n) for n in ("logits_done", "masked", "exp_done", "probs_turned", "probT_made"))
        pv_done, inv_made, head_out = sem("pv_done"), sem("inv_made"), sem("head_out")
        max_step = sem("max_step")
        f_step, f_exp, f_ln, f_cum, f_out = (sem(n) for n in ("f_step", "f_exp", "f_ln", "f_cum", "f_out"))
        gu_tile0, silu_done, hid_done, hid_turned, hid_hi_made, hid_lo_made = (sem(n) for n in (
            "gu_tile0", "silu_done", "hid_done", "hid_turned", "hid_hi_made", "hid_lo_made"))
        added = sem("added")
        route_step, route_exp, route_cum = sem("route_step"), sem("route_exp"), sem("route_cum")
        pick_made, gathered, token_hi, token_lo = sem("pick_made"), sem("gathered"), sem("token_hi"), sem("token_lo")
        gate_picked, scattered = sem("gate_picked"), sem("scattered")
        shifted = sem("shifted")
        h_final, gain_landed, out_made, stored = sem("h_final"), sem("gain_landed"), sem("out_made"), sem("stored")

        def raw_slot(u):
            if u < PRE:
                return u % RING_PRE, u // RING_PRE + 1
            m = u - PRE
            s = m % RING
            return s, (sum(1 for v in range(PRE) if v % RING_PRE == s)) + m // RING + 1

        def raw_at(s, words):
            return raw[:, s * UNIT:s * UNIT + words]

        def words_of(u):
            return unit_words(u) if u < PRE else UNIT

        SPREAD = [0, None, 1, 2, 3, None, 4]
        block_evict = []
        n_dve = n_act = 0
        for kind, _ in BLOCKS:
            for t in range(T):
                if kind in ("v", "copy_k", "copy_q"):
                    n_act += 1
                    block_evict.append((evict_act, n_act))
                else:
                    n_dve += 1
                    block_evict.append((evict_dve, n_dve))
        TURNING = [b for b, (kind, _) in enumerate(BLOCKS) if kind.startswith(("rope", "copy", "tail_a"))]
        ROPING = [b for b, (kind, _) in enumerate(BLOCKS) if kind.startswith(("rope", "tail_a"))]

        TURNED = T * len(TURNING)

        def norm_of(b):
            return None if BLOCKS[b][0] == "res" else 0 if b in B_A else 2 if b < B_ROUTER else 3

        def rstd_of(b, t):
            return rstd[:, 2 * norm_of(b) + t:2 * norm_of(b) + t + 1]

        def spread_bank(s, j):
            return 2 + j % 2 if s in (SPREAD_A, SPREAD_B) else 4 + j

        def spread_round(n):
            return (n - 6) // 4 if n >= 6 and n % 4 == 2 else None

        def turn_no(b, t):
            return T * TURNING.index(b) + t + 1

        def rope_no(b, t):
            return T * ROPING.index(b) + t + 1

        def evict_of(b, t):
            return block_evict[T * b + t]

        def bank_of(b, t):
            return ((b + (b >= B_OUT_B[0])) % 2) * 2 + t

        def block_ready(eng, b, t):
            if t == 0:
                eng.wait_ge(tile0_done, b + 1)
            else:
                eng.wait_ge(used, units_of(b)[-1] + 1)

        def moe_used(eng, it, m):
            eng.wait_ge(used, it * (2 * FFN_UNITS) + (PRE + m + 1))

        def units_of(b):
            n = 1 if BLOCKS[b][0] in WIDTH else 2
            return range(first_unit(b), first_unit(b) + n)

        block = ctx.enter_context(nc.Block())

        @block.sync
        def _(sp):
            sp.dma_start(ident, consts[:, 0:P]).then_inc(ident_landed, 16)
            sp.dma_start(h[:, :, :], x[0].rearrange("(t p) d -> p t d", p=P)).then_inc(x_landed, 16)

            def load(u):
                words = words_of(u)
                s, _ = raw_slot(u)
                src = pre_stream[u, :, 0:words] if u < PRE else moe_stream[u - PRE, :, :]
                sp.dma_start(raw_at(s, words), src).then_inc(landed[s], 16)

            def split_done(n):
                sp.wait_ge(lo_made_dve, n)
                sp.wait_ge(lo_made_pool, n)

            sp.dma_start(gains[:, :], gain_cols).then_inc(small_landed, 16)
            sp.dma_start(bf_rows[:, :], b_f.partition_broadcast(P)).then_inc(small_landed, 16)
            for u in range(RING_PRE):
                if u == 2:
                    sp.dma_start(cst[:, P:], consts[:, P:]).then_inc(consts_landed, 16)
                load(u)
            for u in range(RING_PRE, PRE):
                split_done(u - RING_PRE + 1)
                load(u)
            for m in range(RING):
                if m < RING_PRE:
                    split_done(max(v for v in range(PRE) if v % RING_PRE == m) + 1)
                elif m == RING_PRE:
                    sp.wait_ge(pv_done, 2 * HEADS)
                load(PRE + m)

            def stream(first, last, back):
                with sp.Fori(first, last) as j:
                    for s in range(RING):
                        split_done(j * RING + (PRE - RING + s + 1))
                        sp.dma_start(raw_at(s, UNIT), moe_stream[j * RING + (s - back)]).then_inc(landed[s], 16)

            stream(1, MOE_UNITS // RING, 0)
            sp.wait_ge(route_step, ROUTE_STEPS)
            with sp.If(sp.value_load(flag[0:1, 0:1], min_val=0, max_val=1) > 0):
                stream(MOE_UNITS // RING, 2 * MOE_UNITS // RING, MOE_UNITS)
            sp.wait_ge(h_final, 1)
            sp.dma_start(fin_gain, final_norm.partition_broadcast(P)).then_inc(gain_landed, 16)
            for t in range(T):
                sp.wait_ge(out_made, t + 1)
                sp.dma_start(out[0, t * P:(t + 1) * P, :], xhat[:, t, :]).then_inc(stored, 16)
            sp.wait_ge(stored, 16 * T)

        @block.scalar
        def _(act):
            def hi(u):
                s, n = raw_slot(u)
                words = words_of(u)
                act.wait_ge(landed[s], 16 * n)
                if u >= SPLIT:
                    act.wait_ge(used, u - (SPLIT - 1))
                nc.scalar.activation(w_hi[:, u % SPLIT, 0:words], raw_at(s, words), ACT.Copy).then_inc(hi_made, 1)

            def norm(n):
                for t in range(T):
                    nc.scalar.activation(xhat[:, t, :], h[:, t, :], ACT.Square,
                                         accum_out=ssq[:, 2 * n + t:2 * n + t + 1]).then_inc(squares, 1)
                act.wait_ge(mean_made, n + 1)
                c = 2 * n
                nc.scalar.activation(std[:, c:c + 2], ms[:, c:c + 2], ACT.Sqrt).then_inc(std_made, 1)

            def spread(s, rounds=range(KC // 2)):
                for j in rounds:
                    act.wait_ge(spread_turned, 4 * s + j + 1)
                    if s == 0 and j == 0:
                        act.wait_ge(small_landed, 32)
                    for c in (2 * j, 2 * j + 1):
                        src = ps[:, spread_bank(s, j), (c % 2) * SEQ:(c % 2 + 1) * SEQ]
                        g = SPREAD[s]
                        scale = 1.0 if g is None else gains[:, g * KC + c:g * KC + c + 1]
                        nc.scalar.activation(x_hi[:, c, :], src, ACT.Copy, scale=scale).then_inc(spread_hi, 1)

            def turn_out(b):
                kind, c = BLOCKS[b]
                for t in range(T):
                    act.wait_ge(block_turned, turn_no(b, t))
                    src = ps[:, 4 + t, :].rearrange("p (c n) -> p c n", c=4)
                    tok = slice(t * P, (t + 1) * P)
                    low, high = slice(0, HD), slice(HD, P)
                    if kind == "tail_a":
                        nc.scalar.activation(kiT_low[low, tok], ps[low, 4 + t, 0:P], ACT.Copy)
                        nc.scalar.activation(kiT_high[high, tok], ps[high, 4 + t, 0:P], ACT.Copy).then_inc(turned_out, 1)
                    elif kind.endswith("k"):
                        nc.scalar.activation(kT[low, 0, 4 * c:4 * c + 4, tok], src[low], ACT.Copy)
                        nc.scalar.activation(kT[high, 1, 4 * c:4 * c + 4, tok], src[high], ACT.Copy).then_inc(turned_out, 1)
                    else:
                        dst = qiT if kind == "rope_index" else qT
                        scale = HD ** -0.5 if kind.endswith("q") else 1.0
                        nc.scalar.activation(dst[:, 4 * c:4 * c + 4, tok], src, ACT.Copy, scale=scale).then_inc(turned_out, 1)

            def use(u):
                hi(u + AHEAD)

            def after_block(b):
                kind, c = BLOCKS[b]
                if kind in ("v", "copy_k", "copy_q"):
                    act.wait_ge(rstd_made, norm_of(b) + 1)
                if kind == "v":
                    for t in range(T):
                        block_ready(act, b, t)
                        nc.scalar.activation(val[:, t, c * HALF:(c + 1) * HALF], ps[:, bank_of(b, t), :], ACT.Copy,
                                             scale=rstd_of(b, t)).then_inc(evict_act, 1)
                if kind in ("copy_k", "copy_q"):
                    for t in range(T):
                        block_ready(act, b, t)
                        if t == 0 and b - 1 in TURNING:
                            act.wait_ge(block_turned, turn_no(b - 1, T - 1))
                        nc.scalar.activation(stage[:, t, :], ps[:, bank_of(b, t), :], ACT.Copy,
                                             scale=rstd_of(b, t)).then_inc(evict_act, 1)

            def blocks(bs):
                for b in bs:
                    for u in units_of(b):
                        use(u)
                    if b - 1 in bs and b - 1 in TURNING:
                        turn_out(b - 1)
                    after_block(b)
                    if b == 3:
                        for i in range(IDX_HEADS):
                            act.wait_ge(index_done, i + 1)
                            if i >= 2:
                                act.wait_ge(score_step, 2 * (i - 1))
                            nc.scalar.activation(relu[:, i % 2, :], ps[:, 6 + i % 2, 0:LOG], ACT.Relu).then_inc(relu_done, 1)
                if bs[-1] in TURNING:
                    turn_out(bs[-1])

            def attention(k):
                for n in range(HEADS + 3):
                    if n < HEADS:
                        g = k * HEADS + n
                        act.wait_ge(masked, g + 1)
                        if n >= 2:
                            act.wait_ge(probs_turned, g - 1)
                        for t, cols in ((0, slice(0, P)), (1, slice(P, LOG))):
                            nc.scalar.activation(prob[:, n % 2, cols], logit[:, n % 2, cols], ACT.Exp,
                                                 bias=neg_max[:, 2 * n + t:2 * n + t + 1],
                                                 accum_out=row_sum[:, 2 * n + t:2 * n + t + 1]).then_inc(exp_done, 1)
                    if 1 <= n <= HEADS:
                        g = k * HEADS + n - 1
                        act.wait_ge(probs_turned, g + 1)
                        if n - 1 >= 2:
                            act.wait_ge(pv_done, g - 1)
                        nc.scalar.activation(probT[:, (n - 1) % 2, :], ps[:, 4 + (n - 1) % 2, 0:LOG], ACT.Copy).then_inc(probT_made, 1)
                    if spread_round(n) is not None:
                        spread((SPREAD_A, SPREAD_B)[k], [spread_round(n)])

            spread(0)
            for u in range(AHEAD - 1):
                hi(u)
            act.wait_ge(x_landed, 16)
            norm(0)
            hi(AHEAD - 1)
            blocks(B_A)
            attention(0)
            blocks(B_OUT_A)
            spread(2)
            act.wait_ge(evict_dve, evict_of(B_OUT_A[-1], T - 1)[1])
            norm(1)
            act.wait_ge(rstd_made, 2)
            for b in range(FB + 1):
                if b < FB:
                    use(DENSE_U + gate_up_unit(b, 0))
                if b >= 1:
                    act.wait_ge(hid_turned, b)
                    if b >= 3:
                        act.wait_ge(used, DENSE_U + down_unit(b - 3) + 1)
                    nc.scalar.activation(hid_hi[:, (b - 1) % 2, :, :],
                                         ps[:, 6 + (b - 1) % 2, :].rearrange("p (c n) -> p c n", c=2),
                                         ACT.Copy).then_inc(hid_hi_made, 1)
                if b < FB:
                    use(DENSE_U + gate_up_unit(b, 1))
                    for t in range(T):
                        if t == 0:
                            act.wait_ge(gu_tile0, b + 1)
                        else:
                            act.wait_ge(used, DENSE_U + gate_up_unit(b, 1) + 1)
                        if b >= 1:
                            act.wait_ge(hid_done, T * (b - 1) + t + 1)
                        nc.scalar.activation(silu[:, t, :], ps[:, 4 + t, 0:256], ACT.Silu,
                                             scale=rstd[:, 2 + t:3 + t]).then_inc(silu_done, 1)
                if b >= 1:
                    use(DENSE_U + down_unit(b - 1))
            spread(3)
            act.wait_ge(added, 4)
            norm(2)
            blocks(B_KV)
            spread(4)
            act.wait_ge(f_step, 2)
            nc.scalar.activation(fe[:, :], fa[:, :], ACT.Exp, scale=-1.0).then_inc(f_exp, 1)
            act.wait_ge(f_exp, 1)
            nc.scalar.activation(fl[:, :], fe[:, :], ACT.Ln, bias=1.0).then_inc(f_ln, 1)
            blocks(B_Q)
            attention(1)
            blocks(B_OUT_B)
            spread(6)
            act.wait_ge(evict_dve, evict_of(B_OUT_B[-1], T - 1)[1])
            norm(3)
            blocks([B_ROUTER])
            act.wait_ge(route_step, ROUTE_EXP)
            for t in range(T):
                nc.scalar.activation(r_exp[:, t, :], r_in[:, t, 0:EXPERTS], ACT.Exp, bias=r_neg[:, t:t + 1]).then_inc(route_exp, 1)

            def hi_moe(it, m):
                s = m % RING
                _, n = raw_slot(PRE + m)
                act.wait_ge(landed[s], it * (16 * 2 * FFN_UNITS // RING) + 16 * n)
                moe_used(act, it, m - SPLIT)
                nc.scalar.activation(w_hi[:, (PRE + m) % SPLIT, :], raw_at(s, UNIT), ACT.Copy).then_inc(hi_made, 1)

            def tokens_out(it, e, buf):
                act.wait_ge(gathered, it * 2 + (e + 1))
                for c in range(KC):
                    nc.scalar.activation(x_hi[:, c, buf * P:(buf + 1) * P],
                                         ps[:, 6 + c // 4, (c % 4) * P:(c % 4 + 1) * P], ACT.Copy,
                                         scale=gains[:, 4 * KC + c:4 * KC + c + 1]).then_inc(token_hi, 1)

            def silu_moe(it, n):
                moe_used(act, it, expert_unit(n, "gate_up", 1))
                act.wait_ge(hid_done, it * (2 * FB) + (T * FB + n - 1))
                nc.scalar.activation(silu[:, n % 2, :], ps[:, 2 + n % 2, 0:256], ACT.Silu).then_inc(silu_done, 1)

            def hid_moe(it, n):
                act.wait_ge(hid_turned, it * (2 * FB) + (FB + n + 1))
                moe_used(act, it, 3 * (n - 2) + 4)
                nc.scalar.activation(hid_hi[:, n % 2, :, 0:P],
                                     ps[:, 4 + n % 2, 0:256].rearrange("p (c n) -> p c n", c=2),
                                     ACT.Copy).then_inc(hid_hi_made, 1)

            def split_behind(it, m, last):
                if not last or m + AHEAD < MOE_UNITS * (m // MOE_UNITS + 1):
                    hi_moe(it, m + AHEAD)

            def expert(it, e, last):
                for b in range(2, FB if last else FB + 2):
                    n = FB * e + b
                    hid_moe(it, n - 1)
                    split_behind(it, expert_unit(n, "gate_up", 0), last)
                    if b == 7 and not last:
                        tokens_out(it, e + 1, (e + 1) % 2)
                    if b == 8:
                        act.wait_ge(block_turned, it * 2 + (TURNED + e + 1))
                        nc.scalar.activation(gateT, ps[:, 4 + n % 2, 0:256], ACT.Copy).then_inc(turned_out, 1)
                    silu_moe(it, n)
                    split_behind(it, expert_unit(n, "gate_up", 1), last)
                    if b == FB:
                        y_out_of_psum(it, e)
                    split_behind(it, expert_unit(n - 1, "down"), last)
                if last:
                    hid_moe(it, FB * e + FB - 1)
                    y_out_of_psum(it, e)

            def y_out_of_psum(it, e):
                moe_used(act, it, expert_unit(FB * e + FB - 1, "down"))
                nc.scalar.activation(y_out[:, 0:HALF], ps[:, 0, :], ACT.Copy).then_inc(evict_act, 1)

            def experts(second):
                e0, n0, m0 = EXPERTS * second, EXPERTS * FB * second, MOE_UNITS * second
                if second:
                    for m in range(m0, m0 + AHEAD):
                        hi_moe(0, m)
                tokens_out(0, e0, 0)
                hi_moe(0, m0 + AHEAD)
                silu_moe(0, n0)
                hi_moe(0, m0 + AHEAD + 1)
                hid_moe(0, n0)
                hi_moe(0, m0 + AHEAD + 2)
                silu_moe(0, n0 + 1)
                hi_moe(0, m0 + AHEAD + 3)
                hi_moe(0, m0 + AHEAD + 4)
                with act.Fori(0, EXPERTS // 2 - 1) as it:
                    for p in range(2):
                        expert(it, e0 + p, False)
                expert(0, e0 + EXPERTS - 2, False)
                expert(0, e0 + EXPERTS - 1, True)

            experts(0)
            with act.If(act.value_load(flag[0:1, 0:1], min_val=0, max_val=1) > 0):
                experts(1)
            act.wait_ge(h_final, 1)
            norm(4)

        @block.vector
        def _(dve):
            def lo(u):
                words = words_of(u)
                s, _ = raw_slot(u)
                n = dve_part(words)
                dve.wait_ge(hi_made, u + 1)
                nc.vector.tensor_tensor(w_lo[:, u % SPLIT, 0:n], raw_at(s, n), w_hi[:, u % SPLIT, 0:n].bitcast(F32),
                                        ALU.subtract).then_inc(lo_made_dve, 1)

            def norm(n):
                c = 2 * n
                dve.wait_ge(squares, 2 * (n + 1))
                nc.vector.tensor_scalar(ms[:, c:c + 2], ssq[:, c:c + 2], 1.0 / D, EPS, ALU.mult, ALU.add).then_inc(mean_made, 1)
                dve.wait_ge(std_made, n + 1)
                nc.vector.reciprocal(rstd[:, c:c + 2], std[:, c:c + 2]).then_inc(rstd_made, 1)
                dve.wait_ge(rstd_made, n + 1)
                if n == 3:
                    for t in range(T):
                        nc.vector.tensor_scalar(xhat[:, t, :], h[:, t, :], rstd[:, c + t:c + t + 1], None,
                                                ALU.mult).then_inc(xhat_made, 1)

            def spread(s, rounds=range(KC // 2)):
                for j in rounds:
                    for c in (2 * j, 2 * j + 1):
                        src = ps[:, spread_bank(s, j), (c % 2) * SEQ:(c % 2 + 1) * SEQ]
                        g = SPREAD[s]
                        dve.wait_ge(spread_hi, KC * s + 2 * (j + 1))
                        hi_part = x_hi[:, c, :].bitcast(F32)
                        if g is None:
                            ins = nc.vector.tensor_tensor(x_lo[:, c, :], src, hi_part, ALU.subtract)
                        else:
                            ins = nc.vector.scalar_tensor_tensor(x_lo[:, c, :], src, gains[:, g * KC + c:g * KC + c + 1],
                                                                 hi_part, ALU.mult, ALU.subtract)
                        ins.then_inc(spread_lo, 1)

            f_steps = Count(f_step)

            def rope(b):
                kind, _ = BLOCKS[b]
                heads = 1 if kind == "tail_a" else 8
                for t in range(T):
                    block_ready(dve, b, t)
                    if t == 0 and b - 1 in TURNING:
                        dve.wait_ge(block_turned, turn_no(b - 1, T - 1))
                    src = ps[:, bank_of(b, t), 0:heads * HD].rearrange("p (h j d) -> p h j d", j=2, d=HD // 2)
                    w = turned[:, t, 0:heads * HD].rearrange("p (h j d) -> p h j d", j=2, d=HD // 2)
                    if kind == "tail_a":
                        nc.vector.tensor_scalar(wi[:, t, :], ps[:, bank_of(b, t), HD:A_TAIL], rstd_of(b, t),
                                                IDX_HEADS ** -0.5, ALU.mult, ALU.mult).then_inc(rope_cos, 1)
                    s = sin[:, t, :].rearrange("p (j d) -> p j d", j=2)
                    nc.vector.scalar_tensor_tensor(
                        stage[:, t, 0:heads * HD].rearrange("p (h n) -> p h n", n=HD),
                        ps[:, bank_of(b, t), 0:heads * HD].rearrange("p (h n) -> p h n", n=HD), rstd_of(b, t),
                        cos[:, t, :].unsqueeze(1).to_broadcast([P, heads, HD]), ALU.mult, ALU.mult).then_inc(rope_cos, 1)
                    for j in range(2):
                        ins = nc.vector.scalar_tensor_tensor(w[:, :, j, :], src[:, :, 1 - j, :], rstd_of(b, t),
                                                             s[:, j:j + 1, :].to_broadcast([P, heads, HD // 2]),
                                                             ALU.mult, ALU.mult)
                        ins.then_inc(rope_cos if j == 0 else evict_dve, 1)

            def forget():
                b = B_KV[-1]
                for t in range(T):
                    block_ready(dve, b, t)
                    nc.vector.scalar_tensor_tensor(fz[:, t, :], ps[:, bank_of(b, t), 0:HEADS], rstd_of(b, t), bf_rows[:, :],
                                                   ALU.mult, ALU.add).then_inc(evict_dve, 1)
                dve.wait_ge(evict_dve, evict_of(b, T - 1)[1])
                zf = fz.rearrange("p t n -> p (t n)")
                f_steps.by(nc.vector.scalar_tensor_tensor(fa[:, :], zf, -1.0, zf, ALU.mult, ALU.max))
                f_steps.by(nc.vector.tensor_scalar(f_tok.rearrange("p t n -> p (t n)"), zf, 0.0, None, ALU.min))

            def forget_sum():
                dve.wait_ge(f_ln, 1)
                dve.wait_ge(f_step, 2)
                f_steps.by(nc.vector.tensor_tensor(lf[:, :], f_tok.rearrange("p t n -> p (t n)"), fl[:, :], ALU.subtract))

            def forget_out():
                dve.wait_ge(f_cum, 1)
                nc.vector.tensor_copy(f_tok.rearrange("p t n -> p (t n)"), ps[:, 6, 0:2 * HEADS]).then_inc(f_out, 1)
                dve.wait_ge(zeroed, ZEROED)
                nc.vector.tensor_scalar(neg_fT[0:HEADS, :], ps[0:HEADS, 7, 0:SEQ], -1.0, None, ALU.mult).then_inc(f_out, 1)

            def after_block(b):
                kind, c = BLOCKS[b]
                if b in ROPING:
                    rope(b)
                elif kind == "res":
                    for t in range(T):
                        block_ready(dve, b, t)
                        cols = h[:, t, c * HALF:(c + 1) * HALF]
                        nc.vector.tensor_tensor(cols, ps[:, bank_of(b, t), :], cols, ALU.add).then_inc(evict_dve, 1)
                elif kind == "tail_f":
                    forget()
                elif kind == "router":
                    for t in range(T):
                        block_ready(dve, b, t)
                        nc.vector.tensor_scalar(r_in[:, t, 0:EXPERTS], ps[:, bank_of(b, t), 0:EXPERTS], rstd_of(b, t), None,
                                                ALU.mult).then_inc(evict_dve, 1)

            scores = Count(score_step)
            spans = ((slice(0, P), slice(0, P)), (slice(P, LOG), slice(2 * P, LOG)))

            def add_scores():
                for i in range(IDX_HEADS):
                    dve.wait_ge(relu_done, i + 1)
                    if i:
                        dve.wait_ge(score_step, scores.n)
                    for t, (cols, _) in enumerate(spans):
                        if i == 0:
                            scores.by(nc.vector.tensor_scalar(score[:, cols], relu[:, 0, cols], wi[:, t, 0:1], None, ALU.mult))
                        else:
                            scores.by(nc.vector.scalar_tensor_tensor(score[:, cols], relu[:, i % 2, cols], wi[:, t, i:i + 1],
                                                                     score[:, cols], ALU.mult, ALU.add))
                dve.wait_ge(score_step, scores.n)
                for t, (_, own) in enumerate(spans):
                    scores.by(nc.vector.tensor_tensor(score[:, own], score[:, own], chunk_mask, ALU.add))
                dve.wait_ge(score_step, scores.n)

            def choose_keys():
                for t, (cols, _) in enumerate(spans):
                    scores.by(nc.vector.max(top8[:, t, :], score[:, cols]))
                dve.wait_ge(score_step, scores.n)
                for t, (cols, _) in enumerate(spans):
                    scores.by(nc.vector.match_replace(score[:, cols], top8[:, t, :], score[:, cols], TAKEN))
                dve.wait_ge(score_step, scores.n)

            rounds = [0]

            def blocks(bs):
                for b in bs:
                    for u in units_of(b):
                        lo(u + AHEAD)
                        if b in range(4, 8):
                            choose_keys()
                            rounds[0] += 1
                    after_block(b)
                    if b == 3:
                        add_scores()

            def attention(k):
                for n in range(HEADS + 3):
                    if n < HEADS:
                        g = k * HEADS + n
                        dve.wait_ge(logits_done, g + 1)
                        if n >= 2:
                            dve.wait_ge(exp_done, 2 * (g - 1))
                        for t, cols in ((0, slice(0, P)), (1, slice(P, LOG))):
                            src, dst = ps[:, n % 2, cols], logit[:, n % 2, cols]
                            add = (masks if k == 0 else causal)[:, cols]
                            steps.by(nc.vector.tensor_tensor_reduce(dst, src, add, 1.0, TAKEN, ALU.add, ALU.max,
                                                                    row_max[:, 2 * n + t:2 * n + t + 1]))
                        dve.wait_ge(max_step, steps.n)
                        two = slice(2 * n, 2 * n + 2)
                        if k == 0:
                            nc.vector.tensor_scalar(neg_max[:, two], row_max[:, two], -1.0, None, ALU.mult).then_inc(masked, 1)
                        else:
                            steps.by(nc.vector.tensor_tensor(full_max[:, two], row_max[:, two], f_tok[:, :, n], ALU.add))
                            dve.wait_ge(max_step, steps.n)
                            nc.vector.tensor_tensor(neg_max[:, two], f_tok[:, :, n], full_max[:, two], ALU.subtract).then_inc(masked, 1)
                    if 2 <= n < HEADS + 2:
                        m = n - 2
                        g = k * HEADS + m
                        two = slice(2 * m, 2 * m + 2)
                        dve.wait_ge(exp_done, 2 * (g + 1))
                        nc.vector.reciprocal(row_inv[:, two], row_sum[:, two]).then_inc(inv_made, 1)
                        dve.wait_ge(inv_made, g + 1)
                        dve.wait_ge(pv_done, g + 1)
                        for t in range(T):
                            nc.vector.tensor_scalar(xhat[:, t, m * HD:(m + 1) * HD], ps[:, 6 + m % 2, t * HD:(t + 1) * HD],
                                                    row_inv[:, 2 * m + t:2 * m + t + 1], None, ALU.mult).then_inc(head_out, 1)
                    if spread_round(n) is not None:
                        spread((SPREAD_A, SPREAD_B)[k], [spread_round(n)])

            steps = Count(max_step)
            dve.wait_ge(small_landed, 32)
            spread(0)
            for u in range(AHEAD - 1):
                lo(u)
            norm(0)
            lo(AHEAD - 1)
            dve.wait_ge(consts_landed, 16)
            blocks(B_A)
            assert rounds[0] * 8 == TOPK
            nc.vector.tensor_scalar(masks[:, :], score[:, :], TAKEN / 2, NEG, ALU.is_gt, ALU.mult).then_inc(mask_made, 1)
            dve.wait_ge(mask_made, 1)
            attention(0)
            blocks(B_OUT_A)
            spread(2)
            norm(1)
            for b in range(FB + 1):
                if b < FB:
                    lo(DENSE_U + gate_up_unit(b, 0) + AHEAD)
                if b >= 1:
                    dve.wait_ge(hid_hi_made, b)
                    nc.vector.tensor_tensor(hid_lo[:, (b - 1) % 2, :, :],
                                            ps[:, 6 + (b - 1) % 2, :].rearrange("p (c n) -> p c n", c=2),
                                            hid_hi[:, (b - 1) % 2, :, :].bitcast(F32), ALU.subtract).then_inc(hid_lo_made, 1)
                if b < FB:
                    lo(DENSE_U + gate_up_unit(b, 1) + AHEAD)
                    for t in range(T):
                        dve.wait_ge(silu_done, T * b + t + 1)
                        if b >= 1 and t == 0:
                            dve.wait_ge(hid_turned, b)
                        nc.vector.scalar_tensor_tensor(hid[:, t, :], ps[:, 4 + t, 256:512], rstd[:, 2 + t:3 + t], silu[:, t, :],
                                                       ALU.mult, ALU.mult).then_inc(hid_done, 1)
                if b >= 1:
                    lo(DENSE_U + down_unit(b - 1) + AHEAD)
            dve.wait_ge(used, DENSE_U + FFN_UNITS)
            for c in range(2):
                for t in range(T):
                    cols = h[:, t, c * HALF:(c + 1) * HALF]
                    nc.vector.tensor_tensor(cols, ps[:, 2 * t + c, :], cols, ALU.add).then_inc(added, 1)
            spread(3)
            norm(2)
            blocks(B_KV)
            spread(4)
            forget_sum()
            blocks(B_Q)
            forget_out()
            dve.wait_ge(f_out, 2)
            attention(1)
            blocks(B_OUT_B)
            spread(6)
            norm(3)
            route = Count(route_step)

            def link(ins):
                route.by(ins)
                dve.wait_ge(route_step, route.n)

            nc.vector.memset(r_in[:, :, EXPERTS:14], TAKEN).then_inc(route_step, 1)
            nc.vector.memset(r_rep[:, :, :], TAKEN).then_inc(route_step, 1)
            route.n = 2
            blocks([B_ROUTER])
            dve.wait_ge(evict_dve, n_dve)
            dve.wait_ge(route_step, 2)
            for t in range(T):
                route.by(nc.vector.max(r_top[:, t, :], r_in[:, t, :]))
            dve.wait_ge(route_step, route.n)
            link(nc.vector.tensor_scalar(r_neg, r_top[:, :, 0], -1.0, None, ALU.mult))
            assert route.n == ROUTE_EXP
            link(nc.vector.tensor_copy(r_rep[:, :, 0:2], r_top[:, :, 0:2]))
            for t in range(T):
                route.by(nc.vector.match_replace(r_out[:, t, :], r_rep[:, t, :], r_in[:, t, :], -TAKEN))
            dve.wait_ge(route_step, route.n)
            link(nc.vector.tensor_scalar(chosen, r_out[:, :, 0:EXPERTS], -TAKEN / 2, None, ALU.is_gt))
            assert route.n == ROUTE_CHOSEN
            dve.wait_ge(route_exp, 2)
            link(nc.vector.tensor_tensor(gate, r_exp, chosen, ALU.mult))
            link(nc.vector.tensor_reduce(r_den, gate, AX_X, ALU.add))
            link(nc.vector.reciprocal(r_inv, r_den))
            for t in range(T):
                route.by(nc.vector.tensor_scalar(gate[:, t, :], gate[:, t, :], r_inv[:, t:t + 1], None, ALU.mult))
            dve.wait_ge(route_step, route.n)
            dve.wait_ge(route_cum, 1)
            link(nc.vector.tensor_copy(slot, ps[:, 6, 0:16].rearrange("p (t n) -> p t n", t=T)))
            link(nc.vector.tensor_reduce(r_most, ps[:, 6, 16:24], AX_X, ALU.max))
            link(nc.vector.tensor_scalar(flag[:, :], r_most, float(P), None, ALU.is_gt))
            assert route.n == ROUTE_STEPS

            def lo_moe(it, m):
                s = m % RING
                n = dve_part(UNIT)
                i = (PRE + m) % SPLIT
                dve.wait_ge(hi_made, it * 66 + (PRE + m + 1))
                nc.vector.tensor_tensor(w_lo[:, i, 0:n], raw_at(s, n), w_hi[:, i, 0:n].bitcast(F32),
                                        ALU.subtract).then_inc(lo_made_dve, 1)

            def column(table, t, it, e):
                e = e % EXPERTS
                if isinstance(it, int):
                    return table[:, t, e + 2 * it:e + 2 * it + 1]
                return table[:, t, bass.ds(it * 2 + e, 1)]

            def pick_tokens(it, e):
                dve.wait_ge(gathered, it * 2 + e)
                for t in range(T):
                    ins = nc.vector.tensor_scalar(pick[:, t, :], iota1, column(slot, t, it, e), column(chosen, t, it, e),
                                                  ALU.is_equal, ALU.mult)
                    ins.then_inc(pick_made, 1)

            def pick_gates(it, e):
                dve.wait_ge(block_turned, it * 2 + (TURNED + e))
                for t in range(T):
                    ins = nc.vector.tensor_scalar(pick_gate[:, t, :], iota1, column(slot, t, it, e), column(gate, t, it, e),
                                                  ALU.is_equal, ALU.mult)
                    ins.then_inc(gate_picked, 1)

            def tokens_out(it, e, buf):
                for c in range(KC):
                    dve.wait_ge(token_hi, it * (2 * KC) + (KC * e + 4 * (c // 4 + 1)))
                    nc.vector.scalar_tensor_tensor(x_lo[:, c, buf * P:(buf + 1) * P],
                                                   ps[:, 6 + c // 4, (c % 4) * P:(c % 4 + 1) * P],
                                                   gains[:, 4 * KC + c:4 * KC + c + 1],
                                                   x_hi[:, c, buf * P:(buf + 1) * P].bitcast(F32),
                                                   ALU.mult, ALU.subtract).then_inc(token_lo, 1)

            def hid_moe(it, n):
                dve.wait_ge(silu_done, it * (2 * FB) + (T * FB + n + 1))
                dve.wait_ge(hid_turned, it * (2 * FB) + (FB + n - 1))
                nc.vector.tensor_tensor(hid[:, n % 2, :], ps[:, 2 + n % 2, 256:512], silu[:, n % 2, :], ALU.mult).then_inc(hid_done, 1)

            def hid_lo_moe(it, n):
                dve.wait_ge(hid_hi_made, it * (2 * FB) + (FB + n + 1))
                nc.vector.tensor_tensor(hid_lo[:, n % 2, :, 0:P],
                                        ps[:, 4 + n % 2, 0:256].rearrange("p (c n) -> p c n", c=2),
                                        hid_hi[:, n % 2, :, 0:P].bitcast(F32), ALU.subtract).then_inc(hid_lo_made, 1)

            def split_behind(it, m, last):
                if not last or m + AHEAD < MOE_UNITS * (m // MOE_UNITS + 1):
                    lo_moe(it, m + AHEAD)

            def expert(it, e, last):
                for b in range(2, FB if last else FB + 2):
                    n = FB * e + b
                    hid_lo_moe(it, n - 1)
                    if b == FB + 1:
                        add_experts(it, e)
                    split_behind(it, expert_unit(n, "gate_up", 0), last)
                    if b == 4 and not last:
                        pick_tokens(it, e + 1)
                    if b == 5:
                        pick_gates(it, e)
                    if b == 7 and not last:
                        tokens_out(it, e + 1, (e + 1) % 2)
                    hid_moe(it, n)
                    split_behind(it, expert_unit(n, "gate_up", 1), last)
                    if b == FB:
                        y_out_of_psum(it, e)
                    split_behind(it, expert_unit(n - 1, "down"), last)
                if last:
                    hid_lo_moe(it, FB * e + FB - 1)
                    y_out_of_psum(it, e)
                    add_experts(it, e)

            def y_out_of_psum(it, e):
                moe_used(dve, it, expert_unit(FB * e + FB - 1, "down"))
                nc.vector.tensor_copy(y_out[:, HALF:D], ps[:, 1, :]).then_inc(evict_dve, 1)

            def add_experts(it, e):
                for q in range(4):
                    t, c = q // 2, q % 2
                    dve.wait_ge(scattered, it * 8 + (4 * e + q + 1))
                    cols = h[:, t, c * HALF:(c + 1) * HALF]
                    nc.vector.tensor_tensor(cols, ps[:, 6 + q % 2, :], cols, ALU.add).then_inc(added, 1)

            def experts(second):
                e0, n0, m0 = EXPERTS * second, EXPERTS * FB * second, MOE_UNITS * second
                if second:
                    dve.wait_ge(gate_picked, 2 * EXPERTS)
                    dve.wait_ge(pick_made, 2 * EXPERTS)
                    nc.vector.tensor_scalar(slot, slot, -float(P), None, ALU.add).then_inc(shifted, 1)
                    dve.wait_ge(shifted, 1)
                    for m in range(m0, m0 + AHEAD):
                        lo_moe(0, m)
                pick_tokens(0, e0)
                tokens_out(0, e0, 0)
                lo_moe(0, m0 + AHEAD)
                hid_moe(0, n0)
                lo_moe(0, m0 + AHEAD + 1)
                hid_lo_moe(0, n0)
                lo_moe(0, m0 + AHEAD + 2)
                hid_moe(0, n0 + 1)
                lo_moe(0, m0 + AHEAD + 3)
                lo_moe(0, m0 + AHEAD + 4)
                with dve.Fori(0, EXPERTS // 2 - 1) as it:
                    for p in range(2):
                        expert(it, e0 + p, False)
                expert(0, e0 + EXPERTS - 2, False)
                expert(0, e0 + EXPERTS - 1, True)

            experts(0)
            with dve.If(dve.value_load(flag[0:1, 0:1], min_val=0, max_val=1) > 0):
                experts(1)
            nc.vector.tensor_copy(top8[:, 0, 0:1], row_sum[:, 0:1]).then_inc(h_final, 1)
            norm(4)
            dve.wait_ge(gain_landed, 16)
            for t in range(T):
                nc.vector.scalar_tensor_tensor(xhat[:, t, :], h[:, t, :], rstd[:, 8 + t:9 + t], fin_gain,
                                               ALU.mult, ALU.mult).then_inc(out_made, 1)

        @block.gpsimd
        def _(pool):
            def lo_part(i, s, words):
                n = dve_part(words)
                nc.gpsimd.tensor_tensor(w_lo[:, i, n:words], raw[:, s * UNIT + n:s * UNIT + words],
                                        w_hi[:, i, n:words].bitcast(F32), ALU.subtract).then_inc(lo_made_pool, 1)

            def lo(u):
                pool.wait_ge(hi_made, u + 1)
                lo_part(u % SPLIT, raw_slot(u)[0], words_of(u))

            def rope(b):
                heads = 1 if BLOCKS[b][0] == "tail_a" else 8
                for t in range(T):
                    pool.wait_ge(evict_dve, evict_of(b, t)[1])
                    a, w = stage[:, t, 0:heads * HD], turned[:, t, 0:heads * HD]
                    if heads == 1:
                        nc.gpsimd.tensor_tensor(stage[:, t, HD:2 * HD], a, w, ALU.add).then_inc(index_key_copy, 1)
                        pool.wait_ge(index_key_copy, t + 1)
                    nc.gpsimd.tensor_tensor(a, a, w, ALU.add).then_inc(rope_done, 1)

            zeros = (kT[HD:P, 0, :, :], kT[0:HD, 1, :, :], kiT_low[HD:P, :], kiT_high[0:HD, :], neg_fT[:, :])
            for i, block_of_zeros in enumerate(zeros):
                if i:
                    pool.wait_ge(zeroed, i)
                nc.gpsimd.memset(block_of_zeros, 0.0).then_inc(zeroed, 1)
            assert len(zeros) == ZEROED
            for u in range(AHEAD):
                lo(u)
            for b in range(len(BLOCKS)):
                if b == B_KV[0]:
                    for u in range(DENSE_U, DENSE_U + FFN_UNITS):
                        lo(u + AHEAD)
                for u in units_of(b):
                    lo(u + AHEAD)
                if b in ROPING:
                    rope(b)

            def stream(first, last):
                with pool.Fori(first, last) as j:
                    for m in range(FFN_UNITS):
                        pool.wait_ge(hi_made, j * FFN_UNITS + (PRE + AHEAD + m + 1))
                        lo_part((PRE + AHEAD + m) % SPLIT, (AHEAD + m) % RING, UNIT)

            def tail(base):
                for m in range(base + MOE_UNITS - FFN_UNITS + AHEAD, base + MOE_UNITS):
                    lo(PRE + m)

            stream(0, EXPERTS - 1)
            tail(0)
            with pool.If(pool.value_load(flag[0:1, 0:1], min_val=0, max_val=1) > 0):
                for m in range(MOE_UNITS, MOE_UNITS + AHEAD):
                    lo(PRE + m)
                stream(EXPERTS, 2 * EXPERTS - 1)
                tail(MOE_UNITS)

        @block.tensor
        def _(pe):
            def mm3(dst, xh, xl, wh, wl, first, last):
                pe.matmul(dst, xh, wh, start=first, stop=False)
                pe.matmul(dst, xh, wl, start=False, stop=False)
                return pe.matmul(dst, xl, wh, start=False, stop=last)

            def split_of(u):
                pe.wait_ge(lo_made_dve, u + 1)
                pe.wait_ge(lo_made_pool, u + 1)
                return w_hi[:, u % SPLIT, :], w_lo[:, u % SPLIT, :]

            def spread(s, rounds=range(KC // 2)):
                src = xhat if s in (SPREAD_A, SPREAD_B) else h
                if s == 4:
                    pe.wait_ge(turned_out, turn_no(B_KV[1], T - 1))
                for j in rounds:
                    if s == 0 and j == 0:
                        pe.wait_ge(x_landed, 16)
                    elif s in (SPREAD_A, SPREAD_B):
                        pe.wait_ge(head_out, 2 * (HEADS * (s == SPREAD_B) + 4 * (j + 1)))
                        if j >= 2:
                            pe.wait_ge(spread_lo, KC * s + 2 * (j - 1))
                    elif s in (2, 6):
                        pe.wait_ge(*evict_of((B_OUT_A if s == 2 else B_OUT_B)[j // 2], T - 1))
                    elif s == 3:
                        pe.wait_ge(added, T * (j // 2 + 1))
                    for c in (2 * j, 2 * j + 1):
                        for t in range(T):
                            at_col = (c % 2) * SEQ + t * P
                            mm = pe.transpose(ps[:, spread_bank(s, j), at_col:at_col + P], src[:, t, c * P:(c + 1) * P], ident)
                    mm.then_inc(spread_turned, 1)

            def project(b, s=None):
                kind, _ = BLOCKS[b]
                width = WIDTH.get(kind, HALF)
                us = units_of(b)
                chunks = KC // len(us)
                for i, u in enumerate(us):
                    wh, wl = split_of(u)
                    if s is not None:
                        pe.wait_ge(spread_lo, KC * s + (i + 1) * chunks)
                    for t in range(T):
                        for k in range(chunks):
                            c = i * chunks + k
                            cols = slice(k * width, (k + 1) * width)
                            toks = slice(t * P, (t + 1) * P)
                            mm = mm3(ps[:, bank_of(b, t), 0:width], x_hi[:, c, toks], x_lo[:, c, toks],
                                     wh[:, cols], wl[:, cols], c == 0, c == KC - 1)
                        if i == len(us) - 1 and t == 0:
                            mm.then_inc(tile0_done, 1)
                    mm.then_inc(used, 1)

            def turn(b):
                for t in range(T):
                    if b in ROPING:
                        pe.wait_ge(rope_done, rope_no(b, t))
                    else:
                        pe.wait_ge(*evict_of(b, t))
                    before = TURNING.index(b) - 1
                    if before >= 0:
                        pe.wait_ge(turned_out, T * before + t + 1)
                    n = 1 if BLOCKS[b][0] == "tail_a" else 4
                    for i in range(n):
                        mm = pe.transpose(ps[:, 4 + t, i * P:(i + 1) * P], stage[:, t, i * P:(i + 1) * P], ident)
                    mm.then_inc(block_turned, 1)

            def blocks(bs, s):
                for b in bs:
                    if b - 2 in bs or b in B_Q:
                        for t in range(T):
                            pe.wait_ge(*evict_of(b - 2, t))
                    project(b, s if b == bs[0] else None)
                    if b - 1 in bs and b - 1 in TURNING:
                        turn(b - 1)
                    if b == 3:
                        index()
                if bs[-1] in TURNING:
                    turn(bs[-1])

            def index():
                pe.wait_ge(turned_out, turn_no(1, T - 1))
                pe.wait_ge(zeroed, ZEROED)
                for i in range(IDX_HEADS):
                    if i >= 2:
                        pe.wait_ge(relu_done, i - 1)
                    c, bank, key = i // 2, 6 + i % 2, (kiT_low, kiT_high)[i % 2]
                    pe.matmul(ps[:, bank, 0:P], qiT[:, c, 0:P], key[:, 0:P], start=True, stop=True)
                    pe.matmul(ps[:, bank, P:LOG], qiT[:, c, P:SEQ], key, start=True, stop=True).then_inc(index_done, 1)

            def attention(k):
                for n in range(HEADS + 3):
                    if n < HEADS:
                        g = k * HEADS + n
                        if n >= 2:
                            pe.wait_ge(masked, g - 1)
                        c = n // 2
                        for t, cols, keys in ((0, slice(0, P), P), (1, slice(P, LOG), SEQ)):
                            mm = pe.matmul(ps[:, n % 2, cols], qT[:, c, t * P:(t + 1) * P], kT[:, n % 2, c, 0:keys],
                                           start=True, stop=(k == 0))
                            if k == 1:
                                mm = pe.matmul(ps[:, n % 2, cols], ident[:, n:n + 1].to_broadcast([P, P]), neg_fT[:, 0:keys],
                                               start=False, stop=True)
                        mm.then_inc(logits_done, 1)
                    if 1 <= n <= HEADS:
                        m = n - 1
                        g = k * HEADS + m
                        pe.wait_ge(exp_done, 2 * (g + 1))
                        if m >= 2:
                            pe.wait_ge(probT_made, g - 1)
                        for i in range(3):
                            mm = pe.transpose(ps[:, 4 + m % 2, i * P:(i + 1) * P], prob[:, m % 2, i * P:(i + 1) * P], ident)
                        mm.then_inc(probs_turned, 1)
                    if 2 <= n < HEADS + 2:
                        m = n - 2
                        g = k * HEADS + m
                        pe.wait_ge(probT_made, g + 1)
                        if m >= 2:
                            pe.wait_ge(head_out, 2 * (g - 1))
                        cols = slice(m * HD, (m + 1) * HD)
                        bank = 6 + m % 2
                        pe.matmul(ps[:, bank, 0:HD], probT[:, m % 2, 0:P], val[:, 0, cols], start=True, stop=True)
                        pe.matmul(ps[:, bank, HD:2 * HD], probT[:, m % 2, P:2 * P], val[:, 0, cols], start=True, stop=False)
                        pe.matmul(ps[:, bank, HD:2 * HD], probT[:, m % 2, 2 * P:LOG], val[:, 1, cols],
                                  start=False, stop=True).then_inc(pv_done, 1)
                    if spread_round(n) is not None:
                        spread((SPREAD_A, SPREAD_B)[k], [spread_round(n)])

            def forget():
                pe.wait_ge(f_step, 3)
                l0, l1 = lf[:, 0:HEADS], lf[:, HEADS:2 * HEADS]
                pe.matmul(ps[:, 6, 0:HEADS], upper, l0, start=True, stop=True)
                pe.matmul(ps[:, 6, HEADS:2 * HEADS], ones, l0, start=True, stop=False)
                pe.matmul(ps[:, 6, HEADS:2 * HEADS], upper, l1, start=False, stop=True)
                pe.matmul(ps[0:HEADS, 7, 0:P], l0, upper, start=True, stop=True)
                pe.matmul(ps[0:HEADS, 7, P:SEQ], l0, ones, start=True, stop=False)
                pe.matmul(ps[0:HEADS, 7, P:SEQ], l1, upper, start=False, stop=True).then_inc(f_cum, 1)

            pe.wait_ge(ident_landed, 16)
            spread(0)
            blocks(B_A, 0)
            pe.wait_ge(mask_made, 1)
            pe.wait_ge(*evict_of(7, T - 1))
            pe.wait_ge(turned_out, turn_no(5, T - 1))
            attention(0)
            blocks(B_OUT_A, SPREAD_A)
            spread(2)
            for b in range(FB + 1):
                for i in range(2):
                    if b < FB:
                        wh, wl = split_of(DENSE_U + gate_up_unit(b, i))
                        if b == 0:
                            pe.wait_ge(spread_lo, KC * 2 + 4 * (i + 1))
                        for t in range(T):
                            if b >= 1 and i == 0:
                                pe.wait_ge(hid_done, T * (b - 1) + t + 1)
                            toks = slice(t * P, (t + 1) * P)
                            for k in range(4):
                                c = 4 * i + k
                                mm = mm3(ps[:, 4 + t, :], x_hi[:, c, toks], x_lo[:, c, toks],
                                         wh[:, k * HALF:(k + 1) * HALF], wl[:, k * HALF:(k + 1) * HALF], c == 0, c == KC - 1)
                            if i == 1 and t == 0:
                                mm.then_inc(gu_tile0, 1)
                        mm.then_inc(used, 1)
                    if b >= 1 and i == 0:
                        n = b - 1
                        pe.wait_ge(hid_done, T * (n + 1))
                        if n >= 2:
                            pe.wait_ge(hid_lo_made, n - 1)
                        for c in range(2):
                            for t in range(T):
                                at_col = c * SEQ + t * P
                                mm = pe.transpose(ps[:, 6 + n % 2, at_col:at_col + P], hid[:, t, c * P:(c + 1) * P], ident)
                        mm.then_inc(hid_turned, 1)
                if b >= 1:
                    n = b - 1
                    pe.wait_ge(hid_lo_made, n + 1)
                    wh, wl = split_of(DENSE_U + down_unit(n))
                    for t in range(T):
                        toks = slice(t * P, (t + 1) * P)
                        for c in range(2):
                            for k in range(2):
                                cols = slice(k * D + c * HALF, k * D + (c + 1) * HALF)
                                mm = mm3(ps[:, 2 * t + c, :], hid_hi[:, n % 2, k, toks], hid_lo[:, n % 2, k, toks],
                                         wh[:, cols], wl[:, cols], n == 0 and k == 0, n == FB - 1 and k == 1)
                    mm.then_inc(used, 1)
            spread(3)
            blocks(B_KV, 3)
            spread(4)
            blocks(B_Q, 4)
            pe.wait_ge(consts_landed, 16)
            forget()
            pe.wait_ge(turned_out, turn_no(B_Q[-1], T - 1))
            pe.wait_ge(*evict_of(B_KV[3], T - 1))
            pe.wait_ge(f_out, 2)
            attention(1)
            blocks(B_OUT_B, SPREAD_B)
            spread(6)
            blocks([B_ROUTER], 6)
            pe.wait_ge(route_step, ROUTE_CHOSEN)
            pe.matmul(ps[:, 6, 0:8], upper, chosen[:, 0, :], start=True, stop=True)
            pe.matmul(ps[:, 6, 8:16], ones, chosen[:, 0, :], start=True, stop=False)
            pe.matmul(ps[:, 6, 8:16], upper, chosen[:, 1, :], start=False, stop=True)
            pe.matmul(ps[:, 6, 16:24], ones, chosen[:, 0, :], start=True, stop=False)
            pe.matmul(ps[:, 6, 16:24], ones, chosen[:, 1, :], start=False, stop=True).then_inc(route_cum, 1)

            pe.wait_ge(xhat_made, T)

            def split_of_moe(it, m):
                pe.wait_ge(lo_made_dve, it * (2 * FFN_UNITS) + (PRE + m + 1))
                pe.wait_ge(lo_made_pool, it * (2 * FFN_UNITS) + (PRE + m + 1))
                i = (PRE + m) % SPLIT
                return w_hi[:, i, :], w_lo[:, i, :]

            def gather(it, e):
                pe.wait_ge(pick_made, it * 4 + 2 * (e + 1))
                if e >= 1:
                    pe.wait_ge(added, it * 8 + 4 * e)
                for c in range(KC):
                    for t in range(T):
                        mm = pe.matmul(ps[:, 6 + c // 4, (c % 4) * P:(c % 4 + 1) * P], xhat[:, t, c * P:(c + 1) * P],
                                       pick[:, t, :], start=(t == 0), stop=(t == T - 1))
                mm.then_inc(gathered, 1)

            def gate_up(it, n, i):
                if i == 0:
                    pe.wait_ge(hid_done, it * (2 * FB) + (T * FB + n - 1))
                wh, wl = split_of_moe(it, expert_unit(n, "gate_up", i))
                buf = n // FB % 2
                toks = slice(buf * P, (buf + 1) * P)
                for k in range(4):
                    c = 4 * i + k
                    mm = mm3(ps[:, 2 + n % 2, :], x_hi[:, c, toks], x_lo[:, c, toks],
                             wh[:, k * HALF:(k + 1) * HALF], wl[:, k * HALF:(k + 1) * HALF], c == 0, c == KC - 1)
                mm.then_inc(used, 1)

            def turn_hid(it, n):
                pe.wait_ge(hid_done, it * (2 * FB) + (T * FB + n + 1))
                pe.wait_ge(hid_lo_made, it * (2 * FB) + (FB + n - 1))
                if n % FB == 8:
                    pe.wait_ge(turned_out, it * 2 + (TURNED + n // FB + 1))
                for c in range(2):
                    mm = pe.transpose(ps[:, 4 + n % 2, c * P:(c + 1) * P], hid[:, n % 2, c * P:(c + 1) * P], ident)
                mm.then_inc(hid_turned, 1)

            def down(it, n):
                pe.wait_ge(hid_lo_made, it * (2 * FB) + (FB + n + 1))
                b = n % FB
                if b == 0:
                    pe.wait_ge(evict_act, it * 2 + (n_act + n // FB))
                    pe.wait_ge(evict_dve, it * 2 + (n_dve + n // FB))
                wh, wl = split_of_moe(it, expert_unit(n, "down"))
                for c in range(2):
                    for k in range(2):
                        cols = slice(k * D + c * HALF, k * D + (c + 1) * HALF)
                        mm = mm3(ps[:, c, :], hid_hi[:, n % 2, k, 0:P], hid_lo[:, n % 2, k, 0:P],
                                 wh[:, cols], wl[:, cols], b == 0 and k == 0, b == FB - 1 and k == 1)
                mm.then_inc(used, 1)

            def turn_gates(it, e):
                pe.wait_ge(gate_picked, it * 4 + 2 * (e + 1))
                pe.wait_ge(hid_lo_made, it * (2 * FB) + (FB + FB * e + 7))
                for t in range(T):
                    mm = pe.transpose(ps[:, 4 + (FB * e + 8) % 2, t * P:(t + 1) * P], pick_gate[:, t, :], ident)
                mm.then_inc(block_turned, 1)

            def scatter(it, e, last):
                pe.wait_ge(evict_act, it * 2 + (n_act + e + 1))
                pe.wait_ge(evict_dve, it * 2 + (n_dve + e + 1))
                pe.wait_ge(turned_out, it * 2 + (TURNED + e + 1))
                pe.wait_ge(token_lo, it * (2 * KC) + KC * (e + (1 if last else 2)))
                for q in range(4):
                    t, c = q // 2, q % 2
                    if q >= 2:
                        pe.wait_ge(added, it * 8 + (4 + 4 * e + q - 1))
                    pe.matmul(ps[:, 6 + q % 2, :], gateT[:, t * P:(t + 1) * P], y_out[:, c * HALF:(c + 1) * HALF],
                              start=True, stop=True).then_inc(scattered, 1)

            def expert(it, e, last):
                for b in range(2, FB if last else FB + 2):
                    n = FB * e + b
                    if b == FB:
                        pe.wait_ge(token_lo, it * (2 * KC) + KC * (e + 2))
                    gate_up(it, n, 0)
                    turn_hid(it, n - 1)
                    if b == 8:
                        turn_gates(it, e)
                    if b == FB + 1:
                        scatter(it, e, last)
                    gate_up(it, n, 1)
                    down(it, n - 1)
                    if b == 6 and not last:
                        gather(it, e + 1)
                if last:
                    turn_hid(it, FB * e + FB - 1)
                    down(it, FB * e + FB - 1)
                    scatter(it, e, last)

            def experts(second):
                e0, n0 = EXPERTS * second, EXPERTS * FB * second
                gather(0, e0)
                pe.wait_ge(token_lo, KC * (e0 + 1))
                gate_up(0, n0, 0)
                gate_up(0, n0, 1)
                gate_up(0, n0 + 1, 0)
                turn_hid(0, n0)
                gate_up(0, n0 + 1, 1)
                down(0, n0)
                with pe.Fori(0, EXPERTS // 2 - 1) as it:
                    for p in range(2):
                        expert(it, e0 + p, False)
                expert(0, e0 + EXPERTS - 2, False)
                expert(0, e0 + EXPERTS - 1, True)

            experts(0)
            with pe.If(pe.value_load(flag[0:1, 0:1], min_val=0, max_val=1) > 0):
                experts(1)


def constants():
    row, col = np.arange(P)[:, None], np.arange(P)[None, :]
    upper = (row <= col).astype(np.float32)
    chunks = np.where(col // CHUNK <= row // CHUNK, 0.0, NEG)
    own = np.where(col <= row, 0.0, NEG)
    causal = np.concatenate([own, np.zeros((P, P)), own], 1)
    pos = np.arange(SEQ, dtype=np.float32)
    inv_freq = (np.float32(1.0) / (np.float32(10000.0) ** (np.arange(0, HD, 2, dtype=np.float32) / np.float32(HD)))).astype(np.float32)
    ang = pos[:, None] * inv_freq[None, :]
    cos, sin = np.cos(ang), np.sin(ang)
    by_tile = lambda a: a.reshape(T, P, HD).transpose(1, 0, 2).reshape(P, T * HD)
    return np.concatenate([np.eye(P), upper, np.ones((P, P)), np.broadcast_to(col + 1.0, (P, P)), chunks, causal,
                           by_tile(np.concatenate([cos, cos], 1)), by_tile(np.concatenate([-sin, sin], 1))],
                          1).astype(np.float32)


def kernel(x, a_norm, a_w_in, a_w_out, kv_norm, w_kv, b_f, b_norm, b_w_q, b_w_out, ffn_norm, dense_w_gate_up,
           dense_w_down, moe_router, moe_w_gate_up, moe_w_down, final_norm):
    from concourse import bacc
    from concourse.bass_utils import run_bass_kernel_spmd

    def block_units(w, c):
        part = np.asarray(w)[:, c * HALF:(c + 1) * HALF]
        return list(part.reshape(2, 4, P, HALF).transpose(0, 2, 1, 3).reshape(2, P, UNIT))

    def tail_unit(w):
        n = w.shape[1]
        unit = np.zeros((P, UNIT), w.dtype)
        unit[:, 0:KC * n] = np.asarray(w).reshape(KC, P, n).transpose(1, 0, 2).reshape(P, KC * n)
        return [unit]

    def ffn_units(gate_up, down, to, first, blocks):
        gu = gate_up.reshape(2, 4, P, 2, FB, 256).transpose(4, 0, 2, 1, 3, 5).reshape(FB, 2, P, UNIT)
        dn = down.reshape(FB, 2, P, D).transpose(0, 2, 1, 3).reshape(FB, P, UNIT)
        for b in range(FB):
            n = first + b
            to[gate_up_unit(n, 0)], to[gate_up_unit(n, 1)], to[down_unit(n, blocks)] = gu[b, 0], gu[b, 1], dn[b]

    w_in, w_kv = np.asarray(a_w_in)[0], np.asarray(w_kv)
    hd = HEADS * HD
    q, k, v, qi = 0, hd // HALF, 2 * hd // HALF, 3 * hd // HALF
    units = block_units(w_in, qi) + tail_unit(w_in[:, 3 * hd + HALF:])
    for c in (q, q + 1, k, k + 1, v, v + 1):
        units += block_units(w_in, c)
    for c in range(2):
        units += block_units(a_w_out[0], c)
    dense = np.empty((FFN_UNITS, P, UNIT), np.float32)
    ffn_units(np.asarray(dense_w_gate_up)[0], np.asarray(dense_w_down)[0], dense, 0, FB)
    units += list(dense)
    for c in range(4):
        units += block_units(w_kv, c)
    units += tail_unit(w_kv[:, 2 * hd:])
    for w in (b_w_q, b_w_out):
        for c in range(2):
            units += block_units(w[0], c)
    units += tail_unit(np.asarray(moe_router)[0])
    pre = np.stack(units)
    assert len(pre) == PRE
    moe = np.empty((MOE_UNITS, P, UNIT), np.float32)
    for e in range(EXPERTS):
        ffn_units(np.asarray(moe_w_gate_up)[0, e], np.asarray(moe_w_down)[0, e], moe, FB * e, FB * EXPERTS)
    gain_rows = [a_norm[0], ffn_norm[0], kv_norm, b_norm[0], ffn_norm[1]]
    arrays = {
        "x": np.asarray(x), "pre_stream": pre, "moe_stream": moe,
        "gain_cols": np.ascontiguousarray(np.stack([np.asarray(g) for g in gain_rows]).reshape(5 * KC, P).T),
        "final_norm": np.asarray(final_norm), "b_f": np.asarray(b_f), "consts": constants(),
    }
    nc = bacc.Bacc("TRN2", target_bir_lowering=False, num_devices=1)
    aps = {n: nc.dram_tensor(n, a.shape, F32, kind="ExternalInput").ap() for n, a in arrays.items()}
    out = nc.dram_tensor("out", (1, SEQ, D), F32, kind="ExternalOutput").ap()
    trunk(nc, out=out, **aps)
    return run_bass_kernel_spmd(nc, [arrays], core_ids=[0]).results[0]["out"]
```

```python
from contextlib import ExitStack

import numpy as np

import concourse.bass as bass
from concourse import mybir

F32 = mybir.dt.float32
F32R = mybir.dt.float32r
I32 = mybir.dt.int32
ALU = mybir.AluOpType
ACT = mybir.ActivationFunctionType
AX_X = mybir.AxisListType.X

P = 128
SEQ = 256
D = 1024
HEADS = 16
HD = 64
IDX_HEADS = 8
F = 2816
EXPERTS = 8
CHUNK = 64
TOPK = 64
EPS = 1e-6
T = SEQ // P
KC = D // P
FB = F // 256
HALF = 512
UNIT = 4 * HALF
A_TAIL = HD + IDX_HEADS
LOG = P + SEQ

BLOCKS = [
    ("tail_a", 0), ("rope_index", 0), ("rope_q", 0), ("rope_q", 1), ("rope_k", 0), ("rope_k", 1), ("v", 0), ("v", 1),
    ("res", 0), ("res", 1),
    ("copy_q", 0), ("copy_q", 1),
    ("copy_k", 0), ("copy_k", 1), ("tail_f", 0), ("v", 0), ("v", 1),
    ("res", 0), ("res", 1),
    ("router", 0),
]
WIDTH = {"tail_a": A_TAIL, "tail_f": HEADS, "router": EXPERTS}
B_A, B_OUT_A, B_Q, B_KV, B_OUT_B, B_ROUTER = range(0, 8), range(8, 10), range(10, 12), range(12, 17), range(17, 19), 19
B_FORGET = B_KV[2]
SPREAD_BEHIND = {B_OUT_A[-1]: 2, B_Q[-1]: 4, B_OUT_B[-1]: 6}
NORM_BEHIND = {B_OUT_A[-1]: 1, B_OUT_B[-1]: 3}
BEFORE_ATTENTION = (B_A[-1], B_KV[-1])
BEFORE_ROUTING = (B_OUT_B[-1], B_ROUTER)
SPREAD_A, SPREAD_B = 1, 5
FFN_UNITS = 3 * FB


def first_unit(b):
    before = sum(1 if BLOCKS[i][0] in WIDTH else 2 for i in range(b))
    return before + (FFN_UNITS if b >= B_Q[0] else 0)


DENSE_U = first_unit(9) + 2
PRE = first_unit(B_ROUTER) + 1
MOE_UNITS = EXPERTS * FFN_UNITS
RING_PRE = 6
RING = 11
SPLIT = 3
TURN_LAG, PV_LAG, OUT_LAG, SPREAD_LAG = 1, 2, 2, 4
STEPS = HEADS + SPREAD_LAG
AHEAD = 3
ROUTE_EXP, ROUTE_CHOSEN, ROUTE_STEPS = 5, 9, 17
ZEROED = 4

PICKS_TURN = 3

NEG = -1e30
TAKEN = -3e38


def unit_words(u):
    for b, (kind, _) in enumerate(BLOCKS):
        if kind in WIDTH and first_unit(b) == u:
            return KC * WIDTH[kind]
    return UNIT


def gate_up_unit(b, half):
    return 3 * b - (1 if b else 0) + half


def down_unit(b, blocks=FB):
    return 3 * b + (4 if b < blocks - 1 else 2)


def expert_unit(n, what, half=0):
    second, n = divmod(n, EXPERTS * FB)
    at = gate_up_unit(n, half) if what == "gate_up" else down_unit(n, EXPERTS * FB)
    return second * MOE_UNITS + at


def dve_part(words):
    return (words * 22 // 32) // 8 * 8


class Count:

    def __init__(self, sem, n=0):
        self.sem, self.n = sem, n

    def by(self, instruction, k=1):
        instruction.then_inc(self.sem, k)
        self.n = self.n + k
        return self.n


def trunk(nc, x, pre_stream, moe_stream, gain_cols, final_norm, b_f, consts, out):
    with ExitStack() as ctx:
        def sb(name, shape, dt=F32):
            return ctx.enter_context(nc.sbuf_tensor(name, shape, dt))

        def sem(name):
            return ctx.enter_context(nc.semaphore(name))

        raw = sb("raw", [P, RING * UNIT])
        w_hi = sb("w_hi", [P, SPLIT, UNIT], F32R)
        w_lo = sb("w_lo", [P, SPLIT, UNIT], F32R)
        x_hi = sb("x_hi", [P, KC, SEQ], F32R)
        x_lo = sb("x_lo", [P, KC, SEQ], F32R)
        hid_hi = sb("hid_hi", [P, 2, 2, SEQ], F32R)
        hid_lo = sb("hid_lo", [P, 2, 2, SEQ], F32R)
        y_hi = sb("y_hi", [P, D], F32R)
        y_lo = sb("y_lo", [P, D], F32R)
        pickT = sb("pickT", [P, SEQ], F32R)
        h = sb("h", [P, T, D])
        xhat = sb("xhat", [P, T, D])
        scratch = sb("scratch", [P, 2304])
        cst = sb("cst", [P, 5 * P + LOG + 4 * HD])
        score = sb("score", [P, LOG])
        masks = sb("masks", [P, LOG])
        gains = sb("gains", [P, 5 * KC])
        bf_rows = sb("bf_rows", [P, HEADS])
        small = sb("small", [P, 480])
        flag = sb("flag", [P, 1], I32)
        ps = ctx.enter_context(nc.psum_tensor("ps", [P, 8, HALF], F32))

        region = raw[:, RING_PRE * UNIT:RING * UNIT]
        qT = region[:, 0:2048].rearrange("p (c t) -> p c t", c=KC)
        kT = region[:, 2048:6144].rearrange("p (o c t) -> p o c t", o=2, c=KC)
        val = region[:, 6144:8192].rearrange("p (t d) -> p t d", t=T)
        qT_high = region[:, 8192:10240].rearrange("p (c t) -> p c t", c=KC)
        qiT = region[:, 8192:9216].rearrange("p (c t) -> p c t", c=IDX_HEADS // 2)
        relu = region[:, 9216:9216 + 2 * LOG].rearrange("p (b n) -> p b n", b=2)
        kiT_low = region[:, 9984:10240]
        kiT_high = scratch[:, 2048:2304]
        stage = scratch[:, 0:1024].rearrange("p (t n) -> p t n", t=T)
        turned = scratch[:, 1024:2048].rearrange("p (t n) -> p t n", t=T)
        logit = scratch[:, 0:2 * LOG].rearrange("p (b n) -> p b n", b=2)
        prob = scratch[:, 2 * LOG:4 * LOG].rearrange("p (b n) -> p b n", b=2)
        probT = scratch[:, 4 * LOG:6 * LOG].rearrange("p (b n) -> p b n", b=2)
        silu = scratch[:, 0:512].rearrange("p (b n) -> p b n", b=2)
        hid = scratch[:, 512:1024].rearrange("p (b n) -> p b n", b=2)
        pick = score[:, 0:256].rearrange("p (t s) -> p t s", t=T)
        ident = cst[:, 0:P]
        upper = cst[:, P:2 * P]
        ones = cst[:, 2 * P:3 * P]
        iota1 = cst[:, 3 * P:4 * P]
        chunk_mask = cst[:, 4 * P:5 * P]
        causal = cst[:, 5 * P:5 * P + LOG]
        cos = cst[:, 5 * P + LOG:5 * P + LOG + 2 * HD].rearrange("p (t n) -> p t n", t=T)
        sin = cst[:, 5 * P + LOG + 2 * HD:5 * P + LOG + 4 * HD].rearrange("p (t n) -> p t n", t=T)
        by_column = sb("by_column", [P, 2 * SEQ])
        tailT = by_column[:, 0:SEQ]
        neg_fT = by_column[0:HEADS // 2, :].rearrange("p (o t) -> p o t", o=2)
        at = [0]

        def part(n):
            at[0] += n
            assert at[0] <= 480
            return small[:, at[0] - n:at[0]]

        ssq, ms, std, rstd = part(10), part(10), part(10), part(10)
        wi = part(16).rearrange("p (t n) -> p t n", t=T)
        top8 = part(16).rearrange("p (t n) -> p t n", t=T)
        row_max, neg_max, row_sum, row_inv, full_max = part(32), part(32), part(32), part(32), part(32)
        fz = part(32).rearrange("p (t n) -> p t n", t=T)
        fa, fe, fl, lf = part(32), part(32), part(32), part(32)
        f_tok = part(32).rearrange("p (t n) -> p t n", t=T)
        unused = part(7)
        r_in = row_max[:, 0:28].rearrange("p (t n) -> p t n", t=T)
        r_out = neg_max[:, 0:28].rearrange("p (t n) -> p t n", t=T)
        r_top = row_sum[:, 0:16].rearrange("p (t n) -> p t n", t=T)
        r_rep = row_inv[:, 0:16].rearrange("p (t n) -> p t n", t=T)
        chosen = full_max[:, 0:16].rearrange("p (t n) -> p t n", t=T)
        r_exp = fa[:, 0:16].rearrange("p (t n) -> p t n", t=T)
        gate = fe[:, 0:16].rearrange("p (t n) -> p t n", t=T)
        slot = fl[:, 0:16].rearrange("p (t n) -> p t n", t=T)
        r_den, r_inv, r_neg = lf[:, 0:2], lf[:, 2:4], lf[:, 4:6]
        r_most = lf[:, 6:7]
        slot_gate = lf[:, 7:8]
        expert_gate = lf[:, 8:10]
        fin_gain = raw[:, 0:D]

        x_landed, ident_landed, consts_landed, small_landed = (sem(n) for n in (
            "x_landed", "ident_landed", "consts_landed", "small_landed"))
        zeroed = sem("zeroed")
        landed = [sem(f"landed{s}") for s in range(RING)]
        hi_made, lo_made_dve, lo_made_pool, used = sem("hi_made"), sem("lo_made_dve"), sem("lo_made_pool"), sem("used")
        squares, mean_made, std_made, rstd_made, xhat_made = (sem(n) for n in ("squares", "mean_made", "std_made", "rstd_made", "xhat_made"))
        spread_turned, spread_hi, spread_lo = sem("spread_turned"), sem("spread_hi"), sem("spread_lo")
        tail_product, tail_copied = sem("tail_product"), sem("tail_copied")
        tile0_done, evict_dve, evict_act = sem("tile0_done"), sem("evict_dve"), sem("evict_act")
        rope_cos, rope_done, block_turned, turned_out = sem("rope_cos"), sem("rope_done"), sem("block_turned"), sem("turned_out")
        index_key_copy = sem("index_key_copy")
        index_done, relu_done, score_step = sem("index_done"), sem("relu_done"), sem("score_step")
        mask_made = sem("mask_made")
        logits_done, masked, exp_done, probs_turned, probT_made = (sem(n) for n in ("logits_done", "masked", "exp_done", "probs_turned", "probT_made"))
        pv_done, inv_made, head_out = sem("pv_done"), sem("inv_made"), sem("head_out")
        max_step = sem("max_step")
        f_step, f_exp, f_ln, f_cum, f_out, f_landed, ones_made = (sem(n) for n in (
            "f_step", "f_exp", "f_ln", "f_cum", "f_out", "f_landed", "ones_made"))
        gu_tile0, silu_done, hid_done, hid_turned, hid_hi_made, hid_lo_made = (sem(n) for n in (
            "gu_tile0", "silu_done", "hid_done", "hid_turned", "hid_hi_made", "hid_lo_made"))
        down_half, added = sem("down_half"), sem("added")
        route_step, route_exp, route_cum = sem("route_step"), sem("route_exp"), sem("route_cum")
        pick_made, gathered, token_hi, token_lo = sem("pick_made"), sem("gathered"), sem("token_hi"), sem("token_lo")
        scattered = sem("scattered")
        shifted = sem("shifted")
        h_final, gain_landed, out_made, stored = sem("h_final"), sem("gain_landed"), sem("out_made"), sem("stored")

        def raw_slot(u):
            if u < PRE:
                return u % RING_PRE, u // RING_PRE + 1
            m = u - PRE
            s = m % RING
            return s, (sum(1 for v in range(PRE) if v % RING_PRE == s)) + m // RING + 1

        def raw_at(s, words):
            return raw[:, s * UNIT:s * UNIT + words]

        def words_of(u):
            return unit_words(u) if u < PRE else UNIT

        SPREAD = [0, None, 1, 3, 2, None, 4]
        block_evict = []
        n_dve = n_act = 0
        for kind, _ in BLOCKS:
            for t in range(T):
                if kind in ("v", "copy_k", "copy_q"):
                    n_act += 1
                    block_evict.append((evict_act, n_act))
                else:
                    n_dve += 1
                    block_evict.append((evict_dve, n_dve))
        TURNING = [b for b, (kind, _) in enumerate(BLOCKS) if kind.startswith(("rope", "copy", "tail_a"))]
        ROPING = [b for b, (kind, _) in enumerate(BLOCKS) if kind.startswith(("rope", "tail_a"))]

        TURNED = T * len(TURNING)

        def norm_of(b):
            return None if BLOCKS[b][0] == "res" else 0 if b in B_A else 2 if b < B_ROUTER else 3

        def rstd_of(b, t):
            return rstd[:, 2 * norm_of(b) + t:2 * norm_of(b) + t + 1]

        def spread_bank(s, j):
            return 2 + j % 2 if s in (SPREAD_A, SPREAD_B) else 6 + j % 2 if s == 4 else 4 + j % 2 if s == 2 else 4 + j

        def spread_round(n):
            first = 1 + SPREAD_LAG
            return (n - first) // 2 if n >= first and (n - first) % 2 == 0 else None

        def round_chunks(s):
            return 1 if s in (SPREAD_A, SPREAD_B) else 2

        def round_no(s, j):
            return sum(KC // round_chunks(i) for i in range(s)) + j + 1

        def chunks_of(s, j):
            return range(j * round_chunks(s), (j + 1) * round_chunks(s))

        def turn_no(b, t):
            return T * TURNING.index(b) + t + 1

        def rope_no(b, t):
            return T * ROPING.index(b) + t + 1

        def evict_of(b, t):
            return block_evict[T * b + t]

        def bank_of(b, t):
            return ((b + (b >= B_Q[0])) % 2) * 2 + t

        TAILS = [b for b, (kind, _) in enumerate(BLOCKS) if kind in WIDTH]

        def gate_bank(b, t):
            return (6 if b == 0 else 4) + t

        def block_ready(eng, b, t):
            if t == 0:
                eng.wait_ge(tile0_done, b + 1)
            else:
                eng.wait_ge(used, units_of(b)[-1] + 1)

        def moe_used(eng, it, m):
            eng.wait_ge(used, it * (2 * FFN_UNITS) + (PRE + m + 1))

        def units_of(b):
            n = 1 if BLOCKS[b][0] in WIDTH else 2
            return range(first_unit(b), first_unit(b) + n)

        block = ctx.enter_context(nc.Block())

        @block.sync
        def _(sp):
            sp.dma_start(ident, consts[:, 0:P]).then_inc(ident_landed, 16)
            sp.dma_start(h[:, :, :], x[0].rearrange("(t p) d -> p t d", p=P)).then_inc(x_landed, 16)

            def load(u):
                words = words_of(u)
                s, _ = raw_slot(u)
                src = pre_stream[u, :, 0:words] if u < PRE else moe_stream[u - PRE, :, :]
                sp.dma_start(raw_at(s, words), src).then_inc(landed[s], 16)

            def split_done(n):
                sp.wait_ge(lo_made_dve, n)
                sp.wait_ge(lo_made_pool, n)

            sp.dma_start(gains[:, :], gain_cols).then_inc(small_landed, 16)
            sp.dma_start(bf_rows[:, :], b_f.partition_broadcast(P)).then_inc(small_landed, 16)
            for u in range(RING_PRE):
                if u == 2:
                    sp.dma_start(cst[:, P:], consts[:, P:]).then_inc(consts_landed, 16)
                load(u)
            for u in range(RING_PRE, PRE):
                split_done(u - RING_PRE + 1)
                load(u)
            for m in range(RING):
                if m < RING_PRE:
                    split_done(max(v for v in range(PRE) if v % RING_PRE == m) + 1)
                elif m == RING_PRE:
                    sp.wait_ge(pv_done, 2 * HEADS)
                load(PRE + m)

            def stream(first, last, back):
                with sp.Fori(first, last) as j:
                    for s in range(RING):
                        split_done(j * RING + (PRE - RING + s + 1))
                        sp.dma_start(raw_at(s, UNIT), moe_stream[j * RING + (s - back)]).then_inc(landed[s], 16)

            stream(1, MOE_UNITS // RING, 0)
            sp.wait_ge(route_step, ROUTE_STEPS)
            with sp.If(sp.value_load(flag[0:1, 0:1], min_val=0, max_val=1) > 0):
                stream(MOE_UNITS // RING, 2 * MOE_UNITS // RING, MOE_UNITS)
            sp.wait_ge(h_final, 1)
            sp.dma_start(fin_gain, final_norm.partition_broadcast(P)).then_inc(gain_landed, 16)
            for t in range(T):
                sp.wait_ge(out_made, t + 1)
                sp.dma_start(out[0, t * P:(t + 1) * P, :], xhat[:, t, :]).then_inc(stored, 16)
            sp.wait_ge(stored, 16 * T)

        @block.scalar
        def _(act):
            def hi(u):
                s, n = raw_slot(u)
                words = words_of(u)
                act.wait_ge(landed[s], 16 * n)
                if u >= SPLIT:
                    act.wait_ge(used, u - (SPLIT - 1))
                nc.scalar.activation(w_hi[:, u % SPLIT, 0:words], raw_at(s, words), ACT.Copy).then_inc(hi_made, 1)

            fetched = [0]

            def fetch_table(function):
                nc.scalar.activation(unused[:, fetched[0]:fetched[0] + 1], ident[:, 0:1], function)
                fetched[0] += 1

            def norm(n):
                for t in range(T):
                    nc.scalar.activation(xhat[:, t, :], h[:, t, :], ACT.Square,
                                         accum_out=ssq[:, 2 * n + t:2 * n + t + 1]).then_inc(squares, 1)
                act.wait_ge(mean_made, n + 1)
                c = 2 * n
                nc.scalar.activation(std[:, c:c + 2], ms[:, c:c + 2], ACT.Sqrt).then_inc(std_made, 1)

            def spread(s, rounds=range(KC // 2)):
                for j in rounds:
                    act.wait_ge(spread_turned, round_no(s, j))
                    if s == 0 and j == 0:
                        act.wait_ge(small_landed, 32)
                    for c in chunks_of(s, j):
                        src = ps[:, spread_bank(s, j), (c % 2) * SEQ:(c % 2 + 1) * SEQ]
                        g = SPREAD[s]
                        scale = 1.0 if g is None else gains[:, g * KC + c:g * KC + c + 1]
                        nc.scalar.activation(x_hi[:, c, :], src, ACT.Copy, scale=scale).then_inc(spread_hi, 1)

            def turn_out(b):
                kind, c = BLOCKS[b]
                for t in range(T):
                    act.wait_ge(block_turned, turn_no(b, t))
                    src = ps[:, 4 + t, :].rearrange("p (c n) -> p c n", c=4)
                    tok = slice(t * P, (t + 1) * P)
                    low, high = slice(0, HD), slice(HD, P)
                    if kind == "tail_a":
                        nc.scalar.activation(kiT_low[low, tok], ps[low, 4 + t, 0:P], ACT.Copy)
                        nc.scalar.activation(kiT_high[high, tok], ps[high, 4 + t, 0:P], ACT.Copy).then_inc(turned_out, 1)
                    elif kind.endswith("k"):
                        nc.scalar.activation(kT[low, 0, 4 * c:4 * c + 4, tok], src[low], ACT.Copy)
                        nc.scalar.activation(kT[high, 1, 4 * c:4 * c + 4, tok], src[high], ACT.Copy).then_inc(turned_out, 1)
                    elif kind == "copy_q":
                        scale = HD ** -0.5
                        nc.scalar.activation(qT[low, 4 * c:4 * c + 4, tok], src[low], ACT.Copy, scale=scale)
                        nc.scalar.activation(qT_high[high, 4 * c:4 * c + 4, tok], src[high], ACT.Copy,
                                             scale=scale).then_inc(turned_out, 1)
                    else:
                        dst = qiT if kind == "rope_index" else qT
                        scale = HD ** -0.5 if kind.endswith("q") else 1.0
                        nc.scalar.activation(dst[:, 4 * c:4 * c + 4, tok], src, ACT.Copy, scale=scale).then_inc(turned_out, 1)

            def use(u):
                hi(u + AHEAD)

            def after_block(b):
                kind, c = BLOCKS[b]
                if kind in ("v", "copy_k", "copy_q"):
                    act.wait_ge(rstd_made, norm_of(b) + 1)
                if kind == "v":
                    for t in range(T):
                        block_ready(act, b, t)
                        nc.scalar.activation(val[:, t, c * HALF:(c + 1) * HALF], ps[:, bank_of(b, t), :], ACT.Copy,
                                             scale=rstd_of(b, t)).then_inc(evict_act, 1)
                if kind in ("copy_k", "copy_q"):
                    for t in range(T):
                        block_ready(act, b, t)
                        if t == 0 and b - 1 in TURNING:
                            act.wait_ge(block_turned, turn_no(b - 1, T - 1))
                        nc.scalar.activation(stage[:, t, :], ps[:, bank_of(b, t), :], ACT.Copy,
                                             scale=rstd_of(b, t)).then_inc(evict_act, 1)

            def blocks(bs):
                for b in bs:
                    s = SPREAD_BEHIND.get(b)
                    first, last = units_of(b)[0], units_of(b)[-1]
                    if b == B_FORGET + 2:
                        forget_rows()
                    if first != last:
                        use(first)
                        if b + 1 in NORM_BEHIND:
                            fetch_table(ACT.Sqrt)
                    else:
                        n = TAILS.index(b) + 1
                        act.wait_ge(tail_product, n)
                        width = WIDTH[BLOCKS[b][0]]
                        nc.scalar.activation(tailT[0:width, :], ps[0:width, bank_of(b, 0), 0:SEQ], ACT.Copy).then_inc(tail_copied, 1)
                        if b == 0:
                            hi(AHEAD - 1)
                            fetch_table(ACT.Exp)
                    if s:
                        spread(s, (0, 1))
                    if b == B_FORGET + 1:
                        forget()
                    if b - 1 in TURNING:
                        turn_out(b - 1)
                    after_block(b)
                    if s:
                        spread(s, (2, 3))
                    if b in NORM_BEHIND:
                        act.wait_ge(*evict_of(b, T - 1))
                        norm(NORM_BEHIND[b])
                        if b in BEFORE_ROUTING:
                            fetch_table(ACT.Exp)
                    if b not in BEFORE_ATTENTION + BEFORE_ROUTING:
                        use(last)
                    if b == 3:
                        for i in range(IDX_HEADS):
                            act.wait_ge(index_done, i + 1)
                            if i >= 2:
                                act.wait_ge(score_step, 2 * (i - 1))
                            nc.scalar.activation(relu[:, i % 2, :], ps[:, 6 + i % 2, 0:LOG], ACT.Relu).then_inc(relu_done, 1)

            def forget():
                act.wait_ge(f_step, 2)
                nc.scalar.activation(fe[:, :], fa[:, :], ACT.Exp, scale=-1.0).then_inc(f_exp, 1)
                act.wait_ge(f_exp, 1)
                nc.scalar.activation(fl[:, :], fe[:, :], ACT.Ln, bias=1.0).then_inc(f_ln, 1)
                fetch_table(ACT.Exp)

            def forget_rows():
                act.wait_ge(f_out, 2)
                act.dma_start(kT[HD:HD + 1, 0, :, :], neg_fT[:, 0, :]).then_inc(f_landed, 16)
                act.dma_start(kT[0:1, 1, :, :], neg_fT[:, 1, :]).then_inc(f_landed, 16)

            def attention(k):
                for n in range(STEPS):
                    if n < HEADS:
                        g = k * HEADS + n
                        act.wait_ge(masked, g + 1)
                        if n >= 2:
                            act.wait_ge(probs_turned, g - 1)
                        for t, cols in ((0, slice(0, P)), (1, slice(P, LOG))):
                            nc.scalar.activation(prob[:, n % 2, cols], logit[:, n % 2, cols], ACT.Exp,
                                                 bias=neg_max[:, 2 * n + t:2 * n + t + 1],
                                                 accum_out=row_sum[:, 2 * n + t:2 * n + t + 1]).then_inc(exp_done, 1)
                    m = n - TURN_LAG
                    if 0 <= m < HEADS:
                        g = k * HEADS + m
                        act.wait_ge(probs_turned, g + 1)
                        if m >= 2:
                            act.wait_ge(pv_done, g - 1)
                        nc.scalar.activation(probT[:, m % 2, :], ps[:, 4 + m % 2, 0:LOG], ACT.Copy).then_inc(probT_made, 1)
                    if n == HEADS:
                        use(units_of(BEFORE_ATTENTION[k])[-1])
                    if spread_round(n) is not None:
                        spread((SPREAD_A, SPREAD_B)[k], [spread_round(n)])

            act.wait_ge(ident_landed, 16)
            fetch_table(ACT.Sqrt)
            spread(0)
            for u in range(AHEAD - 1):
                hi(u)
            act.wait_ge(x_landed, 16)
            norm(0)
            blocks(B_A)
            attention(0)
            blocks(B_OUT_A)
            act.wait_ge(rstd_made, 2)
            for b in range(FB + 1):
                if b < FB:
                    use(DENSE_U + gate_up_unit(b, 0))
                if b >= 1:
                    act.wait_ge(hid_turned, b)
                    if b >= 3:
                        act.wait_ge(used, DENSE_U + down_unit(b - 3) + 1)
                    nc.scalar.activation(hid_hi[:, (b - 1) % 2, :, :],
                                         ps[:, 6 + (b - 1) % 2, :].rearrange("p (c n) -> p c n", c=2),
                                         ACT.Copy).then_inc(hid_hi_made, 1)
                if b < FB:
                    use(DENSE_U + gate_up_unit(b, 1))
                    for t in range(T):
                        if t == 0:
                            act.wait_ge(gu_tile0, b + 1)
                        else:
                            act.wait_ge(used, DENSE_U + gate_up_unit(b, 1) + 1)
                        if b >= 1:
                            act.wait_ge(hid_done, T * (b - 1) + t + 1)
                        nc.scalar.activation(silu[:, t, :], ps[:, gate_bank(b, t), 0:256], ACT.Silu,
                                             scale=rstd[:, 2 + t:3 + t]).then_inc(silu_done, 1)
                if 1 <= b < FB - 1:
                    use(DENSE_U + down_unit(b - 1))
            use(DENSE_U + down_unit(FB - 2))
            spread(3)
            use(DENSE_U + down_unit(FB - 1))
            act.wait_ge(added, 4)
            norm(2)
            blocks(B_Q)
            blocks(B_KV)
            attention(1)
            blocks(B_OUT_B)
            blocks([B_ROUTER])
            act.wait_ge(route_step, ROUTE_EXP)
            for t in range(T):
                nc.scalar.activation(r_exp[:, t, :], r_in[:, t, 0:EXPERTS], ACT.Exp, bias=r_neg[:, t:t + 1]).then_inc(route_exp, 1)
            for b in BEFORE_ROUTING:
                use(units_of(b)[-1])

            def hi_moe(it, m):
                s = m % RING
                _, n = raw_slot(PRE + m)
                act.wait_ge(landed[s], it * (16 * 2 * FFN_UNITS // RING) + 16 * n)
                moe_used(act, it, m - SPLIT)
                nc.scalar.activation(w_hi[:, (PRE + m) % SPLIT, :], raw_at(s, UNIT), ACT.Copy).then_inc(hi_made, 1)

            def tokens_out(it, e, buf):
                for c in range(KC):
                    if c % 4 == 0:
                        act.wait_ge(gathered, it * 4 + (2 * e + c // 4 + 1))
                    nc.scalar.activation(x_hi[:, c, buf * P:(buf + 1) * P],
                                         ps[:, 6 + c // 4, (c % 4) * P:(c % 4 + 1) * P], ACT.Copy,
                                         scale=gains[:, 4 * KC + c:4 * KC + c + 1]).then_inc(token_hi, 1)

            def silu_moe(it, n):
                moe_used(act, it, expert_unit(n, "gate_up", 1))
                act.wait_ge(hid_done, it * (2 * FB) + (T * FB + n - 1))
                nc.scalar.activation(silu[:, n % 2, :], ps[:, 2 + n % 2, 0:256], ACT.Silu).then_inc(silu_done, 1)

            def hid_moe(it, n):
                act.wait_ge(hid_turned, it * (2 * FB) + (FB + n + 1))
                moe_used(act, it, 3 * (n - 2) + 4)
                nc.scalar.activation(hid_hi[:, n % 2, :, 0:P],
                                     ps[:, 4 + n % 2, 0:256].rearrange("p (c n) -> p c n", c=2),
                                     ACT.Copy).then_inc(hid_hi_made, 1)

            def split_behind(it, m, last):
                if not last or m + AHEAD < MOE_UNITS * (m // MOE_UNITS + 1):
                    hi_moe(it, m + AHEAD)

            def expert(it, e, last):
                for b in range(2, FB if last else FB + 2):
                    n = FB * e + b
                    hid_moe(it, n - 1)
                    split_behind(it, expert_unit(n, "gate_up", 0), last)
                    if b == 7 and not last:
                        tokens_out(it, e + 1, (e + 1) % 2)
                    if b == PICKS_TURN:
                        act.wait_ge(block_turned, it * 2 + (TURNED + e + 1))
                        nc.scalar.activation(pickT[:, :], ps[:, 4 + n % 2, 0:256], ACT.Copy)
                        nc.scalar.activation(slot_gate, ps[:, 4 + n % 2, 256:257], ACT.Copy).then_inc(turned_out, 1)
                    silu_moe(it, n)
                    split_behind(it, expert_unit(n, "gate_up", 1), last)
                    if b == FB:
                        y_out_of_psum(it, e)
                    split_behind(it, expert_unit(n - 1, "down"), last)
                if last:
                    hid_moe(it, FB * e + FB - 1)
                    y_out_of_psum(it, e)

            def y_out_of_psum(it, e):
                moe_used(act, it, expert_unit(FB * e + FB - 1, "down"))
                act.wait_ge(turned_out, it * 2 + (TURNED + e + 1))
                for c in range(2):
                    nc.scalar.activation(y_hi[:, c * HALF:(c + 1) * HALF], ps[:, c, :], ACT.Copy,
                                         scale=slot_gate).then_inc(evict_act, 1)

            def experts(second):
                e0, n0, m0 = EXPERTS * second, EXPERTS * FB * second, MOE_UNITS * second
                if second:
                    for m in range(m0, m0 + AHEAD):
                        hi_moe(0, m)
                tokens_out(0, e0, 0)
                hi_moe(0, m0 + AHEAD)
                silu_moe(0, n0)
                hi_moe(0, m0 + AHEAD + 1)
                hid_moe(0, n0)
                hi_moe(0, m0 + AHEAD + 2)
                silu_moe(0, n0 + 1)
                hi_moe(0, m0 + AHEAD + 3)
                hi_moe(0, m0 + AHEAD + 4)
                with act.Fori(0, EXPERTS // 2 - 1) as it:
                    for p in range(2):
                        expert(it, e0 + p, False)
                expert(0, e0 + EXPERTS - 2, False)
                expert(0, e0 + EXPERTS - 1, True)

            experts(0)
            with act.If(act.value_load(flag[0:1, 0:1], min_val=0, max_val=1) > 0):
                experts(1)
            fetch_table(ACT.Sqrt)
            act.wait_ge(h_final, 1)
            norm(4)

        @block.vector
        def _(dve):
            def lo(u):
                words = words_of(u)
                s, _ = raw_slot(u)
                n = dve_part(words)
                dve.wait_ge(hi_made, u + 1)
                nc.vector.tensor_tensor(w_lo[:, u % SPLIT, 0:n], raw_at(s, n), w_hi[:, u % SPLIT, 0:n].bitcast(F32),
                                        ALU.subtract).then_inc(lo_made_dve, 1)

            def norm(n):
                c = 2 * n
                dve.wait_ge(squares, 2 * (n + 1))
                nc.vector.tensor_scalar(ms[:, c:c + 2], ssq[:, c:c + 2], 1.0 / D, EPS, ALU.mult, ALU.add).then_inc(mean_made, 1)
                dve.wait_ge(std_made, n + 1)
                nc.vector.reciprocal(rstd[:, c:c + 2], std[:, c:c + 2]).then_inc(rstd_made, 1)
                dve.wait_ge(rstd_made, n + 1)
                if n == 3:
                    for t in range(T):
                        nc.vector.tensor_scalar(xhat[:, t, :], h[:, t, :], rstd[:, c + t:c + t + 1], None,
                                                ALU.mult).then_inc(xhat_made, 1)

            def spread(s, rounds=range(KC // 2)):
                for j in rounds:
                    for c in chunks_of(s, j):
                        src = ps[:, spread_bank(s, j), (c % 2) * SEQ:(c % 2 + 1) * SEQ]
                        g = SPREAD[s]
                        dve.wait_ge(spread_hi, KC * s + round_chunks(s) * (j + 1))
                        hi_part = x_hi[:, c, :].bitcast(F32)
                        if g is None:
                            ins = nc.vector.tensor_tensor(x_lo[:, c, :], src, hi_part, ALU.subtract)
                        else:
                            ins = nc.vector.scalar_tensor_tensor(x_lo[:, c, :], src, gains[:, g * KC + c:g * KC + c + 1],
                                                                 hi_part, ALU.mult, ALU.subtract)
                        ins.then_inc(spread_lo, 1)

            f_steps = Count(f_step)

            def rope(b):
                kind, _ = BLOCKS[b]
                heads = 1 if kind == "tail_a" else 8
                for t in range(T):
                    block_ready(dve, b, t)
                    if t == 0 and b - 1 in TURNING:
                        dve.wait_ge(block_turned, turn_no(b - 1, T - 1))
                    src = ps[:, bank_of(b, t), 0:heads * HD].rearrange("p (h j d) -> p h j d", j=2, d=HD // 2)
                    w = turned[:, t, 0:heads * HD].rearrange("p (h j d) -> p h j d", j=2, d=HD // 2)
                    if kind == "tail_a":
                        nc.vector.tensor_scalar(wi[:, t, :], ps[:, bank_of(b, t), HD:A_TAIL], rstd_of(b, t),
                                                IDX_HEADS ** -0.5, ALU.mult, ALU.mult).then_inc(rope_cos, 1)
                    s = sin[:, t, :].rearrange("p (j d) -> p j d", j=2)
                    nc.vector.scalar_tensor_tensor(
                        stage[:, t, 0:heads * HD].rearrange("p (h n) -> p h n", n=HD),
                        ps[:, bank_of(b, t), 0:heads * HD].rearrange("p (h n) -> p h n", n=HD), rstd_of(b, t),
                        cos[:, t, :].unsqueeze(1).to_broadcast([P, heads, HD]), ALU.mult, ALU.mult).then_inc(rope_cos, 1)
                    for j in range(2):
                        ins = nc.vector.scalar_tensor_tensor(w[:, :, j, :], src[:, :, 1 - j, :], rstd_of(b, t),
                                                             s[:, j:j + 1, :].to_broadcast([P, heads, HD // 2]),
                                                             ALU.mult, ALU.mult)
                        ins.then_inc(rope_cos if j == 0 else evict_dve, 1)

            def forget():
                b = B_FORGET
                for t in range(T):
                    block_ready(dve, b, t)
                    nc.vector.scalar_tensor_tensor(fz[:, t, :], ps[:, bank_of(b, t), 0:HEADS], rstd_of(b, t), bf_rows[:, :],
                                                   ALU.mult, ALU.add).then_inc(evict_dve, 1)
                dve.wait_ge(evict_dve, evict_of(b, T - 1)[1])
                zf = fz.rearrange("p t n -> p (t n)")
                f_steps.by(nc.vector.scalar_tensor_tensor(fa[:, :], zf, -1.0, zf, ALU.mult, ALU.max))
                f_steps.by(nc.vector.tensor_scalar(f_tok.rearrange("p t n -> p (t n)"), zf, 0.0, None, ALU.min))

            def forget_sum():
                dve.wait_ge(f_ln, 1)
                dve.wait_ge(f_step, 2)
                f_steps.by(nc.vector.tensor_tensor(lf[:, :], f_tok.rearrange("p t n -> p (t n)"), fl[:, :], ALU.subtract))

            def forget_out():
                dve.wait_ge(f_cum, 1)
                nc.vector.tensor_copy(f_tok.rearrange("p t n -> p (t n)"), ps[:, 6, 0:2 * HEADS]).then_inc(f_out, 1)
                nc.vector.tensor_scalar(neg_fT, ps[0:HEADS // 2, 7, :].rearrange("c (o t) -> c o t", o=2), -1.0, None,
                                        ALU.mult).then_inc(f_out, 1)

            def after_block(b):
                kind, c = BLOCKS[b]
                if b in ROPING:
                    rope(b)
                elif kind == "res":
                    for t in range(T):
                        block_ready(dve, b, t)
                        cols = h[:, t, c * HALF:(c + 1) * HALF]
                        nc.vector.tensor_tensor(cols, ps[:, bank_of(b, t), :], cols, ALU.add).then_inc(evict_dve, 1)
                elif kind == "tail_f":
                    forget()
                elif kind == "router":
                    for t in range(T):
                        block_ready(dve, b, t)
                        nc.vector.tensor_scalar(r_in[:, t, 0:EXPERTS], ps[:, bank_of(b, t), 0:EXPERTS], rstd_of(b, t), None,
                                                ALU.mult).then_inc(evict_dve, 1)

            scores = Count(score_step)
            spans = ((slice(0, P), slice(0, P)), (slice(P, LOG), slice(2 * P, LOG)))

            def add_scores():
                for i in range(IDX_HEADS):
                    dve.wait_ge(relu_done, i + 1)
                    if i:
                        dve.wait_ge(score_step, scores.n)
                    for t, (cols, _) in enumerate(spans):
                        if i == 0:
                            scores.by(nc.vector.tensor_scalar(score[:, cols], relu[:, 0, cols], wi[:, t, 0:1], None, ALU.mult))
                        else:
                            scores.by(nc.vector.scalar_tensor_tensor(score[:, cols], relu[:, i % 2, cols], wi[:, t, i:i + 1],
                                                                     score[:, cols], ALU.mult, ALU.add))
                dve.wait_ge(score_step, scores.n)
                for t, (_, own) in enumerate(spans):
                    scores.by(nc.vector.tensor_tensor(score[:, own], score[:, own], chunk_mask, ALU.add))
                dve.wait_ge(score_step, scores.n)

            def choose_keys():
                for t, (cols, _) in enumerate(spans):
                    scores.by(nc.vector.max(top8[:, t, :], score[:, cols]))
                dve.wait_ge(score_step, scores.n)
                for t, (cols, _) in enumerate(spans):
                    scores.by(nc.vector.match_replace(score[:, cols], top8[:, t, :], score[:, cols], TAKEN))
                dve.wait_ge(score_step, scores.n)

            rounds = [0]

            def blocks(bs):
                for b in bs:
                    s = SPREAD_BEHIND.get(b)
                    first, last = units_of(b)[0], units_of(b)[-1]
                    if b == B_FORGET + 2:
                        forget_out()
                    if first != last:
                        lo(first + AHEAD)
                    if s:
                        spread(s, (0, 1))
                    if b == B_FORGET + 1:
                        forget_sum()
                    if b == 3:
                        add_scores()
                    for _ in range({4: 2, 5: 2, 6: 4}.get(b, 0)):
                        choose_keys()
                        rounds[0] += 1
                    if b == 6:
                        assert rounds[0] * 8 == TOPK
                        nc.vector.tensor_scalar(masks[:, :], score[:, :], TAKEN / 2, NEG, ALU.is_gt, ALU.mult).then_inc(mask_made, 1)
                    after_block(b)
                    if s:
                        spread(s, (2, 3))
                    if b in NORM_BEHIND:
                        norm(NORM_BEHIND[b])
                    if b not in BEFORE_ATTENTION + BEFORE_ROUTING:
                        lo(last + AHEAD)

            def attention(k):
                for n in range(STEPS):
                    if n < HEADS:
                        g = k * HEADS + n
                        dve.wait_ge(logits_done, g + 1)
                        if n >= 2:
                            dve.wait_ge(exp_done, 2 * (g - 1))
                        for t, cols in ((0, slice(0, P)), (1, slice(P, LOG))):
                            src, dst = ps[:, n % 2, cols], logit[:, n % 2, cols]
                            add = (masks if k == 0 else causal)[:, cols]
                            steps.by(nc.vector.tensor_tensor_reduce(dst, src, add, 1.0, TAKEN, ALU.add, ALU.max,
                                                                    row_max[:, 2 * n + t:2 * n + t + 1]))
                        dve.wait_ge(max_step, steps.n)
                        two = slice(2 * n, 2 * n + 2)
                        if k == 0:
                            nc.vector.tensor_scalar(neg_max[:, two], row_max[:, two], -1.0, None, ALU.mult).then_inc(masked, 1)
                        else:
                            steps.by(nc.vector.tensor_tensor(full_max[:, two], row_max[:, two], f_tok[:, :, n], ALU.add))
                            dve.wait_ge(max_step, steps.n)
                            nc.vector.tensor_tensor(neg_max[:, two], f_tok[:, :, n], full_max[:, two], ALU.subtract).then_inc(masked, 1)
                    m = n - OUT_LAG
                    if 0 <= m < HEADS:
                        g = k * HEADS + m
                        two = slice(2 * m, 2 * m + 2)
                        dve.wait_ge(exp_done, 2 * (g + 1))
                        nc.vector.reciprocal(row_inv[:, two], row_sum[:, two]).then_inc(inv_made, 1)
                        dve.wait_ge(inv_made, g + 1)
                        dve.wait_ge(pv_done, g + 1)
                        for t in range(T):
                            nc.vector.tensor_scalar(xhat[:, t, m * HD:(m + 1) * HD], ps[:, 6 + m % 2, t * HD:(t + 1) * HD],
                                                    row_inv[:, 2 * m + t:2 * m + t + 1], None, ALU.mult).then_inc(head_out, 1)
                    if n == HEADS + 2:
                        lo(units_of(BEFORE_ATTENTION[k])[-1] + AHEAD)
                    if spread_round(n) is not None:
                        spread((SPREAD_A, SPREAD_B)[k], [spread_round(n)])

            steps = Count(max_step)
            dve.wait_ge(small_landed, 32)
            spread(0)
            for u in range(AHEAD - 1):
                lo(u)
            norm(0)
            lo(AHEAD - 1)
            dve.wait_ge(consts_landed, 16)
            blocks(B_A)
            dve.wait_ge(mask_made, 1)
            attention(0)
            blocks(B_OUT_A)
            for b in range(FB + 1):
                if b < FB:
                    lo(DENSE_U + gate_up_unit(b, 0) + AHEAD)
                if b >= 1:
                    dve.wait_ge(hid_hi_made, b)
                    nc.vector.tensor_tensor(hid_lo[:, (b - 1) % 2, :, :],
                                            ps[:, 6 + (b - 1) % 2, :].rearrange("p (c n) -> p c n", c=2),
                                            hid_hi[:, (b - 1) % 2, :, :].bitcast(F32), ALU.subtract).then_inc(hid_lo_made, 1)
                if b < FB:
                    lo(DENSE_U + gate_up_unit(b, 1) + AHEAD)
                    for t in range(T):
                        dve.wait_ge(silu_done, T * b + t + 1)
                        if b >= 1 and t == 0:
                            dve.wait_ge(hid_turned, b)
                        nc.vector.scalar_tensor_tensor(hid[:, t, :], ps[:, gate_bank(b, t), 256:512], rstd[:, 2 + t:3 + t], silu[:, t, :],
                                                       ALU.mult, ALU.mult).then_inc(hid_done, 1)
                if 1 <= b < FB - 1:
                    lo(DENSE_U + down_unit(b - 1) + AHEAD)
            lo(DENSE_U + down_unit(FB - 2) + AHEAD)
            for c in range(2):
                if c == 0:
                    dve.wait_ge(down_half, 1)
                else:
                    dve.wait_ge(used, DENSE_U + FFN_UNITS)
                for t in range(T):
                    cols = h[:, t, c * HALF:(c + 1) * HALF]
                    nc.vector.tensor_tensor(cols, ps[:, 2 * t + c, :], cols, ALU.add).then_inc(added, 1)
            spread(3)
            lo(DENSE_U + down_unit(FB - 1) + AHEAD)
            norm(2)
            blocks(B_Q)
            blocks(B_KV)
            dve.wait_ge(f_out, 2)
            attention(1)
            blocks(B_OUT_B)
            route = Count(route_step)

            def link(ins):
                route.by(ins)
                dve.wait_ge(route_step, route.n)

            nc.vector.memset(r_in[:, :, EXPERTS:14], TAKEN).then_inc(route_step, 1)
            nc.vector.memset(r_rep[:, :, :], TAKEN).then_inc(route_step, 1)
            route.n = 2
            blocks([B_ROUTER])
            dve.wait_ge(evict_dve, n_dve)
            dve.wait_ge(route_step, 2)
            for t in range(T):
                route.by(nc.vector.max(r_top[:, t, :], r_in[:, t, :]))
            dve.wait_ge(route_step, route.n)
            link(nc.vector.tensor_scalar(r_neg, r_top[:, :, 0], -1.0, None, ALU.mult))
            assert route.n == ROUTE_EXP
            link(nc.vector.tensor_copy(r_rep[:, :, 0:2], r_top[:, :, 0:2]))
            for t in range(T):
                route.by(nc.vector.match_replace(r_out[:, t, :], r_rep[:, t, :], r_in[:, t, :], -TAKEN))
            dve.wait_ge(route_step, route.n)
            link(nc.vector.tensor_scalar(chosen, r_out[:, :, 0:EXPERTS], -TAKEN / 2, None, ALU.is_gt))
            assert route.n == ROUTE_CHOSEN
            dve.wait_ge(route_exp, 2)
            link(nc.vector.tensor_tensor(gate, r_exp, chosen, ALU.mult))
            link(nc.vector.tensor_reduce(r_den, gate, AX_X, ALU.add))
            link(nc.vector.reciprocal(r_inv, r_den))
            for t in range(T):
                route.by(nc.vector.tensor_scalar(gate[:, t, :], gate[:, t, :], r_inv[:, t:t + 1], None, ALU.mult))
            dve.wait_ge(route_step, route.n)
            dve.wait_ge(route_cum, 1)
            link(nc.vector.tensor_copy(slot, ps[:, 6, 0:16].rearrange("p (t n) -> p t n", t=T)))
            def lo_moe(it, m):
                s = m % RING
                n = dve_part(UNIT)
                i = (PRE + m) % SPLIT
                dve.wait_ge(hi_made, it * 66 + (PRE + m + 1))
                nc.vector.tensor_tensor(w_lo[:, i, 0:n], raw_at(s, n), w_hi[:, i, 0:n].bitcast(F32),
                                        ALU.subtract).then_inc(lo_made_dve, 1)

            def column(table, t, it, e):
                e = e % EXPERTS
                if isinstance(it, int):
                    return table[:, t, e + 2 * it:e + 2 * it + 1]
                return table[:, t, bass.ds(it * 2 + e, 1)]

            def pick_tokens(it, e):
                dve.wait_ge(gathered, it * 4 + 2 * e)
                dve.wait_ge(block_turned, it * 2 + (TURNED + e))
                for t in range(T):
                    ins = nc.vector.tensor_scalar(pick[:, t, :], iota1, column(slot, t, it, e), column(chosen, t, it, e),
                                                  ALU.is_equal, ALU.mult)
                    ins.then_inc(pick_made, 1)
                if isinstance(it, int):
                    column_now = slice(e % EXPERTS + 2 * it, e % EXPERTS + 2 * it + 1)
                else:
                    column_now = bass.ds(it * 2 + e % EXPERTS, 1)
                nc.vector.tensor_copy(expert_gate, gate[:, :, column_now]).then_inc(pick_made, 1)


            def tokens_out(it, e, buf):
                for c in range(KC):
                    dve.wait_ge(token_hi, it * (2 * KC) + (KC * e + 4 * (c // 4 + 1)))
                    nc.vector.scalar_tensor_tensor(x_lo[:, c, buf * P:(buf + 1) * P],
                                                   ps[:, 6 + c // 4, (c % 4) * P:(c % 4 + 1) * P],
                                                   gains[:, 4 * KC + c:4 * KC + c + 1],
                                                   x_hi[:, c, buf * P:(buf + 1) * P].bitcast(F32),
                                                   ALU.mult, ALU.subtract).then_inc(token_lo, 1)

            def hid_moe(it, n):
                dve.wait_ge(silu_done, it * (2 * FB) + (T * FB + n + 1))
                dve.wait_ge(hid_turned, it * (2 * FB) + (FB + n - 1))
                nc.vector.tensor_tensor(hid[:, n % 2, :], ps[:, 2 + n % 2, 256:512], silu[:, n % 2, :], ALU.mult).then_inc(hid_done, 1)

            def hid_lo_moe(it, n):
                dve.wait_ge(hid_hi_made, it * (2 * FB) + (FB + n + 1))
                nc.vector.tensor_tensor(hid_lo[:, n % 2, :, 0:P],
                                        ps[:, 4 + n % 2, 0:256].rearrange("p (c n) -> p c n", c=2),
                                        hid_hi[:, n % 2, :, 0:P].bitcast(F32), ALU.subtract).then_inc(hid_lo_made, 1)

            def split_behind(it, m, last):
                if not last or m + AHEAD < MOE_UNITS * (m // MOE_UNITS + 1):
                    lo_moe(it, m + AHEAD)

            def expert(it, e, last):
                for b in range(2, FB if last else FB + 2):
                    n = FB * e + b
                    hid_lo_moe(it, n - 1)
                    split_behind(it, expert_unit(n, "gate_up", 0), last)
                    if b == 4 and not last:
                        pick_tokens(it, e + 1)
                    if b == 7 and not last:
                        tokens_out(it, e + 1, (e + 1) % 2)
                    hid_moe(it, n)
                    if b == FB + 1:
                        add_experts(it, e, (0, 1))
                    split_behind(it, expert_unit(n, "gate_up", 1), last)
                    if b == FB + 1:
                        add_experts(it, e, (2, 3))
                    if b == FB:
                        y_out_of_psum(it, e)
                    split_behind(it, expert_unit(n - 1, "down"), last)
                if last:
                    hid_lo_moe(it, FB * e + FB - 1)
                    y_out_of_psum(it, e)
                    add_experts(it, e)

            def y_out_of_psum(it, e):
                for c in range(2):
                    dve.wait_ge(evict_act, it * 4 + (n_act + 2 * e + c + 1))
                    cols = slice(c * HALF, (c + 1) * HALF)
                    nc.vector.scalar_tensor_tensor(y_lo[:, cols], ps[:, c, :], slot_gate, y_hi[:, cols].bitcast(F32),
                                                   ALU.mult, ALU.subtract).then_inc(evict_dve, 1)

            def add_experts(it, e, quarters=range(4)):
                for q in quarters:
                    t, c = q // 2, q % 2
                    dve.wait_ge(scattered, it * 8 + (4 * e + q + 1))
                    cols = h[:, t, c * HALF:(c + 1) * HALF]
                    nc.vector.tensor_tensor(cols, ps[:, 6 + q % 2, :], cols, ALU.add).then_inc(added, 1)

            def overflow_flag():
                dve.wait_ge(route_cum, 2)
                link(nc.vector.tensor_reduce(r_most, ps[:, 3, 0:8], AX_X, ALU.max))
                link(nc.vector.tensor_scalar(flag[:, :], r_most, float(P), None, ALU.is_gt))
                assert route.n == ROUTE_STEPS

            def experts(second):
                e0, n0, m0 = EXPERTS * second, EXPERTS * FB * second, MOE_UNITS * second
                if second:
                    dve.wait_ge(pick_made, (T + 1) * EXPERTS)
                    nc.vector.tensor_scalar(slot, slot, -float(P), None, ALU.add).then_inc(shifted, 1)
                    dve.wait_ge(shifted, 1)
                    for m in range(m0, m0 + AHEAD):
                        lo_moe(0, m)
                pick_tokens(0, e0)
                if not second:
                    overflow_flag()
                    for b in BEFORE_ROUTING:
                        lo(units_of(b)[-1] + AHEAD)
                tokens_out(0, e0, 0)
                lo_moe(0, m0 + AHEAD)
                hid_moe(0, n0)
                lo_moe(0, m0 + AHEAD + 1)
                hid_lo_moe(0, n0)
                lo_moe(0, m0 + AHEAD + 2)
                hid_moe(0, n0 + 1)
                lo_moe(0, m0 + AHEAD + 3)
                lo_moe(0, m0 + AHEAD + 4)
                with dve.Fori(0, EXPERTS // 2 - 1) as it:
                    for p in range(2):
                        expert(it, e0 + p, False)
                expert(0, e0 + EXPERTS - 2, False)
                expert(0, e0 + EXPERTS - 1, True)

            experts(0)
            with dve.If(dve.value_load(flag[0:1, 0:1], min_val=0, max_val=1) > 0):
                experts(1)
            nc.vector.tensor_copy(top8[:, 0, 0:1], row_sum[:, 0:1]).then_inc(h_final, 1)
            norm(4)
            dve.wait_ge(gain_landed, 16)
            for t in range(T):
                nc.vector.scalar_tensor_tensor(xhat[:, t, :], h[:, t, :], rstd[:, 8 + t:9 + t], fin_gain,
                                               ALU.mult, ALU.mult).then_inc(out_made, 1)

        @block.gpsimd
        def _(pool):
            def lo_part(i, s, words):
                n = dve_part(words)
                nc.gpsimd.tensor_tensor(w_lo[:, i, n:words], raw[:, s * UNIT + n:s * UNIT + words],
                                        w_hi[:, i, n:words].bitcast(F32), ALU.subtract).then_inc(lo_made_pool, 1)

            def lo(u):
                pool.wait_ge(hi_made, u + 1)
                lo_part(u % SPLIT, raw_slot(u)[0], words_of(u))

            def rope(b):
                heads = 1 if BLOCKS[b][0] == "tail_a" else 8
                for t in range(T):
                    pool.wait_ge(evict_dve, evict_of(b, t)[1])
                    a, w = stage[:, t, 0:heads * HD], turned[:, t, 0:heads * HD]
                    if heads == 1:
                        nc.gpsimd.tensor_tensor(stage[:, t, HD:2 * HD], a, w, ALU.add).then_inc(index_key_copy, 1)
                        pool.wait_ge(index_key_copy, t + 1)
                    nc.gpsimd.tensor_tensor(a, a, w, ALU.add).then_inc(rope_done, 1)

            zeros = (kT[HD:P, 0, :, :], kT[0:HD, 1, :, :], kiT_low[HD:P, :], kiT_high[0:HD, :])
            for i, block_of_zeros in enumerate(zeros):
                if i:
                    pool.wait_ge(zeroed, i)
                nc.gpsimd.memset(block_of_zeros, 0.0).then_inc(zeroed, 1)
            assert len(zeros) == ZEROED
            for u in range(AHEAD):
                lo(u)
            for b in range(len(BLOCKS)):
                if b == B_Q[0]:
                    pool.wait_ge(pv_done, HEADS)
                    pool.wait_ge(lo_made_pool, DENSE_U + AHEAD)
                    nc.gpsimd.memset(qT[HD:HD + 1, :, :], 1.0).then_inc(ones_made, 1)
                    pool.wait_ge(ones_made, 1)
                    nc.gpsimd.memset(qT_high[0:1, :, :], 1.0).then_inc(ones_made, 1)
                    pool.wait_ge(ones_made, 2)
                    for u in range(DENSE_U, DENSE_U + FFN_UNITS):
                        lo(u + AHEAD)
                for u in units_of(b):
                    lo(u + AHEAD)
                if b in ROPING:
                    rope(b)

            def stream(first, last):
                with pool.Fori(first, last) as j:
                    for m in range(FFN_UNITS):
                        pool.wait_ge(hi_made, j * FFN_UNITS + (PRE + AHEAD + m + 1))
                        lo_part((PRE + AHEAD + m) % SPLIT, (AHEAD + m) % RING, UNIT)

            def tail(base):
                for m in range(base + MOE_UNITS - FFN_UNITS + AHEAD, base + MOE_UNITS):
                    lo(PRE + m)

            stream(0, EXPERTS - 1)
            tail(0)
            with pool.If(pool.value_load(flag[0:1, 0:1], min_val=0, max_val=1) > 0):
                for m in range(MOE_UNITS, MOE_UNITS + AHEAD):
                    lo(PRE + m)
                stream(EXPERTS, 2 * EXPERTS - 1)
                tail(MOE_UNITS)

        @block.tensor
        def _(pe):
            def mm3(dst, xh, xl, wh, wl, first, last):
                pe.matmul(dst, xh, wh, start=first, stop=False)
                pe.matmul(dst, xh, wl, start=False, stop=False)
                return pe.matmul(dst, xl, wh, start=False, stop=last)

            def split_of(u):
                pe.wait_ge(lo_made_dve, u + 1)
                pe.wait_ge(lo_made_pool, u + 1)
                return w_hi[:, u % SPLIT, :], w_lo[:, u % SPLIT, :]

            def spread(s, rounds=range(KC // 2)):
                src = xhat if s in (SPREAD_A, SPREAD_B) else h
                for j in rounds:
                    if s == 0 and j == 0:
                        pe.wait_ge(x_landed, 16)
                    elif s in (SPREAD_A, SPREAD_B):
                        pe.wait_ge(head_out, 2 * (HEADS * (s == SPREAD_B) + 2 * (j + 1)))
                    elif s in (2, 6):
                        pe.wait_ge(*evict_of((B_OUT_A if s == 2 else B_OUT_B)[j // 2], T - 1))
                    elif s == 3:
                        pe.wait_ge(added, T * (j // 2 + 1))
                    if j >= 2 and spread_bank(s, j) == spread_bank(s, j - 2):
                        pe.wait_ge(spread_lo, KC * s + round_chunks(s) * (j - 1))
                    for c in chunks_of(s, j):
                        for t in range(T):
                            at_col = (c % 2) * SEQ + t * P
                            mm = pe.transpose(ps[:, spread_bank(s, j), at_col:at_col + P], src[:, t, c * P:(c + 1) * P], ident)
                    mm.then_inc(spread_turned, 1)

            def project_tail(b, s=None):
                width = WIDTH[BLOCKS[b][0]]
                wh, wl = split_of(units_of(b)[0])
                if s is not None:
                    pe.wait_ge(spread_lo, KC * (s + 1))
                for c in range(KC):
                    cols = slice(c * width, (c + 1) * width)
                    mm = mm3(ps[0:width, bank_of(b, 0), 0:SEQ], wh[:, cols], wl[:, cols], x_hi[:, c, :], x_lo[:, c, :],
                             c == 0, c == KC - 1)
                mm.then_inc(tail_product, 1)
                pe.wait_ge(tail_copied, TAILS.index(b) + 1)
                for t in range(T):
                    pe.transpose(ps[:, bank_of(b, t), 0:width], tailT[0:width, t * P:(t + 1) * P],
                                 ident[0:width, 0:width]).then_inc((tile0_done, used)[t], 1)

            def project(b, s=None):
                if b in TAILS:
                    return project_tail(b, s)
                us = units_of(b)
                chunks = KC // len(us)
                for i, u in enumerate(us):
                    wh, wl = split_of(u)
                    if s is not None:
                        pe.wait_ge(spread_lo, KC * s + (i + 1) * chunks)
                    for t in range(T):
                        for k in range(chunks):
                            c = i * chunks + k
                            cols = slice(k * HALF, (k + 1) * HALF)
                            toks = slice(t * P, (t + 1) * P)
                            mm = mm3(ps[:, bank_of(b, t), 0:HALF], x_hi[:, c, toks], x_lo[:, c, toks],
                                     wh[:, cols], wl[:, cols], c == 0, c == KC - 1)
                        if i == len(us) - 1 and t == 0:
                            mm.then_inc(tile0_done, 1)
                    mm.then_inc(used, 1)
                    if b in SPREAD_BEHIND:
                        spread(SPREAD_BEHIND[b], (2 * i, 2 * i + 1))

            def turn(b):
                for t in range(T):
                    if b in ROPING:
                        pe.wait_ge(rope_done, rope_no(b, t))
                    else:
                        pe.wait_ge(*evict_of(b, t))
                    before = TURNING.index(b) - 1
                    if before >= 0:
                        pe.wait_ge(turned_out, T * before + t + 1)
                    n = 1 if BLOCKS[b][0] == "tail_a" else 4
                    for i in range(n):
                        mm = pe.transpose(ps[:, 4 + t, i * P:(i + 1) * P], stage[:, t, i * P:(i + 1) * P], ident)
                    mm.then_inc(block_turned, 1)

            def blocks(bs, s):
                for b in bs:
                    if b - 2 in bs or b in B_KV:
                        for t in range(T):
                            pe.wait_ge(*evict_of(b - 2, t))
                    project(b, s if b == bs[0] else None)
                    if b - 1 in TURNING:
                        turn(b - 1)
                    if b == 3:
                        index()
                    if b == B_FORGET + 1:
                        forget()

            def index():
                pe.wait_ge(turned_out, turn_no(1, T - 1))
                pe.wait_ge(zeroed, ZEROED)
                for i in range(IDX_HEADS):
                    if i >= 2:
                        pe.wait_ge(relu_done, i - 1)
                    c, bank, key = i // 2, 6 + i % 2, (kiT_low, kiT_high)[i % 2]
                    pe.matmul(ps[:, bank, 0:P], qiT[:, c, 0:P], key[:, 0:P], start=True, stop=True)
                    pe.matmul(ps[:, bank, P:LOG], qiT[:, c, P:SEQ], key, start=True, stop=True).then_inc(index_done, 1)

            def attention(k):
                for n in range(STEPS):
                    if n < HEADS:
                        g = k * HEADS + n
                        if n >= 2:
                            pe.wait_ge(masked, g - 1)
                        c = n // 2
                        q = qT_high if k == 1 and n % 2 else qT
                        for t, cols, keys in ((0, slice(0, P), P), (1, slice(P, LOG), SEQ)):
                            mm = pe.matmul(ps[:, n % 2, cols], q[:, c, t * P:(t + 1) * P], kT[:, n % 2, c, 0:keys],
                                           start=True, stop=True)
                        mm.then_inc(logits_done, 1)
                    m = n - TURN_LAG
                    if 0 <= m < HEADS:
                        g = k * HEADS + m
                        pe.wait_ge(exp_done, 2 * (g + 1))
                        if m >= 2:
                            pe.wait_ge(probT_made, g - 1)
                        for i in range(3):
                            mm = pe.transpose(ps[:, 4 + m % 2, i * P:(i + 1) * P], prob[:, m % 2, i * P:(i + 1) * P], ident)
                        mm.then_inc(probs_turned, 1)
                    m = n - PV_LAG
                    if 0 <= m < HEADS:
                        g = k * HEADS + m
                        pe.wait_ge(probT_made, g + 1)
                        if m == 0:
                            pe.wait_ge(*evict_of((B_A, B_KV)[k][-1], T - 1))
                        if m >= 2:
                            pe.wait_ge(head_out, 2 * (g - 1))
                        cols = slice(m * HD, (m + 1) * HD)
                        bank = 6 + m % 2
                        pe.matmul(ps[:, bank, 0:HD], probT[:, m % 2, 0:P], val[:, 0, cols], start=True, stop=True)
                        pe.matmul(ps[:, bank, HD:2 * HD], probT[:, m % 2, P:2 * P], val[:, 0, cols], start=True, stop=False)
                        pe.matmul(ps[:, bank, HD:2 * HD], probT[:, m % 2, 2 * P:LOG], val[:, 1, cols],
                                  start=False, stop=True).then_inc(pv_done, 1)
                    if spread_round(n) is not None:
                        spread((SPREAD_A, SPREAD_B)[k], [spread_round(n)])

            def forget():
                pe.wait_ge(consts_landed, 16)
                pe.wait_ge(f_step, 3)
                l0, l1 = lf[:, 0:HEADS], lf[:, HEADS:2 * HEADS]
                pe.matmul(ps[:, 6, 0:HEADS], upper, l0, start=True, stop=True)
                pe.matmul(ps[:, 6, HEADS:2 * HEADS], ones, l0, start=True, stop=False)
                pe.matmul(ps[:, 6, HEADS:2 * HEADS], upper, l1, start=False, stop=True)
                pairs = HEADS // 2
                for o in range(2):
                    even_or_odd = slice(o, HEADS, 2)
                    tile0, tile1 = slice(o * SEQ, o * SEQ + P), slice(o * SEQ + P, (o + 1) * SEQ)
                    pe.matmul(ps[0:pairs, 7, tile0], l0[:, even_or_odd], upper, start=True, stop=True)
                    pe.matmul(ps[0:pairs, 7, tile1], l0[:, even_or_odd], ones, start=True, stop=False)
                    mm = pe.matmul(ps[0:pairs, 7, tile1], l1[:, even_or_odd], upper, start=False, stop=True)
                mm.then_inc(f_cum, 1)

            pe.wait_ge(ident_landed, 16)
            spread(0)
            blocks(B_A, 0)
            pe.wait_ge(*evict_of(B_A[-2], T - 1))
            pe.wait_ge(turned_out, turn_no(5, T - 1))
            attention(0)
            blocks(B_OUT_A, SPREAD_A)

            def dense_turn(n):
                pe.wait_ge(hid_done, T * (n + 1))
                if n >= 2:
                    pe.wait_ge(hid_lo_made, n - 1)
                for c in range(2):
                    for t in range(T):
                        at_col = c * SEQ + t * P
                        mm = pe.transpose(ps[:, 6 + n % 2, at_col:at_col + P], hid[:, t, c * P:(c + 1) * P], ident)
                mm.then_inc(hid_turned, 1)

            for b in range(FB + 1):
                for i in range(2):
                    if b < FB:
                        wh, wl = split_of(DENSE_U + gate_up_unit(b, i))
                        if b == 0:
                            pe.wait_ge(spread_lo, KC * 2 + 4 * (i + 1))
                        for t in range(T):
                            if b >= 2 and i == 0:
                                pe.wait_ge(hid_done, T * (b - 1) + t + 1)
                            toks = slice(t * P, (t + 1) * P)
                            for k in range(4):
                                c = 4 * i + k
                                mm = mm3(ps[:, gate_bank(b, t), :], x_hi[:, c, toks], x_lo[:, c, toks],
                                         wh[:, k * HALF:(k + 1) * HALF], wl[:, k * HALF:(k + 1) * HALF], c == 0, c == KC - 1)
                            if i == 1 and t == 0:
                                mm.then_inc(gu_tile0, 1)
                        mm.then_inc(used, 1)
                    if 1 <= b < FB and i == 0:
                        dense_turn(b - 1)
                if b >= 1:
                    n = b - 1
                    pe.wait_ge(hid_lo_made, n + 1)
                    wh, wl = split_of(DENSE_U + down_unit(n))
                    for c in range(2):
                        for t in range(T):
                            toks = slice(t * P, (t + 1) * P)
                            for k in range(2):
                                cols = slice(k * D + c * HALF, k * D + (c + 1) * HALF)
                                mm = mm3(ps[:, 2 * t + c, :], hid_hi[:, n % 2, k, toks], hid_lo[:, n % 2, k, toks],
                                         wh[:, cols], wl[:, cols], n == 0 and k == 0, n == FB - 1 and k == 1)
                        if n == FB - 1 and c == 0:
                            mm.then_inc(down_half, 1)
                        if n == FB - 2 and c == 0:
                            dense_turn(FB - 1)
                    mm.then_inc(used, 1)
            spread(3)
            blocks(B_Q, 3)
            blocks(B_KV, 4)
            pe.wait_ge(turned_out, turn_no(B_KV[1], T - 1))
            pe.wait_ge(*evict_of(B_KV[-2], T - 1))
            pe.wait_ge(f_landed, 32)
            pe.wait_ge(ones_made, 2)
            attention(1)
            blocks(B_OUT_B, SPREAD_B)
            blocks([B_ROUTER], 6)
            pe.wait_ge(route_step, ROUTE_CHOSEN)
            pe.matmul(ps[:, 6, 0:8], upper, chosen[:, 0, :], start=True, stop=True)
            pe.matmul(ps[:, 6, 8:16], ones, chosen[:, 0, :], start=True, stop=False)
            pe.matmul(ps[:, 6, 8:16], upper, chosen[:, 1, :], start=False, stop=True).then_inc(route_cum, 1)
            pe.matmul(ps[:, 3, 0:8], ones, chosen[:, 0, :], start=True, stop=False)
            pe.matmul(ps[:, 3, 0:8], ones, chosen[:, 1, :], start=False, stop=True).then_inc(route_cum, 1)

            pe.wait_ge(xhat_made, T)

            def split_of_moe(it, m):
                pe.wait_ge(lo_made_dve, it * (2 * FFN_UNITS) + (PRE + m + 1))
                pe.wait_ge(lo_made_pool, it * (2 * FFN_UNITS) + (PRE + m + 1))
                i = (PRE + m) % SPLIT
                return w_hi[:, i, :], w_lo[:, i, :]

            def gather(it, e):
                pe.wait_ge(pick_made, it * 2 * (T + 1) + (T + 1) * (e + 1))
                if e >= 1:
                    pe.wait_ge(added, it * 8 + 4 * e)
                for c in range(KC):
                    for t in range(T):
                        mm = pe.matmul(ps[:, 6 + c // 4, (c % 4) * P:(c % 4 + 1) * P], xhat[:, t, c * P:(c + 1) * P],
                                       pick[:, t, :], start=(t == 0), stop=(t == T - 1))
                    if c % 4 == 3:
                        mm.then_inc(gathered, 1)

            def gate_up(it, n, i):
                if i == 0:
                    pe.wait_ge(hid_done, it * (2 * FB) + (T * FB + n - 1))
                wh, wl = split_of_moe(it, expert_unit(n, "gate_up", i))
                buf = n // FB % 2
                toks = slice(buf * P, (buf + 1) * P)
                for k in range(4):
                    c = 4 * i + k
                    mm = mm3(ps[:, 2 + n % 2, :], x_hi[:, c, toks], x_lo[:, c, toks],
                             wh[:, k * HALF:(k + 1) * HALF], wl[:, k * HALF:(k + 1) * HALF], c == 0, c == KC - 1)
                mm.then_inc(used, 1)

            def turn_hid(it, n):
                pe.wait_ge(hid_done, it * (2 * FB) + (T * FB + n + 1))
                pe.wait_ge(hid_lo_made, it * (2 * FB) + (FB + n - 1))
                if n % FB == PICKS_TURN:
                    pe.wait_ge(turned_out, it * 2 + (TURNED + n // FB + 1))
                for c in range(2):
                    mm = pe.transpose(ps[:, 4 + n % 2, c * P:(c + 1) * P], hid[:, n % 2, c * P:(c + 1) * P], ident)
                mm.then_inc(hid_turned, 1)

            def down(it, n):
                pe.wait_ge(hid_lo_made, it * (2 * FB) + (FB + n + 1))
                b = n % FB
                if b == 0:
                    pe.wait_ge(evict_dve, it * 4 + (n_dve + 2 * (n // FB)))
                wh, wl = split_of_moe(it, expert_unit(n, "down"))
                for c in range(2):
                    for k in range(2):
                        cols = slice(k * D + c * HALF, k * D + (c + 1) * HALF)
                        mm = mm3(ps[:, c, :], hid_hi[:, n % 2, k, 0:P], hid_lo[:, n % 2, k, 0:P],
                                 wh[:, cols], wl[:, cols], b == 0 and k == 0, b == FB - 1 and k == 1)
                mm.then_inc(used, 1)

            def turn_pick(it, e):
                pe.wait_ge(hid_lo_made, it * (2 * FB) + (FB + FB * e + PICKS_TURN - 1))
                bank = 4 + (FB * e + PICKS_TURN) % 2
                for t in range(T):
                    pe.transpose(ps[:, bank, t * P:(t + 1) * P], pick[:, t, :], ident)
                for t in range(T):
                    mm = pe.matmul(ps[:, bank, SEQ:SEQ + 1], pick[:, t, :], expert_gate[:, t:t + 1], start=(t == 0), stop=(t == T - 1))
                mm.then_inc(block_turned, 1)

            def scatter(it, e, last, quarters=range(4)):
                pe.wait_ge(evict_dve, it * 4 + (n_dve + 2 * (e + 1)))
                pe.wait_ge(turned_out, it * 2 + (TURNED + e + 1))
                pe.wait_ge(token_lo, it * (2 * KC) + KC * (e + (1 if last else 2)))
                for q in quarters:
                    t, c = q // 2, q % 2
                    if q >= 2:
                        pe.wait_ge(added, it * 8 + (4 + 4 * e + q - 1))
                    toks, cols = slice(t * P, (t + 1) * P), slice(c * HALF, (c + 1) * HALF)
                    pe.matmul(ps[:, 6 + q % 2, :], pickT[:, toks], y_hi[:, cols], start=True, stop=False)
                    pe.matmul(ps[:, 6 + q % 2, :], pickT[:, toks], y_lo[:, cols], start=False, stop=True).then_inc(scattered, 1)

            def expert(it, e, last):
                for b in range(2, FB if last else FB + 2):
                    n = FB * e + b
                    if b == FB:
                        pe.wait_ge(token_lo, it * (2 * KC) + KC * (e + 2))
                    gate_up(it, n, 0)
                    turn_hid(it, n - 1)
                    if b == PICKS_TURN:
                        turn_pick(it, e)
                    gate_up(it, n, 1)
                    if b == FB + 1:
                        scatter(it, e, last, (0, 1))
                    down(it, n - 1)
                    if b == FB + 1:
                        scatter(it, e, last, (2, 3))
                    if b == 6 and not last:
                        gather(it, e + 1)
                if last:
                    turn_hid(it, FB * e + FB - 1)
                    down(it, FB * e + FB - 1)
                    scatter(it, e, last)

            def experts(second):
                e0, n0 = EXPERTS * second, EXPERTS * FB * second
                gather(0, e0)
                pe.wait_ge(token_lo, KC * e0 + KC // 2)
                gate_up(0, n0, 0)
                pe.wait_ge(token_lo, KC * (e0 + 1))
                gate_up(0, n0, 1)
                gate_up(0, n0 + 1, 0)
                turn_hid(0, n0)
                gate_up(0, n0 + 1, 1)
                down(0, n0)
                with pe.Fori(0, EXPERTS // 2 - 1) as it:
                    for p in range(2):
                        expert(it, e0 + p, False)
                expert(0, e0 + EXPERTS - 2, False)
                expert(0, e0 + EXPERTS - 1, True)

            experts(0)
            with pe.If(pe.value_load(flag[0:1, 0:1], min_val=0, max_val=1) > 0):
                experts(1)


def constants():
    row, col = np.arange(P)[:, None], np.arange(P)[None, :]
    upper = (row <= col).astype(np.float32)
    chunks = np.where(col // CHUNK <= row // CHUNK, 0.0, NEG)
    own = np.where(col <= row, 0.0, NEG)
    causal = np.concatenate([own, np.zeros((P, P)), own], 1)
    pos = np.arange(SEQ, dtype=np.float32)
    inv_freq = (np.float32(1.0) / (np.float32(10000.0) ** (np.arange(0, HD, 2, dtype=np.float32) / np.float32(HD)))).astype(np.float32)
    ang = pos[:, None] * inv_freq[None, :]
    cos, sin = np.cos(ang), np.sin(ang)
    by_tile = lambda a: a.reshape(T, P, HD).transpose(1, 0, 2).reshape(P, T * HD)
    return np.concatenate([np.eye(P), upper, np.ones((P, P)), np.broadcast_to(col + 1.0, (P, P)), chunks, causal,
                           by_tile(np.concatenate([cos, cos], 1)), by_tile(np.concatenate([-sin, sin], 1))],
                          1).astype(np.float32)


def kernel(x, a_norm, a_w_in, a_w_out, kv_norm, w_kv, b_f, b_norm, b_w_q, b_w_out, ffn_norm, dense_w_gate_up,
           dense_w_down, moe_router, moe_w_gate_up, moe_w_down, final_norm):
    from concourse import bacc
    from concourse.bass_utils import run_bass_kernel_spmd

    def block_units(w, c):
        part = np.asarray(w)[:, c * HALF:(c + 1) * HALF]
        return list(part.reshape(2, 4, P, HALF).transpose(0, 2, 1, 3).reshape(2, P, UNIT))

    def tail_unit(w):
        n = w.shape[1]
        unit = np.zeros((P, UNIT), w.dtype)
        unit[:, 0:KC * n] = np.asarray(w).reshape(KC, P, n).transpose(1, 0, 2).reshape(P, KC * n)
        return [unit]

    def ffn_units(gate_up, down, to, first, blocks):
        gu = gate_up.reshape(2, 4, P, 2, FB, 256).transpose(4, 0, 2, 1, 3, 5).reshape(FB, 2, P, UNIT)
        dn = down.reshape(FB, 2, P, D).transpose(0, 2, 1, 3).reshape(FB, P, UNIT)
        for b in range(FB):
            n = first + b
            to[gate_up_unit(n, 0)], to[gate_up_unit(n, 1)], to[down_unit(n, blocks)] = gu[b, 0], gu[b, 1], dn[b]

    w_in, w_kv = np.asarray(a_w_in)[0], np.asarray(w_kv)
    hd = HEADS * HD
    q, k, v, qi = 0, hd // HALF, 2 * hd // HALF, 3 * hd // HALF
    units = tail_unit(w_in[:, 3 * hd + HALF:]) + block_units(w_in, qi)
    for c in (q, q + 1, k, k + 1, v, v + 1):
        units += block_units(w_in, c)
    for c in range(2):
        units += block_units(a_w_out[0], c)
    dense = np.empty((FFN_UNITS, P, UNIT), np.float32)
    ffn_units(np.asarray(dense_w_gate_up)[0], np.asarray(dense_w_down)[0], dense, 0, FB)
    units += list(dense)
    for c in range(2):
        units += block_units(b_w_q[0], c)
    for c in range(2):
        units += block_units(w_kv, c)
    units += tail_unit(w_kv[:, 2 * hd:])
    for c in range(2, 4):
        units += block_units(w_kv, c)
    for c in range(2):
        units += block_units(b_w_out[0], c)
    units += tail_unit(np.asarray(moe_router)[0])
    pre = np.stack(units)
    assert len(pre) == PRE
    moe = np.empty((MOE_UNITS, P, UNIT), np.float32)
    for e in range(EXPERTS):
        ffn_units(np.asarray(moe_w_gate_up)[0, e], np.asarray(moe_w_down)[0, e], moe, FB * e, FB * EXPERTS)
    gain_rows = [a_norm[0], ffn_norm[0], kv_norm, b_norm[0], ffn_norm[1]]
    arrays = {
        "x": np.asarray(x), "pre_stream": pre, "moe_stream": moe,
        "gain_cols": np.ascontiguousarray(np.stack([np.asarray(g) for g in gain_rows]).reshape(5 * KC, P).T),
        "final_norm": np.asarray(final_norm), "b_f": np.asarray(b_f), "consts": constants(),
    }
    nc = bacc.Bacc("TRN2", target_bir_lowering=False, num_devices=1)
    aps = {n: nc.dram_tensor(n, a.shape, F32, kind="ExternalInput").ap() for n, a in arrays.items()}
    out = nc.dram_tensor("out", (1, SEQ, D), F32, kind="ExternalOutput").ap()
    trunk(nc, out=out, **aps)
    return run_bass_kernel_spmd(nc, [arrays], core_ids=[0]).results[0]["out"]
```
